# Optimizing a Trainium2 kernel written in Bass

```python
import jax, jax.numpy as jnp
from jax import lax
import numpy as np

D_MODEL = 1024
BATCH = 1
SEQ = 1024
DEPTH = 1

CHUNK = 64
POOL_WIDTH = 1024
POOL_WINDOWS = (2, 4, 8, 16)
POOL_GROUPS = len(POOL_WINDOWS)
POOL_GROUP_WIDTH = POOL_WIDTH // POOL_GROUPS
HGRN_WIDTH = 1024
HGRN_EXPAND = 128
HGRN_HEADS = HGRN_WIDTH // HGRN_EXPAND
HGRN_HEAD_V = HGRN_WIDTH // HGRN_HEADS
MIX_WIDTH = POOL_WIDTH + HGRN_WIDTH
IN_WIDTH = 2 * POOL_WIDTH + 4 * HGRN_WIDTH
EPS = 1e-6


def rms_norm(x, w):
    xf = x.astype(jnp.float32)
    xf = xf * lax.rsqrt(jnp.mean(xf * xf, axis=-1, keepdims=True) + EPS)
    return xf * w.astype(jnp.float32)

def multiscale_pool(u, pool_w, pool_scale):
    B, S, _ = u.shape
    cs = jnp.cumsum(u, axis=1)
    count = jnp.arange(1, S + 1, dtype=jnp.float32)[None, :, None]
    outs = []
    for g, w in enumerate(POOL_WINDOWS):
        lo, hi = g * POOL_GROUP_WIDTH, (g + 1) * POOL_GROUP_WIDTH
        cs_g = cs[..., lo:hi]
        prev = jnp.pad(cs_g, ((0, 0), (w, 0), (0, 0)))[:, :S]
        mean = (cs_g - prev) / jnp.minimum(count, float(w))
        outs.append(mean - u[..., lo:hi])
    d = jnp.stack(outs, axis=2)
    y = jnp.einsum('bsgc,gcd->bsgd', d, pool_w.astype(jnp.float32))
    return y.reshape(B, S, POOL_WIDTH) * pool_scale.astype(jnp.float32)

def _to_chunks(t):
    B, S, H, D = t.shape
    return t.reshape(B, S // CHUNK, CHUNK, H, D).transpose(1, 0, 3, 2, 4)

def hgrn2_chunkwise(q, log_f, k, v):
    B, S, H, dk = q.shape
    dv = v.shape[-1]
    causal = jnp.tril(jnp.ones((CHUNK, CHUNK), dtype=bool))[:, :, None]

    def step(state, xs):
        qc, lfc, kc, vc = xs
        b = jnp.cumsum(lfc, axis=2)
        o_inter = jnp.einsum('bhtk,bhkv->bhtv', qc * jnp.exp(b), state)
        diff = b[:, :, :, None, :] - b[:, :, None, :, :]
        decay = jnp.exp(jnp.where(causal, diff, -jnp.inf))
        attn = jnp.einsum('bhtk,bhsk,bhtsk->bhts', qc, kc, decay)
        o_intra = jnp.einsum('bhts,bhsv->bhtv', attn, vc)
        b_last = b[:, :, -1, :]
        k_dec = kc * jnp.exp(b_last[:, :, None, :] - b)
        new_state = jnp.exp(b_last)[..., None] * state + jnp.einsum('bhsk,bhsv->bhkv', k_dec, vc)
        return new_state, o_inter + o_intra

    state0 = jnp.zeros((B, H, dk, dv), jnp.float32)
    _, o = lax.scan(step, state0, (_to_chunks(q), _to_chunks(log_f), _to_chunks(k), _to_chunks(v)))
    return o.transpose(1, 0, 3, 2, 4).reshape(B, S, H, dv)

def first_inputs(seed: int = 0) -> dict:
    key = jax.random.key(seed)
    ks = jax.random.split(key, 12)
    f32 = jnp.float32
    x = jax.random.normal(ks[0], (BATCH, SEQ, D_MODEL), f32)
    c = jax.random.normal(ks[1], (BATCH, D_MODEL), f32)
    norm_pre_w = 1.0 + 0.05 * jax.random.normal(ks[2], (DEPTH, D_MODEL), f32)
    ada_w = 0.5 * D_MODEL ** -0.5 * jax.random.normal(ks[3], (DEPTH, D_MODEL, 3 * D_MODEL), f32)
    ada_b = 0.01 * jax.random.normal(ks[4], (DEPTH, 3 * D_MODEL), f32)
    w_in = D_MODEL ** -0.5 * jax.random.normal(ks[5], (DEPTH, D_MODEL, IN_WIDTH), f32)
    pool_w = POOL_GROUP_WIDTH ** -0.5 * jax.random.normal(
        ks[6], (DEPTH, POOL_GROUPS, POOL_GROUP_WIDTH, POOL_GROUP_WIDTH), f32)
    pool_scale = 1.0 + 0.05 * jax.random.normal(ks[7], (DEPTH, POOL_WIDTH), f32)
    hgrn_lower_bounds = 0.5 * jax.random.normal(ks[8], (DEPTH, HGRN_WIDTH), f32)
    hgrn_norm_w = 1.0 + 0.05 * jax.random.normal(ks[9], (DEPTH, HGRN_HEAD_V), f32)
    w_out = MIX_WIDTH ** -0.5 * jax.random.normal(ks[10], (DEPTH, MIX_WIDTH, D_MODEL), f32)
    norm_post_w = 1.0 + 0.05 * jax.random.normal(ks[11], (DEPTH, D_MODEL), f32)
    return {"x": x, "c": c, "norm_pre_w": norm_pre_w, "ada_w": ada_w, "ada_b": ada_b,
            "w_in": w_in, "pool_w": pool_w, "pool_scale": pool_scale,
            "hgrn_lower_bounds": hgrn_lower_bounds, "hgrn_norm_w": hgrn_norm_w,
            "w_out": w_out, "norm_post_w": norm_post_w}

def first_block(x, c, norm_pre_w, ada_w, ada_b, w_in, pool_w, pool_scale,
              hgrn_lower_bounds, hgrn_norm_w, w_out, norm_post_w):
    B, S, D = x.shape
    f32 = jnp.float32
    lb_sm = jax.nn.softmax(hgrn_lower_bounds.astype(f32), axis=0)
    lower_bounds = jnp.cumsum(lb_sm, axis=0) - lb_sm[0]
    silu_c = jax.nn.silu(c.astype(f32))
    h_res = x.astype(f32)
    for l in range(DEPTH):
        mod = silu_c @ ada_w[l].astype(f32) + ada_b[l].astype(f32)
        shift, scale, gate = jnp.split(mod[:, None, :], 3, axis=-1)
        h = rms_norm(h_res, norm_pre_w[l]) * (1.0 + scale) + shift
        z = h @ w_in[l].astype(f32)
        u_pool, g_pool, q, f_pre, i_in, g_h = jnp.split(
            z, np.cumsum([POOL_WIDTH, POOL_WIDTH, HGRN_WIDTH, HGRN_WIDTH, HGRN_WIDTH]), axis=-1)
        pool_out = multiscale_pool(u_pool, pool_w[l], pool_scale[l]) * jax.nn.silu(g_pool)
        lb = lower_bounds[l]
        f = lb + (1.0 - lb) * jax.nn.sigmoid(f_pre)
        log_f = jnp.log(f)
        k = 1.0 - f
        heads = lambda t, d: t.reshape(B, S, HGRN_HEADS, d)
        o = hgrn2_chunkwise(heads(q, HGRN_EXPAND), heads(log_f, HGRN_EXPAND),
                            heads(k, HGRN_EXPAND), heads(i_in, HGRN_HEAD_V))
        o = rms_norm(o, hgrn_norm_w[l]) * jax.nn.silu(heads(g_h, HGRN_HEAD_V))
        hgrn_out = o.reshape(B, S, HGRN_WIDTH)
        y = jnp.concatenate([pool_out, hgrn_out], axis=-1) @ w_out[l].astype(f32)
        h_res = h_res + gate * rms_norm(y, norm_post_w[l])
    return h_res.astype(x.dtype)


MIX_WIDTH_2 = D_MODEL
HEAD_DIM = 64
ATTN_WIDTH = MIX_WIDTH_2 // 2
ATTN_HEADS = ATTN_WIDTH // HEAD_DIM
SGU_WIDTH = MIX_WIDTH_2 - ATTN_WIDTH
SGU_GROUP_DIM = 64
SGU_GROUPS = SGU_WIDTH // SGU_GROUP_DIM
SGU_CHUNK = 128
DILATED_PATTERNS = ((128, 1), (512, 4), (2048, 16))
BLOCK_Q = 128
ROPE_THETA = 500000.0
ROT_DIM = HEAD_DIM // 4
ROT_HALF = ROT_DIM // 2
D_FF = ((8 * D_MODEL // 3 + 255) // 256) * 256
IN_PROJ_WIDTH = 3 * ATTN_WIDTH + 2 * SGU_WIDTH
RMS_EPS = 1e-6
LN_EPS = 1e-5


def rms_norm_2(x, gain):
    xf = x.astype(jnp.float32)
    y = xf * lax.rsqrt(jnp.mean(xf * xf, axis=-1, keepdims=True) + RMS_EPS)
    return (y * gain.astype(jnp.float32)).astype(x.dtype)

def layer_norm(x, gain, bias):
    xf = x.astype(jnp.float32)
    mu = jnp.mean(xf, axis=-1, keepdims=True)
    xc = xf - mu
    y = xc * lax.rsqrt(jnp.mean(xc * xc, axis=-1, keepdims=True) + LN_EPS)
    return (y * gain.astype(jnp.float32) + bias.astype(jnp.float32)).astype(x.dtype)

def partial_rotary(x, positions):
    inv_freq = ROPE_THETA ** (-jnp.arange(0, ROT_DIM, 2, dtype=jnp.float32) / ROT_DIM)
    ang = positions.astype(jnp.float32)[:, :, None, None] * inv_freq
    cos, sin = jnp.cos(ang), jnp.sin(ang)
    xf = x.astype(jnp.float32)
    x1 = xf[..., :ROT_HALF]
    x2 = xf[..., ROT_HALF:ROT_DIM]
    out = jnp.concatenate([x1 * cos - x2 * sin, x2 * cos + x1 * sin, xf[..., ROT_DIM:]], axis=-1)
    return out.astype(x.dtype)

def dilated_window_attention(q, k, v, window, dilation):
    B, H, S, Dh = q.shape
    L = S // dilation
    W = window // dilation
    nblk = -(-L // BLOCK_Q)
    Lp = nblk * BLOCK_Q

    def strided(t):
        return t.reshape(B, H, L, dilation, Dh).transpose(0, 1, 3, 2, 4)

    qs, ks, vs = strided(q), strided(k), strided(v)
    qs = jnp.pad(qs, ((0, 0), (0, 0), (0, 0), (0, Lp - L), (0, 0)))
    kv_pad = ((0, 0), (0, 0), (0, 0), (W, Lp - L), (0, 0))
    kp = jnp.pad(ks, kv_pad)
    vp = jnp.pad(vs, kv_pad)
    blk = jnp.arange(nblk)[:, None]
    col = jnp.arange(BLOCK_Q + W)[None, :]
    idx = blk * BLOCK_Q + col
    kb = kp[:, :, :, idx]
    vb = vp[:, :, :, idx]
    qb = qs.reshape(B, H, dilation, nblk, BLOCK_Q, Dh)

    scale = 1.0 / np.sqrt(HEAD_DIM)
    s = jnp.einsum('bhrnqd,bhrnkd->bhrnqk', qb, kb,
                   preferred_element_type=jnp.float32) * scale
    row = jnp.arange(BLOCK_Q)[:, None]
    dist = row + W - jnp.arange(BLOCK_Q + W)[None, :]
    key_pos = jnp.arange(nblk)[:, None, None] * BLOCK_Q + jnp.arange(BLOCK_Q + W)[None, None, :] - W
    mask = (dist >= 0)[None] & (dist <= W)[None] & (key_pos >= 0)
    s = jnp.where(mask, s, jnp.finfo(jnp.float32).min)
    m = jnp.max(s, axis=-1, keepdims=True)
    p = jnp.exp(s - m)
    denom = jnp.sum(p, axis=-1, keepdims=True)
    o = jnp.einsum('bhrnqk,bhrnkd->bhrnqd', p, vb.astype(jnp.float32)) / denom
    lse = (m + jnp.log(denom))[..., 0]
    o = o.reshape(B, H, dilation, Lp, Dh)[:, :, :, :L]
    lse = lse.reshape(B, H, dilation, Lp)[:, :, :, :L]
    o = o.transpose(0, 1, 3, 2, 4).reshape(B, H, S, Dh)
    lse = lse.transpose(0, 1, 3, 2).reshape(B, H, S)
    return o, lse

def dilated_mixture_attention(q, k, v):
    outs, lses = [], []
    for window, dilation in DILATED_PATTERNS:
        o, lse = dilated_window_attention(q, k, v, window, dilation)
        outs.append(o)
        lses.append(lse)
    wts = jax.nn.softmax(jnp.stack(lses, axis=0), axis=0)
    o = jnp.sum(wts[..., None] * jnp.stack(outs, axis=0), axis=0)
    return o.astype(q.dtype)

def spatial_gating(u, v, ln_gain, ln_bias, w_spatial, b_spatial):
    B, S, _ = u.shape
    u = jax.nn.gelu(u, approximate=False)
    v = layer_norm(jax.nn.gelu(v, approximate=False), ln_gain, ln_bias)
    vc = v.reshape(B, S // SGU_CHUNK, SGU_CHUNK, SGU_GROUPS, SGU_GROUP_DIM)
    causal = jnp.tril(jnp.ones((SGU_CHUNK, SGU_CHUNK), dtype=bool))
    w = jnp.where(causal[None], w_spatial, 0.0).astype(v.dtype)
    mixed = jnp.einsum('gij,bnjgc->bnigc', w, vc) + b_spatial.T[:, :, None].astype(v.dtype)
    return u * mixed.reshape(B, S, SGU_WIDTH)

def second_inputs(seed: int = 0) -> dict:
    key = jax.random.key(seed)
    ks = jax.random.split(key, 20)
    f32 = jnp.float32

    def nrm(k, shape, scale):
        return jax.random.normal(k, shape, f32) * scale

    def gain(k, width):
        return 1.0 + 0.05 * jax.random.normal(k, (DEPTH, width), f32)

    x = jax.random.normal(ks[0], (BATCH, SEQ, D_MODEL), f32)
    offsets = jax.random.randint(ks[1], (BATCH, 1), 0, 4096, dtype=jnp.int32)
    positions = (jnp.arange(SEQ, dtype=jnp.int32)[None, :] + offsets).astype(jnp.int32)
    return {
        "x": x,
        "positions": positions,
        "pre_mix_norm": gain(ks[2], D_MODEL),
        "w_in": nrm(ks[3], (DEPTH, D_MODEL, IN_PROJ_WIDTH), D_MODEL ** -0.5),
        "sgu_ln_gain": gain(ks[4], SGU_WIDTH),
        "sgu_ln_bias": nrm(ks[5], (DEPTH, SGU_WIDTH), 0.02),
        "sgu_w_spatial": nrm(ks[6], (DEPTH, SGU_GROUPS, SGU_CHUNK, SGU_CHUNK), 0.5 * SGU_CHUNK ** -0.5),
        "sgu_b_spatial": 1.0 + nrm(ks[7], (DEPTH, SGU_GROUPS, SGU_CHUNK), 0.1),
        "attn_out_norm": gain(ks[8], ATTN_WIDTH),
        "sgu_out_norm": gain(ks[9], SGU_WIDTH),
        "w_out": nrm(ks[10], (DEPTH, MIX_WIDTH_2, D_MODEL), MIX_WIDTH_2 ** -0.5),
        "post_mix_norm": gain(ks[11], D_MODEL),
        "pre_ffn_norm": gain(ks[12], D_MODEL),
        "w_gate": nrm(ks[13], (DEPTH, D_MODEL, D_FF), D_MODEL ** -0.5),
        "w_up": nrm(ks[14], (DEPTH, D_MODEL, D_FF), D_MODEL ** -0.5),
        "w_down": nrm(ks[15], (DEPTH, D_FF, D_MODEL), D_FF ** -0.5),
        "post_ffn_norm": gain(ks[16], D_MODEL),
    }

def second_block(x, positions, pre_mix_norm, w_in, sgu_ln_gain, sgu_ln_bias, sgu_w_spatial,
              sgu_b_spatial, attn_out_norm, sgu_out_norm, w_out, post_mix_norm,
              pre_ffn_norm, w_gate, w_up, w_down, post_ffn_norm):
    B, S, _ = x.shape
    for l in range(DEPTH):
        h = rms_norm_2(x, pre_mix_norm[l])
        proj = h @ w_in[l]
        q, k, v_a, u, v_s = jnp.split(
            proj, [ATTN_WIDTH, 2 * ATTN_WIDTH, 3 * ATTN_WIDTH, 3 * ATTN_WIDTH + SGU_WIDTH], axis=-1)
        q = partial_rotary(q.reshape(B, S, ATTN_HEADS, HEAD_DIM), positions).transpose(0, 2, 1, 3)
        k = partial_rotary(k.reshape(B, S, ATTN_HEADS, HEAD_DIM), positions).transpose(0, 2, 1, 3)
        v_a = v_a.reshape(B, S, ATTN_HEADS, HEAD_DIM).transpose(0, 2, 1, 3)
        attn = dilated_mixture_attention(q, k, v_a)
        attn = attn.transpose(0, 2, 1, 3).reshape(B, S, ATTN_WIDTH)
        sgu = spatial_gating(u, v_s, sgu_ln_gain[l], sgu_ln_bias[l],
                             sgu_w_spatial[l], sgu_b_spatial[l])
        mixed = jnp.concatenate([rms_norm_2(attn, attn_out_norm[l]),
                                 rms_norm_2(sgu, sgu_out_norm[l])], axis=-1)
        y = mixed @ w_out[l]
        x = x + rms_norm_2(y, post_mix_norm[l])
        h = rms_norm_2(x, pre_ffn_norm[l])
        f = (jax.nn.silu(h @ w_gate[l]) * (h @ w_up[l])) @ w_down[l]
        x = x + rms_norm_2(f, post_ffn_norm[l])
    return x


def setup_inputs(seed=0):
    out = dict(first_inputs(seed))
    for name, value in second_inputs(seed + 1).items():
        if name != "x":
            out[name + "_2"] = value
    return out


def reference(
    x, c, norm_pre_w, ada_w, ada_b, w_in, pool_w, pool_scale, hgrn_lower_bounds, hgrn_norm_w,
    w_out, norm_post_w, positions_2, pre_mix_norm_2, w_in_2, sgu_ln_gain_2, sgu_ln_bias_2,
    sgu_w_spatial_2, sgu_b_spatial_2, attn_out_norm_2, sgu_out_norm_2, w_out_2, post_mix_norm_2,
    pre_ffn_norm_2, w_gate_2, w_up_2, w_down_2, post_ffn_norm_2,
):
    x = first_block(
        x, c, norm_pre_w, ada_w, ada_b, w_in, pool_w, pool_scale, hgrn_lower_bounds,
        hgrn_norm_w, w_out, norm_post_w,
    )
    return second_block(
        x, positions_2, pre_mix_norm_2, w_in_2, sgu_ln_gain_2, sgu_ln_bias_2, sgu_w_spatial_2,
        sgu_b_spatial_2, attn_out_norm_2, sgu_out_norm_2, w_out_2, post_mix_norm_2,
        pre_ffn_norm_2, w_gate_2, w_up_2, w_down_2, post_ffn_norm_2,
    )


_drawn_inputs = setup_inputs


def setup_inputs(seed=0):
    import zlib

    import numpy as np

    out = dict(_drawn_inputs(seed))
    spreads = {}
    factors = {'ada_b': 3.178,
     'pool_scale': 12.975,
     'hgrn_norm_w': 10.055,
     'sgu_ln_gain_2': 6.401,
     'sgu_ln_bias_2': 35.819}
    for name, (base, spread) in spreads.items():
        noise = np.random.default_rng([zlib.crc32(name.encode()), seed]).standard_normal(out[name].shape)
        drawn = base * np.exp(spread * noise) if base else spread * noise
        out[name] = __import__('jax').numpy.asarray(drawn.astype(out[name].dtype))
    for name, factor in factors.items():
        out[name] = (out[name] * factor).astype(out[name].dtype)
    return out
```

```python
import math
from contextlib import ExitStack

import numpy as np

import concourse.bass as bass
import concourse.mybir as mybir

F32 = mybir.dt.float32
F32R = mybir.dt.float32r
I32 = mybir.dt.int32
ACT = mybir.ActivationFunctionType
ALU = mybir.AluOpType
AX = mybir.AxisListType

P = 128
D = 1024
S = 1024
KT = D // P
NT = S // P
HALF = 512
PAGE = 1024

HEADS = 8
SPANS = [64, 32, 16, 8, 4, 2, 1]
NL = len(SPANS)
POOL_WINDOWS = (2, 4, 8, 16)
GROUPS = 4
F_MIN = 1e-19

DH = 64
AH = 8
ATT = 512
ROT = 8
SGU_G = 8
D_FF = 2816
FT = D_FF // P
EPS = 1e-6
LN_EPS = 1e-5
TWO_PI = 2 * math.pi
TWO_PI_HI = 6.28125
TWO_PI_LO = TWO_PI - TWO_PI_HI
PI_IN = 3.1415925
ROPE_STEPS = 17
NEG = -1e30

VEC = [("c", 8), ("ada_b", 24), ("norm_pre_w", 8), ("pool_scale", 8), ("hgrn_lower_bounds", 8),
       ("hgrn_norm_w", 1), ("pre_mix_norm_2", 8), ("attn_out_norm_2", 4), ("sgu_out_norm_2", 4),
       ("pre_ffn_norm_2", 8), ("sgu_b_spatial_2", 8)]
VROW, VROWS = {}, 0
for _name, _n in VEC:
    VROW[_name] = VROWS
    VROWS += _n

U_HGRN = 0
U_POOL = U_HGRN + 4 * HEADS
U_OUT = U_POOL + 4 * GROUPS
U_IN2 = U_OUT + 16
U_OUT2 = U_IN2 + 20
U_GU = U_OUT2 + 8
U_DOWN = U_GU + 2 * FT
UNITS = U_DOWN + FT
RAW = 4
C_U, C_G, C_Q, C_F, C_V, C_GH = 0, 8, 16, 24, 32, 40
IN2_BLOCKS = [4, 3, 2, 0, 1]


def program(nc, ap):
    ctx = ExitStack()
    with ctx:
        def sb(name, shape, dt=F32):
            return ctx.enter_context(nc.sbuf_tensor(name, shape, dt))

        def sem(name):
            return ctx.enter_context(nc.semaphore(name))

        h_hi = sb("h_hi", [P, KT, S], F32R)
        h_lo = sb("h_lo", [P, KT, S], F32R)
        w_raw = sb("w_raw", [P, RAW, 1024])
        w_hi = sb("w_hi", [P, 2, 1024], F32R)
        w_lo = sb("w_lo", [P, 2, 1024], F32R)
        arena = sb("arena", [P, 27 * PAGE])
        ident = sb("ident", [P, P])
        ones = sb("ones", [P, P])
        cols = sb("cols", [P, VROWS])
        lvl_mask = sb("lvl_mask", [P, NL, 64], I32)
        st = sb("st", [P, 160])
        psum = ctx.enter_context(nc.psum_tensor("psum", [P, 8, HALF], F32))

        def page(i, n=1):
            return arena[:, i * PAGE:(i + n) * PAGE]

        def tiles(i, n=NT):
            return page(i, n).rearrange("p (t c) -> p t c", c=PAGE)

        def two_banks(slot):
            return psum[:, 2 * slot:2 * slot + 2, :].rearrange("p b n -> p (b n)")

        def col(name, i=0, n=1):
            return cols[:, VROW[name] + i:VROW[name] + i + n]

        silu_c = st[:, 0:8]
        mod = st[:, 8:24]
        mul_a = st[:, 24:32]
        lb = st[:, 32:40]
        one_lb = st[:, 40:48]
        lb_tmp = st[:, 48:56]
        ss = st[:, 56:72]
        ms = st[:, 72:80]
        rstd = st[:, 80:88]
        end_decay = st[:, 88:96]
        mean = st[:, 96:104]
        neg_max = st[:, 104:112]
        r_den = st[:, 112:120]
        pos = st[:, 120:128]
        sums = st[:, 128:136]
        den_ = page(24)[:, 0:AH * NT]

        X0 = 0
        ADA = 8
        ACC = 17
        JUNK0 = 20
        ADAB = 21
        GATE_ROW = 26
        NPOST = 25
        MIX = 0
        B_SIG, B_K, B_B, B_Q, B_QE, B_VT, B_V, B_KDT, B_KD, B_ATT = range(16, 26)
        B_S, B_D, B_KL, B_QL = 2, 3, 5, 7
        U_PAGES = [(16, 21), (17, 18)]
        S_A, S_B = 22, 24
        PW = [23, 19]
        RC = 20
        IDM = ident

        gate_row = page(GATE_ROW)
        mixp = [page(MIX + i) for i in range(16)]
        Y = tiles(16)
        XR = tiles(0)
        vs_b, u_b, v_b, q_b, k_b = [page(4 * i, 4).rearrange("p (t c) -> p t c", c=ATT) for i in range(5)]
        SPAT, SPAT_T = 20, 21
        ROPE = page(22)
        ROPE_T = [page(23)[:, 0:512], page(23)[:, 512:1024], page(26)[:, 0:512]]
        JUNK3 = page(26)[:, 512:1024]
        LN_ROWS = page(24)
        BIAS = page(25)
        probs = [page(16 + i) for i in range(4)]
        probs_t = [page(0 + i) for i in range(2)]
        att_o = q_b
        POST_ROW = page(24)
        ROW_F = page(26)
        actp = [page(i) for i in range(FT)]
        y_half0 = page(22, 4).rearrange("p (t c) -> p t c", c=HALF)
        y_half1 = page(8, 4).rearrange("p (t c) -> p t c", c=HALF)

        x_mid = [nc.dram_tensor(f"x_mid{i}", [NT, P, D], F32, kind="Internal").ap() for i in range(2)]

        raw_in = [sem(f"raw_in{i}") for i in range(RAW)]
        w_rounded, w_ready, w_used = sem("w_rounded"), sem("w_ready"), sem("w_used")
        const_in, vec_in, pos_in, row_in = sem("const_in"), sem("vec_in"), sem("pos_in"), sem("row_in")
        x_in = [sem(f"x_in{t}") for t in range(NT)]
        ada_in = [sem(f"ada_in{i}") for i in range(3)]
        ones_set, vec_t, cols_done = sem("ones_set"), sem("vec_t"), sem("cols_done")
        silu_done, ada_acc, mod_mm, mod_done = sem("silu_done"), sem("ada_acc"), sem("mod_mm"), sem("mod_done")
        lb_step, lb_exp = sem("lb_step"), sem("lb_exp")
        ss_done, ms_done, sqrt_done, rstd_done = sem("ss_done"), sem("ms_done"), sem("sqrt_done"), sem("rstd_done")
        xn_done, tr_full, hi_done, lo_tmp, lo_done = (sem("xn_done"), sem("tr_full"), sem("hi_done"),
                                                      sem("lo_tmp"), sem("lo_done"))
        sig_done, gsig_done, g_done, vt_done, q_done = (sem("sig_done"), sem("gsig_done"), sem("g_done"),
                                                        sem("vt_done"), sem("q_done"))
        f_done, k_done, fc_done, lf_done, b_done = (sem("f_done"), sem("k_done"), sem("fc_done"),
                                                    sem("lf_done"), sem("b_done"))
        eb_done, end_done, dk_done, ek_done, kdec_done, qe_done = (
            sem("eb_done"), sem("end_done"), sem("dk_done"), sem("ek_done"), sem("kdec_done"), sem("qe_done"))
        d_done, e_done, kl_done, lvl_done, task_full = (sem("d_done"), sem("e_done"), sem("kl_done"),
                                                        sem("lvl_done"), sem("task_full"))
        v_done, kd_done, diag_done, pick_done, s_done = (sem("v_done"), sem("kd_done"), sem("diag_done"),
                                                         sem("pick_done"), sem("s_done"))
        sq_done, ln_done, rs_done, o1_done, o_done = (sem("sq_done"), sem("ln_done"), sem("rs_done"),
                                                      sem("o1_done"), sem("o_done"))
        pu_done, pgs_done, pg_done, win_step, pd_done, pm_full, pmix_done, pw_in, rc_in = (
            sem("pu_done"), sem("pgs_done"), sem("pg_done"), sem("win_step"), sem("pd_done"), sem("pm_full"),
            sem("pmix_done"), sem("pw_in"), sem("rc_in"))
        sp_hi, sp_lo, yb_full, ycp_done, ysq_done = (sem("sp_hi"), sem("sp_lo"), sem("yb_full"),
                                                     sem("ycp_done"), sem("ysq_done"))
        sum_done, res_step, res_done, spilled = sem("sum_done"), sem("res_step"), sem("res_done"), [sem("spilled0"), sem("spilled1")]
        in2_free, in2_full, lnrow_in, spat_in, bias_in, freq_in = (
            sem("in2_free"), sem("in2_full"), sem("lnrow_in"), sem("spat_in"), sem("bias_in"), sem("freq_in"))
        gelu_done, mean_done, var_done, lnorm = sem("gelu_done"), sem("mean_done"), sem("var_done"), sem("lnorm")
        tril_done, spat_full, spat_tr, sgu_full, sgu_done = (sem("tril_done"), sem("spat_full"), sem("spat_tr"),
                                                             sem("sgu_full"), sem("sgu_done"))
        rope_step, trig_done, rope_done = sem("rope_step"), sem("trig_done"), sem("rope_done")
        s_full, s_moved, max_done, p_done, pt_full, pt_done, pv_full, den_done, ao_done = (
            sem("s_full"), sem("s_moved"), sem("max_done"), sem("p_done"), sem("pt_full"), sem("pt_done"),
            sem("pv_full"), sem("den_done"), sem("ao_done"))
        gate_silu, act_done, out_sent, mixn_done = sem("gate_silu"), sem("act_done"), sem("out_sent"), sem("mixn_done")
        ln2_done = sem("ln2_done")

        block = ctx.enter_context(nc.Block())

        fm = lambda w: w[0].rearrange("(k p) (f c) -> f p k c", p=P, c=P)
        tm = lambda w: w[0].rearrange("(j k p) (n c) -> n j p k c", k=2, p=P, c=HALF)
        w_in_fm, gate_fm, up_fm = fm(ap["w_in"]), fm(ap["w_gate_2"]), fm(ap["w_up_2"])
        w_out_tm, w_in2_tm, w_out2_tm, down_tm = tm(ap["w_out"]), tm(ap["w_in_2"]), tm(ap["w_out_2"]), tm(ap["w_down_2"])

        @block.sync
        def _(sp):
            for name, n in VEC:
                r = VROW[name]
                src = ap[name]
                src = src[0] if len(src.shape) > 2 else src
                if name == "sgu_b_spatial_2":
                    flat = src
                else:
                    flat = src.rearrange("a (r c) -> (a r) c", c=P)
                sp.dma_start(arena[r:r + n, JUNK0 * PAGE:JUNK0 * PAGE + P], flat).then_inc(vec_in, 16)
            sp.dma_start(pos.bitcast(I32), ap["positions_2"][0].rearrange("(t p) -> p t", p=P), allow_slow_non_contiguous=True).then_inc(pos_in, 16)
            sp.dma_start(ident[:], ap["k_ident"]).then_inc(const_in, 16)
            sp.dma_start(lvl_mask[:], ap["k_level_mask"]).then_inc(const_in, 16)
            ada_v = ap["ada_w"][0].rearrange("(k p) n -> k p n", p=P)
            for k in range(KT):
                if k >= 3:
                    sp.wait_ge(ada_acc, k - 2)
                sp.dma_start(page(ADA + 3 * (k % 3), 3), ada_v[k]).then_inc(ada_in[k % 3], 16)
                if k == 2:
                    sp.dma_start(arena[0:1, ADAB * PAGE:(ADAB + 1) * PAGE], ap["ada_b"][0:1, 2 * D:3 * D]).then_inc(row_in, 16)
                    sp.dma_start(page(NPOST), ap["norm_post_w"][0].partition_broadcast(P)).then_inc(row_in, 16)

            def slot_fm(s):
                return w_raw[:, s, :].rearrange("p (k c) -> p k c", c=P)

            def slot_tm(s):
                return w_raw[:, s, :].rearrange("p (k c) -> p k c", c=HALF)

            def load(s, dst, src):
                sp.dma_start(dst, src).then_inc(raw_in[s], 16)

            for s, c in enumerate((C_F, C_GH, C_V, C_Q)):
                load(s, slot_fm(s), w_in_fm[c])
            with sp.Fori(1, HEADS) as h:
                for s, c in enumerate((C_F, C_GH, C_V, C_Q)):
                    sp.wait_ge(w_ready, 4 * h + s - 3)
                    load(s, slot_fm(s), w_in_fm[h + c])
            with sp.Fori(0, GROUPS) as g:
                for s in range(4):
                    sp.wait_ge(w_ready, 4 * g + (U_POOL + s - 3))
                    load(s, slot_fm(s), w_in_fm[2 * g + (s // 2 + (C_U, C_G)[s % 2])])
            for n in range(2):
                with sp.Fori(0, 2) as j:
                    for s in range(4):
                        sp.wait_ge(w_ready, 4 * j + (U_OUT + 8 * n + s - 3))
                        load(s, slot_tm(s), w_out_tm[n][4 * j + s])
            for t in range(NT):
                sp.wait_ge(sp_lo, 16 + t + 1)
                sp.dma_start(XR[:, t, :], ap["x"][0, t * P:(t + 1) * P, :]).then_inc(x_in[t], 16)
            for b, blk in enumerate(IN2_BLOCKS):
                for s in range(4):
                    sp.wait_ge(w_ready, U_IN2 + 4 * b + s - 3)
                    load(s, slot_tm(s), w_in2_tm[blk][s])
            for n in range(2):
                for s in range(4):
                    sp.wait_ge(w_ready, U_OUT2 + 4 * n + s - 3)
                    load(s, slot_tm(s), w_out2_tm[n][s])
            for t in range(NT):
                sp.wait_ge(tr_full, 32)
                sp.wait_ge(spilled[0], 16 * NT)
                sp.dma_start(XR[:, t, :], x_mid[0][t]).then_inc(x_in[t], 16)
            with sp.Fori(0, FT // 2) as i:
                for s in range(4):
                    sp.wait_ge(w_ready, 4 * i + (U_GU + s - 3))
                    load(s, slot_fm(s), (gate_fm, up_fm)[s % 2][2 * i + s // 2])
            for j in range(FT):
                s = j % RAW
                sp.wait_ge(w_ready, U_DOWN + j - 3)
                load(s, slot_tm(s), down_tm[j // 11][j % 11])
            for t in range(NT):
                sp.wait_ge(sp_lo, 32 + FT + t + 1)
                sp.wait_ge(spilled[1], 16 * NT)
                sp.dma_start(XR[:, t, :], x_mid[1][t]).then_inc(x_in[t], 16)
            for t in range(NT):
                sp.wait_ge(res_done, 2 * NT + t + 1)
                sp.dma_start(ap["out"][t], XR[:, t, :]).then_inc(out_sent, 16)
            sp.wait_ge(out_sent, 16 * NT)

        @block.gpsimd
        def _(pool):
            unit_scale = ones[:].rearrange("p (a n) -> p a n", a=1).to_broadcast([P, KT, P])

            def split(i, s, first):
                c = s % 2
                raw = w_raw[:, s, :]
                pool.wait_ge(raw_in[s], 16 * i + 16)
                if not (first and s < 2):
                    pool.wait_ge(w_used, 4 * i + s - 1)
                pool.tensor_tensor(w_hi[:, c, :].rearrange("p (a n) -> p a n", n=P), raw.rearrange("p (a n) -> p a n", n=P),
                                   unit_scale, ALU.mult).then_inc(w_rounded, 1)
                pool.wait_ge(w_rounded, 4 * i + s + 1)
                pool.tensor_tensor(w_lo[:, c, :], raw, w_hi[:, c, :].bitcast(F32), ALU.subtract).then_inc(w_ready, 1)

            pool.wait_ge(ones_set, 1)
            for s in range(4):
                split(0, s, True)
            with pool.Fori(1, UNITS // 4) as i:
                for s in range(4):
                    split(i, s, False)
            for s in range(UNITS % 4):
                split(UNITS // 4, s, False)

        @block.tensor
        def _(pe):
            def fm_unit(c, out):
                for half in range(2):
                    o = out[:, half * HALF:(half + 1) * HALF]
                    for k in range(KT):
                        wh = w_hi[:, c, k * P:(k + 1) * P]
                        wl = w_lo[:, c, k * P:(k + 1) * P]
                        xh = h_hi[:, k, half * HALF:(half + 1) * HALF]
                        xl = h_lo[:, k, half * HALF:(half + 1) * HALF]
                        pe.matmul(o, wh, xh, start=(k == 0), stop=False)
                        pe.matmul(o, wh, xl, start=False, stop=False)
                        mm = pe.matmul(o, wl, xh, start=False, stop=(k == KT - 1))
                return mm

            def tm_rows(c, kk, k, t, start, stop):
                xh = h_hi[:, k, t * P:(t + 1) * P]
                xl = h_lo[:, k, t * P:(t + 1) * P]
                wh = w_hi[:, c, kk * HALF:(kk + 1) * HALF]
                wl = w_lo[:, c, kk * HALF:(kk + 1) * HALF]
                pe.matmul(psum[:, t, :], xh, wh, start=start, stop=False)
                pe.matmul(psum[:, t, :], xh, wl, start=False, stop=False)
                return pe.matmul(psum[:, t, :], xl, wh, start=False, stop=stop)

            def transposes(n, src):
                for k in range(KT):
                    if k >= 2:
                        pe.wait_ge(hi_done, 8 * n + k - 1)
                        pe.wait_ge(lo_done, 8 * n + k - 1)
                    for t in range(NT):
                        o = two_banks(2 + k % 2)[:, t * P:(t + 1) * P]
                        mm = pe.transpose(o, src(t, k), ident[:])
                    mm.then_inc(tr_full, 1)

            pe.wait_ge(vec_in, 16 * len(VEC))
            pe.wait_ge(const_in, 32)
            pe.transpose(psum[:, 4, 0:VROWS], arena[0:VROWS, JUNK0 * PAGE:JUNK0 * PAGE + P], ident[0:VROWS, 0:VROWS]).then_inc(vec_t, 1)
            pe.wait_ge(ada_acc, KT)
            pe.wait_ge(ones_set, 1)
            acc = page(ACC, 3)
            for f in range(16):
                mm = pe.matmul(psum[:, 5, f:f + 1], acc[:, f * P:(f + 1) * P], ones[:, 0:1], start=True, stop=True)
            mm.then_inc(mod_mm, 1)
            pe.wait_ge(row_in, 32)
            for n in range(2):
                pe.matmul(psum[:, n, :], ones[:], acc[:, 2 * D + n * HALF:2 * D + (n + 1) * HALF], start=True, stop=False)
                mm = pe.matmul(psum[:, n, :], ones[0:1, :], arena[0:1, ADAB * PAGE + n * HALF:ADAB * PAGE + (n + 1) * HALF],
                               start=False, stop=True)
            mm.then_inc(mod_mm, 1)
            pe.wait_ge(xn_done, NT)
            pe.wait_ge(mod_done, 3)
            x0 = tiles(X0)
            transposes(0, lambda t, k: x0[:, t, k * P:(k + 1) * P])
            pe.wait_ge(hi_done, 8)
            pe.wait_ge(lo_done, 8)

            V, KD, ATTN, SST = page(B_V), page(B_KD), page(B_ATT), page(B_S)

            def z_unit(u, j, out):
                pe.wait_ge(w_ready, u + 1)
                fm_unit(j % 2, out).then_inc(w_used, 1)

            def blocks128(x, i):
                return x[:, i * P:(i + 1) * P]

            def hgrn_a(h):
                pe.wait_ge(vt_done, h + 1)
                pe.wait_ge(qe_done, h + 1)
                for i in range(NT):
                    mm = pe.transpose(blocks128(two_banks(2), i), blocks128(page(B_VT), i), ident[:])
                mm.then_inc(task_full, 1)

            def hgrn_b(h):
                pe.wait_ge(kdec_done, h + 1)
                pe.wait_ge(eb_done, h + 1)
                for i in range(NT):
                    mm = pe.transpose(blocks128(two_banks(3), i), blocks128(page(B_KDT), i), ident[:])
                mm.then_inc(task_full, 1)
                pe.wait_ge(v_done, h + 1)
                pe.wait_ge(q_done, h + 1)
                pe.wait_ge(k_done, h + 1)
                for i in range(NT):
                    mm = pe.matmul(blocks128(two_banks(2), i), blocks128(page(B_K), i), blocks128(page(B_Q), i), start=True, stop=True)
                mm.then_inc(task_full, 1)
                pe.wait_ge(kd_done, h + 1)
                levels(h, 0, 3)

            def levels(h, j0, slot):
                for j in (j0, j0 + 1):
                    if j >= NL:
                        continue
                    pe.wait_ge(lvl_done, NL * h + j + 1)
                    kl, ql = page(B_KL + j % 2), page(B_QL)[:, (j % 2) * HALF:(j % 2 + 1) * HALF]
                    for i in range(NT):
                        mm = pe.matmul(psum[:, 2 * slot + j - j0, i * 64:(i + 1) * 64], blocks128(kl, i),
                                       ql[:, i * 64:(i + 1) * 64], start=True, stop=True)
                mm.then_inc(task_full, 1)

            def hgrn_c(h):
                pe.wait_ge(diag_done, h + 1)
                levels(h, 2, 2)
                pe.wait_ge(pick_done, NL * h + 2)
                levels(h, 4, 3)
                pe.wait_ge(pick_done, NL * h + 4)
                levels(h, 6, 2)
                pe.wait_ge(pick_done, NL * h + 6)
                for i in range(NT - 1):
                    mm = pe.matmul(blocks128(two_banks(3), i), blocks128(KD, i), blocks128(V, i), start=True, stop=True)
                mm.then_inc(task_full, 1)

            def hgrn_d(h):
                pe.wait_ge(pick_done, NL * h + NL)
                pe.wait_ge(s_done, (NT - 1) * h + NT - 1)
                pe.wait_ge(qe_done, h + 1)
                for i in range(NT):
                    mm = pe.matmul(blocks128(two_banks(2), i), blocks128(V, i), blocks128(ATTN, i), start=True, stop=(i == 0))
                    if i:
                        mm = pe.matmul(blocks128(two_banks(2), i), blocks128(SST, i - 1), blocks128(page(B_QE), i), start=False, stop=True)
                mm.then_inc(task_full, 1)
                pe.wait_ge(sq_done, h + 1)
                for half in range(2):
                    mm = pe.matmul(psum[:, 6 + half, :], ones[:], page(B_QL)[:, half * HALF:(half + 1) * HALF], start=True, stop=True)
                mm.then_inc(task_full, 1)

            for j in range(4):
                if j >= 2:
                    pe.wait_ge(sig_done, 1)
                    pe.wait_ge(g_done, 1)
                z_unit(j, j, two_banks(j % 2))
            with pe.Fori(1, HEADS) as it:
                pe.wait_ge(vt_done, it)
                z_unit(4 * it, 0, two_banks(0))
                hgrn_a(it - 1)
                pe.wait_ge(q_done, it)
                z_unit(4 * it + 1, 1, two_banks(1))
                hgrn_b(it - 1)
                pe.wait_ge(sig_done, it + 1)
                z_unit(4 * it + 2, 0, two_banks(0))
                hgrn_c(it - 1)
                pe.wait_ge(g_done, it + 1)
                z_unit(4 * it + 3, 1, two_banks(1))
                hgrn_d(it - 1)

            def pool_unit(g, j):
                if j % 2 == 0:
                    pe.wait_ge(pu_done, 2 * g + j // 2) if g or j else pe.wait_ge(vt_done, HEADS)
                else:
                    pe.wait_ge(pg_done, 2 * g + j // 2) if g or j > 1 else pe.wait_ge(q_done, HEADS)
                z_unit(U_POOL + 4 * g + j, j, two_banks(j % 2))

            def pool_mix(g):
                pe.wait_ge(pd_done, 2 * g + 2)
                pe.wait_ge(pw_in, 32)
                pw = page(PW[g // 2])[:, (g % 2) * HALF:(g % 2 + 1) * HALF].rearrange("p (c d) -> p c d", c=2)
                for dt in range(2):
                    if g:
                        pe.wait_ge(pmix_done, 2 * g + dt - 1)
                    else:
                        pe.wait_ge(o1_done if dt == 0 else ln_done, HEADS)
                    for half in range(2):
                        for c in range(2):
                            mm = pe.matmul(psum[:, 4 + 2 * dt + half, :], pw[:, c, dt * P:(dt + 1) * P],
                                           page(U_PAGES[g % 2][c])[:, half * HALF:(half + 1) * HALF],
                                           start=(c == 0), stop=(c == 1))
                    mm.then_inc(pm_full, 1)

            h = HEADS - 1
            pool_unit(0, 0)
            hgrn_a(h)
            pool_unit(0, 1)
            hgrn_b(h)
            pool_unit(0, 2)
            hgrn_c(h)
            pool_unit(0, 3)
            hgrn_d(h)
            for g in range(1, GROUPS):
                for j in range(4):
                    pool_unit(g, j)
                pool_mix(g - 1)
            pool_mix(GROUPS - 1)

            def ring_unit(u, j, s0, start, last, e, n):
                pe.wait_ge(w_ready, u + 1)
                c, slot = u_par(u, j), j_par(j)
                for kk in range(2):
                    pe.wait_ge(sp_lo, s0 + kk + 1)
                    for t in range(NT):
                        if start and kk == 0 and n:
                            pe.wait_ge(ycp_done, 16 * e + 8 * (n - 1) + t + 1)
                        mm = tm_rows(c, kk, 2 * slot + kk, t, start and kk == 0, last and kk == 1)
                        if last and kk == 1 and t < NT - 1:
                            mm.then_inc(yb_full, 1)
                mm.then_inc(w_used, 1)

            par = [0, 0]

            def u_par(u, j):
                return par[0]

            def j_par(j):
                return par[1]

            def stage_ring(e, U0, s_base, per):
                for n in range(2):
                    j0 = per * n
                    edge = [0] + ([per - 1] if per % 2 == 0 else [per - 2, per - 1])
                    mid = per - len(edge)
                    par[:] = [(U0 + j0) % 2, j0 % 2]
                    ring_unit(U0 + j0, j0, s_base + 2 * j0, True, False, e, n)
                    with pe.Fori(0, mid // 2) as i:
                        for a in range(2):
                            j = j0 + 1 + a
                            par[:] = [(U0 + j) % 2, j % 2]
                            ring_unit(2 * i + (U0 + j), None, 4 * i + (s_base + 2 * j), False, False, e, n)
                    for q in edge[1:]:
                        j = j0 + q
                        par[:] = [(U0 + j) % 2, j % 2]
                        ring_unit(U0 + j, j, s_base + 2 * j, False, q == per - 1, e, n)

            stage_ring(0, U_OUT, 0, 8)

            pe.wait_ge(xn_done, 2 * NT)
            transposes(1, lambda t, k: Y[:, t, k * P:(k + 1) * P])
            pe.wait_ge(hi_done, 16)
            pe.wait_ge(lo_done, 16)

            def tm_block(u, first, on_last, free):
                for j in range(4):
                    pe.wait_ge(w_ready, u + (j + 1))
                    for kk in range(2):
                        k = 2 * j + kk
                        for t in range(NT):
                            if k == 0 and free is not None:
                                free(t)
                            mm = tm_rows(j % 2, kk, k, t, k == 0, k == KT - 1)
                            if k == KT - 1 and t < NT - 1:
                                mm.then_inc(on_last, 1)
                    mm.then_inc(w_used, 1)

            tm_block(U_IN2, True, in2_full, None)
            with pe.Fori(1, 5) as b:
                tm_block(4 * b + U_IN2, False, in2_full, lambda t: pe.wait_ge(in2_free, 8 * b + (t - 7)))

            pe.wait_ge(in2_free, 40)
            pe.wait_ge(tril_done, 1)
            for g in range(SGU_G):
                mm = pe.transpose(blocks128(two_banks(0), g), blocks128(page(SPAT), g), ident[:])
            mm.then_inc(spat_full, 1)
            pe.wait_ge(spat_tr, 1)
            pe.wait_ge(ln2_done, 1)
            for g in range(SGU_G):
                if g >= 2:
                    pe.wait_ge(sgu_done, g - 1)
                pe.matmul(psum[:, 2 + g % 2, :], blocks128(page(SPAT_T), g), vs_b[:, :, g * DH:(g + 1) * DH],
                          start=True, stop=True).then_inc(sgu_full, 1)

            pe.wait_ge(rope_done, 2)
            transposes(2, lambda t, k: (q_b, k_b)[k // 4][:, t, (k % 4) * P:(k % 4 + 1) * P])
            pe.wait_ge(hi_done, 24)
            pe.wait_ge(lo_done, 24)
            pe.wait_ge(sgu_done, 8)

            def qk(n):
                i, h = n // AH, n % AH
                if n >= 2:
                    pe.wait_ge(s_moved, n - 1)
                po = DH * (h % 2)
                for c0 in range(0, (i + 1) * P, HALF):
                    c1 = min(c0 + HALF, (i + 1) * P)
                    o = two_banks(n % 2)[:, c0:c1]
                    qh, ql = [x[po:po + DH, h // 2, i * P:(i + 1) * P] for x in (h_hi, h_lo)]
                    kh, kl = [x[po:po + DH, 4 + h // 2, c0:c1] for x in (h_hi, h_lo)]
                    pe.matmul(o, qh, kh, start=True, stop=False)
                    pe.matmul(o, qh, kl, start=False, stop=False)
                    mm = pe.matmul(o, ql, kh, start=False, stop=True)
                mm.then_inc(s_full, 1)

            def p_t(n):
                pe.wait_ge(p_done, n + 1)
                if n:
                    pe.wait_ge(pt_done, n)
                for j in range(n // AH + 1):
                    mm = pe.transpose(blocks128(two_banks(2), j), blocks128(probs[n % 4], j), ident[:])
                mm.then_inc(pt_full, 1)

            def pv(n):
                i, h = n // AH, n % AH
                pe.wait_ge(pt_done, n + 1)
                if i >= 2:
                    pe.wait_ge(ao_done, i - 1)
                for j in range(i + 1):
                    mm = pe.matmul(psum[:, 6 + i % 2, h * DH:(h + 1) * DH], blocks128(probs_t[n % 2], j),
                                   v_b[:, j, h * DH:(h + 1) * DH], start=(j == 0), stop=(j == i))
                mm.then_inc(pv_full, 1)

            N = AH * NT
            for n in range(N + 3):
                if n < N:
                    qk(n)
                if 0 <= n - 2 < N:
                    p_t(n - 2)
                if 0 <= n - 3 < N:
                    pv(n - 3)

            pe.wait_ge(mixn_done, 2 * NT)
            transposes(3, lambda t, k: (att_o, u_b)[k // 4][:, t, (k % 4) * P:(k % 4 + 1) * P])
            pe.wait_ge(hi_done, 32)
            pe.wait_ge(lo_done, 32)
            tm_block(U_OUT2, True, yb_full, None)

            def y_free(t):
                pe.wait_ge(ycp_done, 16 + t + 1)
            tm_block(U_OUT2 + 4, False, yb_full, y_free)

            pe.wait_ge(xn_done, 3 * NT)
            transposes(4, lambda t, k: Y[:, t, k * P:(k + 1) * P])
            pe.wait_ge(hi_done, 40)
            pe.wait_ge(lo_done, 40)

            def gu_unit(i, j, first):
                if not first:
                    pe.wait_ge(gate_silu if j % 2 == 0 else act_done, 2 * i + (j // 2 - 1))
                pe.wait_ge(w_ready, 4 * i + (U_GU + j + 1))
                fm_unit(j % 2, two_banks(j)).then_inc(w_used, 1)

            for j in range(4):
                gu_unit(0, j, True)
            with pe.Fori(1, FT // 2) as i:
                for j in range(4):
                    gu_unit(i, j, False)
            pe.wait_ge(act_done, FT)
            stage_ring(2, U_DOWN, 32, 11)

        @block.scalar
        def _(act):
            A = act.activation

            def copy(out, in_):
                return A(out, in_, ACT.Copy)

            for t in range(NT):
                act.dma_start(tiles(X0)[:, t, :], ap["x"][0, t * P:(t + 1) * P, :]).then_inc(x_in[t], 16)
            act.wait_ge(cols_done, 1)
            A(silu_c, col("c", 0, 8), ACT.Silu).then_inc(silu_done, 1)
            act.wait_ge(lb_step, 1)
            A(lb_tmp, lb_tmp, ACT.Exp).then_inc(lb_exp, 1)

            def squares(n, src, junk, count):
                for t in range(NT):
                    if n + t:
                        act.wait_ge(ss_done, n + t)
                    A(junk, src(t), ACT.Square, accum_out=ss[:, t:t + 1]).then_inc(ss_done, 1)

            def root(m):
                act.wait_ge(ms_done, m + 1)
                A(ms, ms, ACT.Sqrt).then_inc(sqrt_done, 1)

            def take_hi(n, mul=None, add=None):
                for k in range(KT):
                    act.wait_ge(tr_full, 8 * n + k + 1)
                    src = two_banks(2 + k % 2)
                    if mul is None:
                        copy(h_hi[:, k, :], src).then_inc(hi_done, 1)
                    else:
                        A(h_hi[:, k, :], src, ACT.Identity, scale=mul(k), bias=add(k) if add else 0.0).then_inc(hi_done, 1)

            act.wait_ge(vec_t, 1)
            for t in range(NT):
                act.wait_ge(x_in[t], 16)
                if t:
                    act.wait_ge(ss_done, t)
                A(page(JUNK0), tiles(X0)[:, t, :], ACT.Square, accum_out=ss[:, t:t + 1]).then_inc(ss_done, 1)
            root(0)
            act.wait_ge(mod_done, 2)
            take_hi(0, lambda k: mul_a[:, k:k + 1], lambda k: mod[:, k:k + 1])

            bB, qe, vt = page(B_B), page(B_QE), page(B_VT)

            def span_exp(h, j):
                act.wait_ge(d_done, NL * h + j + 1)
                A(page(B_D + j % 2), page(B_D + j % 2), ACT.Exp).then_inc(e_done, 1)

            def front(it, z0):
                act.wait_ge(w_used, z0 + 1)
                if not (type(it) is int and it == 0):
                    act.wait_ge(fc_done, it)
                A(page(B_SIG), two_banks(0), ACT.Sigmoid).then_inc(sig_done, 1)
                act.wait_ge(w_used, z0 + 2)

            def logs(it):
                act.wait_ge(fc_done, it + 1)
                A(bB, bB, ACT.Ln).then_inc(lf_done, 1)
                act.wait_ge(b_done, it + 1)
                A(end_decay, bB.rearrange("p (c t) -> p c t", t=P)[:, :, P - 1], ACT.Exp).then_inc(end_done, 1)
                act.wait_ge(dk_done, it + 1)
                A(page(B_KDT), page(B_KDT), ACT.Exp).then_inc(ek_done, 1)

            def take_q(it, z0):
                act.wait_ge(w_used, z0 + 4)
                if not (type(it) is int and it == 0):
                    act.wait_ge(lvl_done, NL * it)
                copy(page(B_Q), two_banks(1)).then_inc(q_done, 1)

            def take_v(it, z0):
                act.wait_ge(w_used, z0 + 3)
                copy(vt, two_banks(0)).then_inc(vt_done, 1)

            def back_a(h):
                act.wait_ge(b_done, h + 1)
                A(qe, bB, ACT.Exp).then_inc(eb_done, 1)
                span_exp(h, 0)
                span_exp(h, 1)
                act.wait_ge(task_full, 10 * h + 1)
                copy(page(B_V), two_banks(2)).then_inc(v_done, 1)
                act.wait_ge(task_full, 10 * h + 2)
                copy(page(B_KD), two_banks(3)).then_inc(kd_done, 1)
                span_exp(h, 2)
                span_exp(h, 3)

            def back_b(h):
                for j in range(4, NL):
                    span_exp(h, j)

            def back_c(h):
                act.wait_ge(task_full, 10 * h + 9)
                A(page(B_QL), two_banks(2), ACT.Square).then_inc(sq_done, 1)
                act.wait_ge(task_full, 10 * h + 10)
                A(page(B_KL), two_banks(3), ACT.Ln, scale=1.0 / P, bias=EPS).then_inc(ln_done, 1)
                act.wait_ge(ln_done, h + 1)
                A(page(B_KL), page(B_KL), ACT.Exp, scale=-0.5).then_inc(rs_done, 1)

            def mix_slot(it):
                return arena[:, bass.ds((MIX + 8 + it) * PAGE, PAGE)]

            front(0, 0)
            A(mix_slot(0), two_banks(1), ACT.Sigmoid).then_inc(gsig_done, 1)
            take_v(0, 0)
            logs(0)
            take_q(0, 0)
            with act.Fori(1, HEADS) as it:
                back_a(it - 1)
                front(it, 4 * it)
                A(mix_slot(it), two_banks(1), ACT.Sigmoid).then_inc(gsig_done, 1)
                back_b(it - 1)
                take_v(it, 4 * it)
                logs(it)
                take_q(it, 4 * it)
                back_c(it - 1)

            def pool_in(g, j):
                act.wait_ge(w_used, U_POOL + 4 * g + j + 1)
                if j % 2 == 0:
                    if g >= 2:
                        act.wait_ge(pm_full, 2 * (g - 2) + 2)
                    copy(page(U_PAGES[g % 2][j // 2]), two_banks(0)).then_inc(pu_done, 1)
                else:
                    A(mixp[2 * g + j // 2], two_banks(1), ACT.Sigmoid).then_inc(pgs_done, 1)

            h = HEADS - 1
            back_a(h)
            act.dma_start(page(PW[0]).rearrange("p (g c d) -> p g c d", g=2, c=2),
                          ap["pool_w"][0, 0:2].rearrange("g (c p) d -> p g c d", p=P)).then_inc(pw_in, 16)
            act.wait_ge(fc_done, HEADS)
            pool_in(0, 0)
            pool_in(0, 1)
            back_b(h)
            pool_in(0, 2)
            pool_in(0, 3)
            back_c(h)
            act.dma_start(page(PW[1]).rearrange("p (g c d) -> p g c d", g=2, c=2),
                          ap["pool_w"][0, 2:4].rearrange("g (c p) d -> p g c d", p=P)).then_inc(pw_in, 16)
            act.dma_start(page(RC)[:, 0:64], ap["k_inv_count"]).then_inc(rc_in, 16)
            for g in range(1, GROUPS):
                for j in range(4):
                    pool_in(g, j)

            def ring_hi(s0, u0, srcs, j0=0):
                for a, src in enumerate(srcs):
                    j = j0 + a // 2
                    if a % 2 == 0 and j >= 2:
                        act.wait_ge(w_used, u0 + j - 1)
                    copy(h_hi[:, 2 * (j % 2) + a % 2, :], src).then_inc(sp_hi, 1)

            def y_squares(e, n, src):
                for t in range(NT):
                    act.wait_ge(ycp_done, 16 * e + 8 * n + t + 1)
                    if 8 * n + t + 16 * e:
                        act.wait_ge(ysq_done, 16 * e + 8 * n + t)
                    A(h_hi[:, 7, 0:HALF] if e == 2 else page(25)[:, 0:HALF], src(t), ACT.Square,
                      accum_out=ss[:, 8 * n + t:8 * n + t + 1]).then_inc(ysq_done, 1)

            act.wait_ge(w_used, U_OUT)
            act.wait_ge(o_done, HEADS)
            act.wait_ge(pmix_done, 8)
            ring_hi(0, U_OUT, mixp)
            y_squares(0, 0, lambda t: Y[:, t, 0:HALF])
            ring_hi(16, U_OUT, mixp, 8)
            y_squares(0, 1, lambda t: Y[:, t, HALF:D])

            def residual_squares(n, done, spill, sem_out):
                for t in range(NT):
                    act.wait_ge(res_done, n + t + 1)
                    act.wait_ge(ss_done, done + t)
                    A(page(25), XR[:, t, :], ACT.Square, accum_out=ss[:, t:t + 1]).then_inc(ss_done, 1)
                    act.dma_start(spill[t], XR[:, t, :]).then_inc(sem_out, 16)

            root(1)
            act.wait_ge(rstd_done, 2)
            residual_squares(0, 8, x_mid[0], spilled[0])
            root(2)
            take_hi(1, lambda k: col("pre_mix_norm_2", k))

            act.wait_ge(tr_full, 16)
            act.wait_ge(ss_done, 16)
            act.dma_start(LN_ROWS[:, 0:512], ap["sgu_ln_gain_2"][0].partition_broadcast(P)).then_inc(lnrow_in, 16)
            act.dma_start(LN_ROWS[:, 512:1024], ap["sgu_ln_bias_2"][0].partition_broadcast(P)).then_inc(lnrow_in, 16)
            act.dma_start(page(SPAT).rearrange("p (g j) -> p g j", g=SGU_G), ap["sgu_w_spatial_2"][0].rearrange("g i j -> i g j")).then_inc(spat_in, 16)
            act.dma_start(page(25)[:, 0:P], ap["k_tril"]).then_inc(spat_in, 16)
            act.dma_start(ROPE[:, 320:328], ap["k_inv_freq"]).then_inc(freq_in, 16)
            act.wait_ge(spilled[0], 16 * NT)
            for b, dst in enumerate((vs_b, u_b)):
                for t in range(NT):
                    if t < NT - 1:
                        act.wait_ge(in2_full, 7 * b + t + 1)
                    else:
                        act.wait_ge(w_used, U_IN2 + 4 * b + 4)
                    kw = {"accum_out": sums[:, t:t + 1]} if b == 0 else {}
                    A(dst[:, t, :], psum[:, t, :], ACT.Gelu, **kw).then_inc(in2_free, 1)
            act.wait_ge(mean_done, 1)
            for t in range(NT):
                if t:
                    act.wait_ge(var_done, t)
                A(JUNK3, vs_b[:, t, :], ACT.Square, bias=mean[:, t:t + 1], accum_out=ss[:, t:t + 1]).then_inc(var_done, 1)
            root(3)
            act.wait_ge(rope_step, ROPE_STEPS)
            A(ROPE[:, 0:64], ROPE[:, 0:64], ACT.Sin).then_inc(trig_done, 1)
            A(ROPE[:, 64:128], ROPE[:, 64:128], ACT.Sin).then_inc(trig_done, 1)
            act.wait_ge(spat_full, 1)
            copy(page(SPAT_T), two_banks(0)).then_inc(spat_tr, 1)
            act.wait_ge(tril_done, 1)
            act.dma_start(BIAS, ap["k_bias"]).then_inc(bias_in, 16)
            take_hi(2)

            N = AH * NT

            def pt_copy(n):
                w = (n // AH + 1) * P
                act.wait_ge(pt_full, n + 1)
                if n >= 2:
                    act.wait_ge(pv_full, n - 1)
                else:
                    act.wait_ge(sgu_full, SGU_G)
                copy(probs_t[n % 2][:, 0:w], two_banks(2)[:, 0:w]).then_inc(pt_done, 1)

            for n in range(N + 2):
                if n < N:
                    w = (n // AH + 1) * P
                    act.wait_ge(max_done, n + 1)
                    A(probs[n % 4][:, 0:w], probs[n % 4][:, 0:w], ACT.Exp, bias=neg_max[:, n % 8:n % 8 + 1],
                      accum_out=den_[:, n:n + 1]).then_inc(p_done, 1)
                if n >= 2:
                    pt_copy(n - 2)

            for a, (src, row) in enumerate(((att_o, ao_done), (u_b, sgu_done))):
                act.wait_ge(row, 8)
                for t in range(NT):
                    act.wait_ge(ss_done, 16 + 8 * a + t)
                    A(JUNK3, src[:, t, :], ACT.Square, accum_out=ss[:, t + 8 * a:t + 8 * a + 1]).then_inc(ss_done, 1)
            root(4)
            root(5)
            take_hi(3, lambda k: cols[:, VROW["attn_out_norm_2"] + k:VROW["attn_out_norm_2"] + k + 1])
            act.dma_start(POST_ROW, ap["post_mix_norm_2"][0].partition_broadcast(P)).then_inc(row_in, 16)

            y_squares(1, 0, lambda t: Y[:, t, 0:HALF])
            y_squares(1, 1, lambda t: Y[:, t, HALF:D])
            root(6)
            act.wait_ge(rstd_done, 7)
            residual_squares(NT, 32, x_mid[1], spilled[1])
            root(7)
            take_hi(4, lambda k: col("pre_ffn_norm_2", k))
            act.dma_start(ROW_F, ap["post_ffn_norm_2"][0].partition_broadcast(P)).then_inc(row_in, 16)

            act.wait_ge(spilled[1], 16 * NT)
            act.wait_ge(tr_full, 40)
            with act.Fori(0, FT // 2) as i:
                for j in range(2):
                    act.wait_ge(w_used, 4 * i + (U_GU + 2 * j + 1))
                    A(arena[:, bass.ds((2 * i + j) * PAGE, PAGE)], two_banks(2 * j), ACT.Silu).then_inc(gate_silu, 1)
            act.wait_ge(act_done, FT)
            act.wait_ge(w_used, U_DOWN)
            ring_hi(32, U_DOWN, actp)
            y_squares(2, 0, lambda t: y_half0[:, t, :])
            ring_hi(32 + FT, U_DOWN, actp, 11)
            y_squares(2, 1, lambda t: y_half1[:, t, :])
            root(8)

        @block.vector
        def _(dve):
            TT, TS, STT = dve.tensor_tensor, dve.tensor_scalar, dve.scalar_tensor_tensor

            def stats(m, src, width, eps):
                TS(ms, src, 1.0 / width, eps, ALU.mult, ALU.add).then_inc(ms_done, 1)
                dve.wait_ge(sqrt_done, m + 1)
                dve.reciprocal(rstd, ms).then_inc(rstd_done, 1)
                dve.wait_ge(rstd_done, m + 1)

            def take_lo(n, mul=None, add=None):
                for k in range(KT):
                    dve.wait_ge(hi_done, 8 * n + k + 1)
                    src = two_banks(2 + k % 2)
                    hi = h_hi[:, k, :].bitcast(F32)
                    if mul is None:
                        TT(h_lo[:, k, :], src, hi, ALU.subtract).then_inc(lo_done, 1)
                    elif add is None:
                        STT(h_lo[:, k, :], src, mul(k), hi, ALU.mult, ALU.subtract).then_inc(lo_done, 1)
                    else:
                        if k:
                            dve.wait_ge(lo_done, 8 * n + k)
                        TS(page(JUNK0), src, mul(k), add(k), ALU.mult, ALU.add).then_inc(lo_tmp, 1)
                        dve.wait_ge(lo_tmp, k + 1)
                        TT(h_lo[:, k, :], page(JUNK0), hi, ALU.subtract).then_inc(lo_done, 1)

            dve.memset(ones[:], 1.0).then_inc(ones_set, 1)
            dve.wait_ge(vec_t, 1)
            dve.tensor_copy(cols[:], psum[:, 4, 0:VROWS]).then_inc(cols_done, 1)
            dve.wait_ge(cols_done, 1)
            TT(lb_tmp, col("hgrn_lower_bounds", 0, 8), col("hgrn_lower_bounds", 0, 8), ALU.subtract).then_inc(lb_step, 1)
            dve.wait_ge(lb_exp, 1)
            dve.reciprocal(lb, lb_tmp).then_inc(lb_step, 1)
            dve.wait_ge(lb_step, 2)
            TT(lb_tmp, lb_tmp, lb, ALU.mult).then_inc(lb_step, 1)
            dve.wait_ge(lb_step, 3)
            TT(lb, lb_tmp, lb_tmp, ALU.subtract).then_inc(lb_step, 1)
            dve.wait_ge(lb_step, 4)
            TS(one_lb, lb, -1.0, 1.0, ALU.mult, ALU.add).then_inc(lb_step, 1)
            dve.wait_ge(silu_done, 1)
            acc = page(ACC, 3)
            x0 = tiles(X0)
            for k in range(KT):
                if k == 4:
                    dve.wait_ge(ss_done, NT)
                    stats(0, ss[:, 0:8], D, EPS)
                    for t in range(NT):
                        TS(x0[:, t, :], x0[:, t, :], rstd[:, t:t + 1], None, ALU.mult).then_inc(xn_done, 1)
                dve.wait_ge(ada_in[k % 3], 16 * (k // 3 + 1))
                w = page(ADA + 3 * (k % 3), 3)
                if k == 0:
                    TS(acc, w, silu_c[:, 0:1], None, ALU.mult).then_inc(ada_acc, 1)
                else:
                    dve.wait_ge(ada_acc, k)
                    STT(acc, w, silu_c[:, k:k + 1], acc, ALU.mult, ALU.add).then_inc(ada_acc, 1)
            dve.wait_ge(mod_mm, 1)
            TT(mod, psum[:, 5, 0:16], col("ada_b", 0, 16), ALU.add).then_inc(mod_done, 1)
            dve.wait_ge(mod_done, 1)
            STT(mul_a, mod[:, 8:16], 1.0, col("norm_pre_w", 0, 8), ALU.add, ALU.mult).then_inc(mod_done, 1)
            dve.wait_ge(mod_done, 2)
            dve.wait_ge(mod_mm, 2)
            dve.wait_ge(row_in, 32)
            TT(gate_row, two_banks(0), page(NPOST), ALU.mult).then_inc(mod_done, 1)
            take_lo(0, lambda k: mul_a[:, k:k + 1], lambda k: mod[:, k:k + 1])

            sig, kk_, bb, qq, qe = page(B_SIG), page(B_K), page(B_B), page(B_Q), page(B_QE)
            b_chunks = bb.rearrange("p (c t) -> p c t", t=P)

            def gate_g(it):
                dve.wait_ge(gsig_done, it + 1)
                m = arena[:, bass.ds((MIX + 8 + it) * PAGE, PAGE)]
                TT(m, m, two_banks(1), ALU.mult).then_inc(g_done, 1)

            def gates(it, i):
                dve.wait_ge(sig_done, it + 1)
                dve.wait_ge(lb_step, 5)
                TS(sig, sig, one_lb[:, bass.ds(i, 1)], lb[:, bass.ds(i, 1)], ALU.mult, ALU.add).then_inc(f_done, 1)
                dve.wait_ge(f_done, it + 1)
                TS(kk_, sig, -1.0, 1.0, ALU.mult, ALU.add).then_inc(k_done, 1)
                TS(bb, sig, F_MIN, None, ALU.max).then_inc(fc_done, 1)
                dve.wait_ge(lf_done, it + 1)
                for c in range(NT):
                    x = dve.tensor_tensor_scan(b_chunks[:, c, :], ones[:], b_chunks[:, c, :], 0.0, ALU.mult, ALU.add)
                x.then_inc(b_done, 1)
                dve.wait_ge(b_done, it + 1)
                kdt = page(B_KDT)
                TT(kdt.rearrange("p (c t) -> p c t", t=P), b_chunks[:, :, P - 1:P].to_broadcast([P, NT, P]), b_chunks, ALU.subtract).then_inc(dk_done, 1)
                dve.wait_ge(ek_done, it + 1)
                TT(kdt, kdt, kk_, ALU.mult).then_inc(kdec_done, 1)

            def halves(x, w):
                return x.rearrange("p (n u w) -> p n u w", u=2, w=w)

            def span_d(h, j):
                w = SPANS[j]
                d, b4 = halves(page(B_D + j % 2), w), halves(bb, w)
                ref = b4[:, :, 0, w - 1:w].to_broadcast([P, S // (2 * w), w])
                if j >= 2:
                    dve.wait_ge(lvl_done, NL * h + j - 1)
                else:
                    dve.wait_ge(qe_done, h + 1)
                TT(d[:, :, 1, :], b4[:, :, 1, :], ref, ALU.subtract)
                TT(d[:, :, 0, :], ref, b4[:, :, 0, :], ALU.subtract).then_inc(d_done, 1)

            def span_kq(h, j):
                w = SPANS[j]
                e = page(B_D + j % 2)
                dve.wait_ge(e_done, NL * h + j + 1)
                if j >= 2:
                    dve.wait_ge(task_full, 10 * h + 4 + (j - 2) // 2)
                TT(page(B_KL + j % 2), kk_, e, ALU.mult).then_inc(kl_done, 1)
                ql = page(B_QL)[:, (j % 2) * HALF:(j % 2 + 1) * HALF].rearrange("p (n w) -> p n w", w=w)
                TT(ql, halves(qq, w)[:, :, 1, :], halves(e, w)[:, :, 1, :], ALU.mult).then_inc(lvl_done, 1)

            att3 = page(B_ATT).rearrange("p (i t) -> p i t", t=P)

            def pick(h, j, at):
                w = SPANS[j]
                slot = 3 if (j // 2) % 2 == 0 else 2
                dve.wait_ge(const_in, 32)
                dve.wait_ge(task_full, at[j][0])
                dve.wait_ge(pick_done if j else diag_done, at[j][1])
                to = page(B_ATT).rearrange("p (n u w) -> p n u w", u=2, w=w)[:, :, 1, :]
                nb = P // (2 * w)
                data = psum[:, 2 * slot + j % 2, :]
                m = lvl_mask[:, j, :]
                if w == 64:
                    dve.copy_predicated(to, m.rearrange("p (a c) -> p a c", a=1).to_broadcast([P, NT, 64]),
                                        data.rearrange("p (i c) -> p i c", c=64)).then_inc(pick_done, 1)
                else:
                    to = page(B_ATT).rearrange("p (i n u w) -> p i n u w", i=NT, u=2, w=w)[:, :, :, 1, :]
                    dve.copy_predicated(to, m.rearrange("p (a n w) -> p a n w", a=1, w=w).to_broadcast([P, NT, nb, w]),
                                        data.rearrange("p (i n w) -> p i n w", i=NT, w=w)).then_inc(pick_done, 1)

            def back_1(h):
                dve.wait_ge(eb_done, h + 1)
                dve.wait_ge(q_done, h + 1)
                TT(qe, qe, qq, ALU.mult).then_inc(qe_done, 1)
                span_d(h, 0)
                span_d(h, 1)
                span_kq(h, 0)
                span_kq(h, 1)
                span_d(h, 2)
                span_d(h, 3)
                dve.wait_ge(task_full, 10 * h + 3)
                TT(att3, two_banks(2).rearrange("p (i t) -> p i t", t=P), IDM[:].rearrange("p (a t) -> p a t", a=1).to_broadcast([P, NT, P]), ALU.mult).then_inc(diag_done, 1)

            def back_2(h):
                at = [(10 * h + (4 + j // 2 if j < NL - 1 else 8), NL * h + j if j else h + 1) for j in range(NL)]
                if type(h) is not int:
                    at = [tuple(dve.snap(x) for x in a) for a in at]
                span_kq(h, 2)
                span_kq(h, 3)
                span_d(h, 4)
                span_d(h, 5)
                pick(h, 0, at)
                pick(h, 1, at)
                span_kq(h, 4)
                span_kq(h, 5)
                span_d(h, 6)
                pick(h, 2, at)
                pick(h, 3, at)
                span_kq(h, 6)
                pick(h, 4, at)
                pick(h, 5, at)
                dve.wait_ge(task_full, 10 * h + 8)
                dve.wait_ge(end_done, h + 1)
                sst = page(B_S)
                for c in range(NT - 1):
                    u = two_banks(3)[:, c * P:(c + 1) * P]
                    if c == 0:
                        dve.tensor_copy(sst[:, 0:P], u).then_inc(s_done, 1)
                    else:
                        dve.wait_ge(s_done, (NT - 1) * h + c)
                        STT(sst[:, c * P:(c + 1) * P], sst[:, (c - 1) * P:c * P], end_decay[:, c:c + 1], u, ALU.mult, ALU.add).then_inc(s_done, 1)
                pick(h, 6, at)

            def back_3(h):
                dve.wait_ge(rs_done, h + 1)
                t1 = page(B_ATT)
                STT(t1, two_banks(2), col("hgrn_norm_w"), page(B_KL), ALU.mult, ALU.mult).then_inc(o1_done, 1)
                dve.wait_ge(o1_done, h + 1)
                dve.wait_ge(g_done, h + 1)
                m = arena[:, bass.ds((MIX + 8 + h) * PAGE, PAGE)]
                TT(m, m, t1, ALU.mult).then_inc(o_done, 1)

            gate_g(0)
            gates(0, 0)
            with dve.Fori(1, HEADS) as it:
                back_1(it - 1)
                gate_g(it)
                back_2(it - 1)
                gates(it, it)
                back_3(it - 1)

            def pool_gate(g, j):
                dve.wait_ge(pgs_done, 2 * g + j + 1)
                m = mixp[2 * g + j]
                TT(m, m, two_banks(1), ALU.mult).then_inc(pg_done, 1)

            steps = [0]

            def step(x):
                x.then_inc(win_step, 1)
                steps[0] += 1
                dve.wait_ge(win_step, steps[0])

            def window(g):
                for c in range(2):
                    dve.wait_ge(pu_done, 2 * g + c + 1)
                    u = page(U_PAGES[g % 2][c])
                    src, w = u, 1
                    for a in range(g + 1):
                        dst = page((S_A, S_B)[a % 2])
                        dve.tensor_copy(dst[:, 0:w], src[:, 0:w]).then_inc(win_step, 1)
                        steps[0] += 1
                        step(TT(dst[:, w:S], src[:, w:S], src[:, 0:S - w], ALU.add))
                        src, w = dst, 2 * w
                    dve.wait_ge(rc_in, 16)
                    step(TT(src[:, 0:w], src[:, 0:w], page(RC)[:, 16 * g:16 * g + w], ALU.mult))
                    TT(u[:, 0:w], src[:, 0:w], u[:, 0:w], ALU.subtract).then_inc(win_step, 1)
                    steps[0] += 1
                    STT(u[:, w:S], src[:, w:S], 1.0 / w, u[:, w:S], ALU.mult, ALU.subtract).then_inc(pd_done, 1)
                    dve.wait_ge(pd_done, 2 * g + c + 1)

            def pool_out(g):
                for dt in range(2):
                    dve.wait_ge(pm_full, 2 * g + dt + 1)
                    dve.wait_ge(pg_done, 2 * g + dt + 1)
                    m = mixp[2 * g + dt]
                    STT(m, two_banks(2 + dt), col("pool_scale", 2 * g + dt), m, ALU.mult, ALU.mult).then_inc(pmix_done, 1)

            h = HEADS - 1
            back_1(h)
            pool_gate(0, 0)
            back_2(h)
            pool_gate(0, 1)
            back_3(h)
            window(0)
            for g in range(1, GROUPS):
                pool_gate(g, 0)
                pool_gate(g, 1)
                pool_out(g - 1)
                window(g)
            pool_out(GROUPS - 1)

            def ring_lo(s0, u0, srcs, j0=0):
                for a, src in enumerate(srcs):
                    j = j0 + a // 2
                    k = 2 * (j % 2) + a % 2
                    dve.wait_ge(sp_hi, s0 + a + 1)
                    TT(h_lo[:, k, :], src, h_hi[:, k, :].bitcast(F32), ALU.subtract).then_inc(sp_lo, 1)

            def y_copy(e, n, u_last, dst):
                for t in range(NT):
                    if t < NT - 1:
                        dve.wait_ge(yb_full, 14 * e + 7 * n + t + 1)
                    else:
                        dve.wait_ge(w_used, u_last)
                    dve.tensor_copy(dst(t), psum[:, t, :]).then_inc(ycp_done, 1)

            def post(e, m, y):
                dve.wait_ge(ysq_done, 16 * e + 16)
                dve.wait_ge(ycp_done, 16 * e + 16)
                TT(sums, ss[:, 0:8], ss[:, 8:16], ALU.add).then_inc(sum_done, 1)
                dve.wait_ge(sum_done, e + 1)
                stats(m, sums, D, EPS)
                for t in range(NT):
                    yy = y(t)
                    for i, (o, r) in enumerate(yy):
                        x = STT(o, o, rstd[:, t:t + 1], r, ALU.mult, ALU.mult)
                        x.then_inc(res_step, 1)
                    dve.wait_ge(res_step, res_n[0] + len(yy))
                    res_n[0] += len(yy)
                    dve.wait_ge(x_in[t], 16 * (e + 2))
                    for i, (o, r) in enumerate(yy):
                        w = D // len(yy)
                        x = TT(XR[:, t, i * w:(i + 1) * w], XR[:, t, i * w:(i + 1) * w], o, ALU.add)
                    x.then_inc(res_done, 1)
            res_n = [0]

            def next_norm(m, done):
                dve.wait_ge(ss_done, done)
                stats(m, ss[:, 0:8], D, EPS)
                for t in range(NT):
                    TS(Y[:, t, :], XR[:, t, :], rstd[:, t:t + 1], None, ALU.mult).then_inc(xn_done, 1)

            ring_lo(0, U_OUT, mixp)
            y_copy(0, 0, U_OUT + 8, lambda t: Y[:, t, 0:HALF])
            ring_lo(16, U_OUT, mixp, 8)
            y_copy(0, 1, U_OUT + 16, lambda t: Y[:, t, HALF:D])
            post(0, 1, lambda t: [(Y[:, t, :], gate_row)])
            next_norm(2, 16)
            take_lo(1, lambda k: col("pre_mix_norm_2", k))

            dve.wait_ge(spat_in, 32)
            dve.wait_ge(tr_full, 16)
            sp3 = page(SPAT).rearrange("p (g j) -> p g j", g=SGU_G)
            tril = page(25)[:, 0:P].rearrange("p (a j) -> p a j", a=1).to_broadcast([P, SGU_G, P])
            TT(sp3, sp3, tril, ALU.mult).then_inc(tril_done, 1)

            steps_r = [0]

            def rstep(x):
                x.then_inc(rope_step, 1)
                steps_r[0] += 1
                dve.wait_ge(rope_step, steps_r[0])

            dve.wait_ge(pos_in, 16)
            dve.wait_ge(freq_in, 16)
            ang, ang2, turns, wrap = [ROPE[:, 64 * i:64 * (i + 1)] for i in range(4)]
            turns_i = ROPE[:, 256:320].bitcast(I32)
            freq, posf = ROPE[:, 320:328], ROPE[:, 328:336]
            rstep(dve.tensor_copy(posf, pos.bitcast(I32)))
            rstep(TT(ang.rearrange("p (t f) -> p t f", f=ROT),
                     posf.rearrange("p (t a) -> p t a", a=1).to_broadcast([P, NT, ROT]),
                     freq.rearrange("p (a f) -> p a f", a=1).to_broadcast([P, NT, ROT]), ALU.mult))
            rstep(TS(turns_i, ang, 1.0 / TWO_PI, None, ALU.mult))
            rstep(dve.tensor_copy(turns, turns_i))
            rstep(STT(ang, turns, -TWO_PI_HI, ang, ALU.mult, ALU.add))
            rstep(STT(ang, turns, -TWO_PI_LO, ang, ALU.mult, ALU.add))

            def wrapped(x):
                rstep(TS(wrap, x, math.pi, -TWO_PI, ALU.is_gt, ALU.mult))
                rstep(TT(x, x, wrap, ALU.add))
                rstep(TS(wrap, x, -math.pi, TWO_PI, ALU.is_lt, ALU.mult))
                rstep(TT(x, x, wrap, ALU.add))
                rstep(TS(x, x, PI_IN, -PI_IN, ALU.min, ALU.max))

            wrapped(ang)
            rstep(TS(ang2, ang, math.pi / 2, None, ALU.add))
            wrapped(ang2)
            assert steps_r[0] == ROPE_STEPS

            dve.wait_ge(in2_free, NT)
            TS(mean, sums, -1.0 / ATT, None, ALU.mult).then_inc(mean_done, 1)
            dve.wait_ge(var_done, NT)
            stats(3, ss[:, 0:8], ATT, LN_EPS)
            dve.wait_ge(lnrow_in, 32)
            for t in range(NT):
                x = TS(vs_b[:, t, :], vs_b[:, t, :], mean[:, t:t + 1], rstd[:, t:t + 1], ALU.add, ALU.mult)
            x.then_inc(lnorm, 1)
            dve.wait_ge(lnorm, 1)
            row3 = [LN_ROWS[:, a * ATT:(a + 1) * ATT].rearrange("p (a c) -> p a c", a=1).to_broadcast([P, NT, ATT]) for a in range(2)]
            TT(vs_b, vs_b, row3[0], ALU.mult).then_inc(lnorm, 1)
            dve.wait_ge(lnorm, 2)
            TT(vs_b, vs_b, row3[1], ALU.add).then_inc(ln2_done, 1)

            def in2_copy(b, dst, scale):
                for t in range(NT):
                    if t < NT - 1:
                        dve.wait_ge(in2_full, 7 * b + t + 1)
                    else:
                        dve.wait_ge(w_used, U_IN2 + 4 * b + 4)
                    if scale is None:
                        dve.tensor_copy(dst[:, t, :], psum[:, t, :]).then_inc(in2_free, 1)
                    else:
                        TS(dst[:, t, :], psum[:, t, :], scale, None, ALU.mult).then_inc(in2_free, 1)

            in2_copy(2, v_b, None)
            in2_copy(3, q_b, DH ** -0.5)
            in2_copy(4, k_b, None)

            dve.wait_ge(trig_done, 2)
            dve.wait_ge(in2_free, 40)
            sin4, cos4 = [x.rearrange("p (t a f) -> p t a f", t=NT, a=1).to_broadcast([P, NT, AH, ROT]) for x in (ang, ang2)]
            tmp = [x.rearrange("p (t h f) -> p t h f", t=NT, h=AH) for x in ROPE_T]
            for i, x in enumerate((q_b, k_b)):
                x1, x2 = [x.rearrange("p t (h d) -> p t h d", d=DH)[:, :, :, a * ROT:(a + 1) * ROT] for a in range(2)]
                rstep(TT(tmp[0], x1, cos4, ALU.mult))
                rstep(TT(tmp[1], x2, sin4, ALU.mult))
                rstep(TT(tmp[0], tmp[0], tmp[1], ALU.subtract))
                rstep(TT(tmp[1], x2, cos4, ALU.mult))
                rstep(TT(tmp[2], x1, sin4, ALU.mult))
                rstep(dve.tensor_copy(x1, tmp[0]))
                TT(x2, tmp[1], tmp[2], ALU.add).then_inc(rope_done, 1)
                dve.wait_ge(rope_done, i + 1)

            for g in range(SGU_G):
                dve.wait_ge(sgu_full, g + 1)
                ug = u_b[:, :, g * DH:(g + 1) * DH]
                STT(ug, psum[:, 2 + g % 2, :].rearrange("p (t c) -> p t c", c=DH), col("sgu_b_spatial_2", g), ug,
                    ALU.add, ALU.mult).then_inc(sgu_done, 1)
            take_lo(2)

            dve.wait_ge(bias_in, 16)

            def attended(i):
                dve.wait_ge(pv_full, AH * (i + 1))
                dve.reciprocal(r_den, den_[:, AH * i:AH * (i + 1)]).then_inc(den_done, 1)
                dve.wait_ge(den_done, i + 1)
                TT(att_o[:, i, :].rearrange("p (h d) -> p h d", d=DH), psum[:, 6 + i % 2, :].rearrange("p (h d) -> p h d", d=DH),
                   r_den.rearrange("p (h a) -> p h a", a=1).to_broadcast([P, AH, DH]), ALU.mult).then_inc(ao_done, 1)

            for n in range(AH * NT):
                i = n // AH
                w = (i + 1) * P
                dve.wait_ge(s_full, n + 1)
                if n >= 4:
                    dve.wait_ge(pt_full, n - 3)
                TT(probs[n % 4][:, 0:w], two_banks(n % 2)[:, 0:w], BIAS[:, PAGE - w:PAGE], ALU.add).then_inc(s_moved, 1)
                dve.wait_ge(s_moved, n + 1)
                dve.reduce_max(neg_max[:, n % 8:n % 8 + 1], probs[n % 4][:, 0:w], AX.X, negate=True).then_inc(max_done, 1)
                if n % AH == 4 and i:
                    attended(i - 1)
            attended(NT - 1)

            for a, x in enumerate((att_o, u_b)):
                dve.wait_ge(ss_done, 24 + 8 * a)
                stats(4 + a, ss[:, 8 * a:8 * a + 8], ATT, EPS)
                for t in range(NT):
                    TS(x[:, t, :], x[:, t, :], rstd[:, t:t + 1], None, ALU.mult).then_inc(mixn_done, 1)
                dve.wait_ge(mixn_done, NT * (a + 1))
            take_lo(3, lambda k: cols[:, VROW["attn_out_norm_2"] + k:VROW["attn_out_norm_2"] + k + 1])
            y_copy(1, 0, U_OUT2 + 4, lambda t: Y[:, t, 0:HALF])
            y_copy(1, 1, U_OUT2 + 8, lambda t: Y[:, t, HALF:D])
            dve.wait_ge(row_in, 48)
            post(1, 6, lambda t: [(Y[:, t, :], POST_ROW)])
            next_norm(7, 40)
            take_lo(4, lambda k: col("pre_ffn_norm_2", k))

            with dve.Fori(0, FT // 2) as i:
                for j in range(2):
                    dve.wait_ge(gate_silu, 2 * i + (j + 1))
                    dve.wait_ge(w_used, 4 * i + (U_GU + 2 * j + 2))
                    a = arena[:, bass.ds((2 * i + j) * PAGE, PAGE)]
                    TT(a, a, two_banks(2 * j + 1), ALU.mult).then_inc(act_done, 1)
            ring_lo(32, U_DOWN, actp)
            y_copy(2, 0, U_DOWN + 11, lambda t: y_half0[:, t, :])
            ring_lo(32 + FT, U_DOWN, actp, 11)
            y_copy(2, 1, U_DOWN + 22, lambda t: y_half1[:, t, :])
            dve.wait_ge(row_in, 64)
            post(2, 8, lambda t: [(y_half0[:, t, :], ROW_F[:, 0:HALF]), (y_half1[:, t, :], ROW_F[:, HALF:D])])


def constants():
    i = np.arange(P)
    mask = np.zeros((P, NL, 64), np.int32)
    for j, w in enumerate(SPANS):
        x = np.arange(64)
        block = x // w
        mask[:, j, :] = (i[:, None] // (2 * w) == block[None, :]) & (i[:, None] % (2 * w) < w)
    d = (S - P) + i[:, None] - np.arange(S)[None, :]
    n = ((d >= 0) & (d <= 128)).astype(int) + ((d >= 0) & (d <= 512) & (d % 4 == 0)) + ((d >= 0) & (d % 16 == 0))
    bias = np.where(n > 0, np.log(np.maximum(n, 1)), NEG).astype(np.float32)
    freq = np.float32(500000.0) ** (-np.arange(0, 2 * ROT, 2, dtype=np.float32) / np.float32(2 * ROT))
    count = np.array([[1.0 / min(t + 1, w) for t in range(16)] for w in POOL_WINDOWS], np.float32).reshape(1, 64)
    return {
        "k_ident": np.eye(P, dtype=np.float32),
        "k_level_mask": mask,
        "k_tril": np.tril(np.ones((P, P), np.float32)),
        "k_bias": bias,
        "k_inv_freq": np.repeat(freq.astype(np.float32).reshape(1, ROT), P, 0),
        "k_inv_count": np.repeat(count, P, 0),
    }


INPUTS = ["x", "c", "norm_pre_w", "ada_w", "ada_b", "w_in", "pool_w", "pool_scale", "hgrn_lower_bounds",
          "hgrn_norm_w", "w_out", "norm_post_w", "positions_2", "pre_mix_norm_2", "w_in_2", "sgu_ln_gain_2",
          "sgu_ln_bias_2", "sgu_w_spatial_2", "sgu_b_spatial_2", "attn_out_norm_2", "sgu_out_norm_2", "w_out_2",
          "post_mix_norm_2", "pre_ffn_norm_2", "w_gate_2", "w_up_2", "w_down_2", "post_ffn_norm_2"]


def kernel(**inputs):
    import concourse.bacc as bacc
    from concourse.bass_utils import run_bass_kernel_spmd

    nc = bacc.Bacc("TRN2", target_bir_lowering=False, num_devices=1)
    arrays = {name: np.ascontiguousarray(inputs[name]) for name in INPUTS}
    arrays.update(constants())
    ap = {}
    for name, a in arrays.items():
        ap[name] = nc.dram_tensor(name, a.shape, mybir.dt.from_np(a.dtype), kind="ExternalInput").ap()
    out = nc.dram_tensor("out", (1, S, D), F32, kind="ExternalOutput").ap()
    ap["out"] = out.rearrange("b (t p) d -> (b t) p d", p=P)
    program(nc, ap)
    r = run_bass_kernel_spmd(nc, [arrays], core_ids=[0])
    return r.results[0]["out"]
```

```python
import math
from contextlib import ExitStack

import numpy as np

import concourse.bass as bass
import concourse.mybir as mybir

F32 = mybir.dt.float32
F32R = mybir.dt.float32r
I32 = mybir.dt.int32
ACT = mybir.ActivationFunctionType
ALU = mybir.AluOpType
AX = mybir.AxisListType

P = 128
D = 1024
S = 1024
KT = D // P
NT = S // P
HALF = 512
PAGE = 1024

HEADS = 8
SPANS = [64, 32, 16, 8, 4, 2, 1]
NL = len(SPANS)
POOL_WINDOWS = (2, 4, 8, 16)
GROUPS = 4
F_MIN = 1e-19

DH = 64
AH = 8
ATT = 512
ROT = 8
SGU_G = 8
D_FF = 2816
FT = D_FF // P
EPS = 1e-6
LN_EPS = 1e-5
TWO_PI = 2 * math.pi
TWO_PI_HI = 6.28125
TWO_PI_LO = TWO_PI - TWO_PI_HI
PI_IN = 3.1415925
ROPE_STEPS = 17
NEG = -1e30

VEC = [("c", 8), ("ada_b", 24), ("norm_pre_w", 8), ("pool_scale", 8), ("hgrn_lower_bounds", 8),
       ("hgrn_norm_w", 1), ("pre_mix_norm_2", 8), ("attn_out_norm_2", 4), ("sgu_out_norm_2", 4),
       ("pre_ffn_norm_2", 8), ("sgu_b_spatial_2", 8)]
VROW, VROWS = {}, 0
for _name, _n in VEC:
    VROW[_name] = VROWS
    VROWS += _n

U_HGRN = 0
U_POOL = U_HGRN + 4 * HEADS
U_OUT = U_POOL + 4 * GROUPS
U_IN2 = U_OUT + 16
U_OUT2 = U_IN2 + 20
U_GU = U_OUT2 + 8
U_DOWN = U_GU + 2 * FT
UNITS = U_DOWN + FT
RAW = 4

TASKS = 13
SPAN_TASK = [4, 5, 6, 8, 9, 10, 11]
SPAN_SLOT = [3, 2, 3, 3, 2, 3, 2]
TASK_U, TASK_O, TASK_MS = 7, 12, 13
C_U, C_G, C_Q, C_F, C_V, C_GH = 0, 8, 16, 24, 32, 40
IN2_BLOCKS = [0, 4, 1, 2, 3]
B_IQ, B_IK, B_IV, B_IU, B_IVS = [IN2_BLOCKS.index(_b) for _b in range(5)]
N_SGU, N_SGU_SQ, N_SGU_NORM = 8, 17, 28
MIX2_ORDER = [4, 5, 6, 7, 0, 1, 2, 3]


def program(nc, ap):
    ctx = ExitStack()
    with ctx:
        def sb(name, shape, dt=F32):
            return ctx.enter_context(nc.sbuf_tensor(name, shape, dt))

        def sem(name):
            return ctx.enter_context(nc.semaphore(name))

        h_hi = sb("h_hi", [P, KT, S], F32R)
        h_lo = sb("h_lo", [P, KT, S], F32R)
        w_raw = sb("w_raw", [P, RAW, 1024])
        w_hi = sb("w_hi", [P, 2, 1024], F32R)
        w_lo = sb("w_lo", [P, 2, 1024], F32R)
        arena = sb("arena", [P, 27 * PAGE])
        ident = sb("ident", [P, P])
        ones = sb("ones", [P, P])
        cols = sb("cols", [P, VROWS])
        lvl_mask = sb("lvl_mask", [P, NL, 64], I32)
        st = sb("st", [P, 160])
        psum = ctx.enter_context(nc.psum_tensor("psum", [P, 8, HALF], F32))

        def page(i, n=1):
            return arena[:, i * PAGE:(i + n) * PAGE]

        def tiles(i, n=NT):
            return page(i, n).rearrange("p (t c) -> p t c", c=PAGE)

        def two_banks(slot):
            return psum[:, 2 * slot:2 * slot + 2, :].rearrange("p b n -> p (b n)")

        def col(name, i=0, n=1):
            return cols[:, VROW[name] + i:VROW[name] + i + n]

        silu_c = st[:, 0:8]
        mod = st[:, 8:24]
        mul_a = st[:, 24:32]
        lb = st[:, 32:40]
        one_lb = st[:, 40:48]
        lb_tmp = st[:, 48:56]
        ss = st[:, 56:72]
        ms = st[:, 72:80]
        rstd = st[:, 80:88]
        end_decay = st[:, 88:96]
        mean = st[:, 96:104]
        neg_max = st[:, 104:112]
        r_den = st[:, 112:120]
        pos = st[:, 120:128]
        sums = st[:, 128:136]
        den_ = page(26)[:, 0:AH * NT]

        X0 = 0
        ADA = 8
        ACC = 17
        JUNK0 = 20
        ADAB = 21
        GATE_ROW = 26
        NPOST = 25
        MIX = 0
        B_SIG, B_K, B_B, B_Q, B_QE, B_VT, B_V, B_KDT, B_KD, B_ATT = range(16, 26)
        B_SQ = 7
        B_S, B_D, B_KL = 2, (3, 4, 7), 5
        U_PAGES = [(16, 21), (17, 18)]
        S_A, S_B = 22, 24
        PW = [23, 19]
        RC = 20
        IDM = ident

        gate_row = page(GATE_ROW)
        mixp = [page(MIX + i) for i in range(16)]
        Y = tiles(16)
        XR = tiles(0)
        vs_b, u_b, v_b, q_b, k_b = [page(4 * i, 4).rearrange("p (t c) -> p t c", c=ATT) for i in range(5)]
        SPAT, SPAT_T = 20, 21
        ROPE = page(22)
        ROPE_T = [page(23)[:, 0:512], page(23)[:, 512:1024], page(26)[:, 0:512]]
        JUNK3 = page(26)[:, 512:1024]
        LN_ROWS = page(24)
        BIAS = page(25)
        probs = [page(16 + i) for i in range(4)]
        probs_t = [page(22 + i) for i in range(2)]
        att_o = q_b
        POST_ROW = page(24)
        ROW_F = page(26)
        actp = [page(i) for i in range(FT)]
        y_half0 = page(22, 4).rearrange("p (t c) -> p t c", c=HALF)
        y_half1 = page(8, 4).rearrange("p (t c) -> p t c", c=HALF)

        x_mid = [nc.dram_tensor(f"x_mid{i}", [NT, P, D], F32, kind="Internal").ap() for i in range(2)]

        raw_in = [sem(f"raw_in{i}") for i in range(RAW)]
        w_rounded, w_ready, w_used = sem("w_rounded"), sem("w_ready"), sem("w_used")
        const_in, vec_in, pos_in, row_in = sem("const_in"), sem("vec_in"), sem("pos_in"), sem("row_in")
        x_in = [sem(f"x_in{t}") for t in range(NT)]
        ada_in = [sem(f"ada_in{i}") for i in range(3)]
        ones_set, vec_t, cols_done = sem("ones_set"), sem("vec_t"), sem("cols_done")
        silu_done, ada_acc, mod_mm, mod_done = sem("silu_done"), sem("ada_acc"), sem("mod_mm"), sem("mod_done")
        lb_step, lb_exp = sem("lb_step"), sem("lb_exp")
        ss_done, ms_done, sqrt_done, rstd_done = sem("ss_done"), sem("ms_done"), sem("sqrt_done"), sem("rstd_done")
        xn_done, tr_full, hi_done, lo_tmp, lo_done = (sem("xn_done"), sem("tr_full"), sem("hi_done"),
                                                      sem("lo_tmp"), sem("lo_done"))
        sig_done, gsig_done, g_done, vt_done, q_done = (sem("sig_done"), sem("gsig_done"), sem("g_done"),
                                                        sem("vt_done"), sem("q_done"))
        f_done, k_done, fc_done, lf_done, b_done = (sem("f_done"), sem("k_done"), sem("fc_done"),
                                                    sem("lf_done"), sem("b_done"))
        eb_done, end_done, dk_done, ek_done, kdec_done, qe_done = (
            sem("eb_done"), sem("end_done"), sem("dk_done"), sem("ek_done"), sem("kdec_done"), sem("qe_done"))
        d_done, e_done, kl_done, lvl_done, task_full = (sem("d_done"), sem("e_done"), sem("kl_done"),
                                                        sem("lvl_done"), sem("task_full"))
        v_done, kd_done, diag_done, pick_done, s_done = (sem("v_done"), sem("kd_done"), sem("diag_done"),
                                                         sem("pick_done"), sem("s_done"))
        sq_done, ln_done, rs_done, o1_done, o_done = (sem("sq_done"), sem("ln_done"), sem("rs_done"),
                                                      sem("o1_done"), sem("o_done"))
        pu_done, pgs_done, pg_done, win_step, pd_done, pm_full, pmix_done, pw_in, rc_in = (
            sem("pu_done"), sem("pgs_done"), sem("pg_done"), sem("win_step"), sem("pd_done"), sem("pm_full"),
            sem("pmix_done"), sem("pw_in"), sem("rc_in"))
        sp_hi, sp_lo, yb_full, ycp_done, ysq_done = (sem("sp_hi"), sem("sp_lo"), sem("yb_full"),
                                                     sem("ycp_done"), sem("ysq_done"))
        sum_done, res_step, res_done, spilled = sem("sum_done"), sem("res_step"), sem("res_done"), [sem("spilled0"), sem("spilled1")]
        in2_free, in2_full, lnrow_in, spat_in, bias_in, freq_in = (
            sem("in2_free"), sem("in2_full"), sem("lnrow_in"), sem("spat_in"), sem("bias_in"), sem("freq_in"))
        gelu_done, mean_done, var_done, lnorm = sem("gelu_done"), sem("mean_done"), sem("var_done"), sem("lnorm")
        tril_done, spat_full, spat_tr, sgu_full, sgu_done = (sem("tril_done"), sem("spat_full"), sem("spat_tr"),
                                                             sem("sgu_full"), sem("sgu_done"))
        rope_step, trig_done, rope_done = sem("rope_step"), sem("trig_done"), sem("rope_done")
        s_full, s_moved, max_done, p_done, pt_full, pt_done, pv_full, den_done, ao_done = (
            sem("s_full"), sem("s_moved"), sem("max_done"), sem("p_done"), sem("pt_full"), sem("pt_done"),
            sem("pv_full"), sem("den_done"), sem("ao_done"))
        gate_silu, act_done, out_sent, mixn_done = sem("gate_silu"), sem("act_done"), sem("out_sent"), sem("mixn_done")
        ln2_done = sem("ln2_done")

        block = ctx.enter_context(nc.Block())

        fm = lambda w: w[0].rearrange("(k p) (f c) -> f p k c", p=P, c=P)
        tm = lambda w: w[0].rearrange("(j k p) (n c) -> n j p k c", k=2, p=P, c=HALF)
        w_in_fm, gate_fm, up_fm = fm(ap["w_in"]), fm(ap["w_gate_2"]), fm(ap["w_up_2"])
        w_out_tm, w_in2_tm, w_out2_tm, down_tm = tm(ap["w_out"]), tm(ap["w_in_2"]), tm(ap["w_out_2"]), tm(ap["w_down_2"])

        @block.sync
        def _(sp):
            for name, n in VEC:
                r = VROW[name]
                src = ap[name]
                src = src[0] if len(src.shape) > 2 else src
                if name == "sgu_b_spatial_2":
                    flat = src
                else:
                    flat = src.rearrange("a (r c) -> (a r) c", c=P)
                sp.dma_start(arena[r:r + n, JUNK0 * PAGE:JUNK0 * PAGE + P], flat).then_inc(vec_in, 16)
            sp.dma_start(pos.bitcast(I32), ap["positions_2"][0].rearrange("(t p) -> p t", p=P), allow_slow_non_contiguous=True).then_inc(pos_in, 16)
            sp.dma_start(ident[:], ap["k_ident"]).then_inc(const_in, 16)
            sp.dma_start(lvl_mask[:], ap["k_level_mask"]).then_inc(const_in, 16)
            ada_v = ap["ada_w"][0].rearrange("(k p) n -> k p n", p=P)
            for k in range(KT):
                if k >= 3:
                    sp.wait_ge(ada_acc, k - 2)
                sp.dma_start(page(ADA + 3 * (k % 3), 3), ada_v[k]).then_inc(ada_in[k % 3], 16)
                if k == 2:
                    sp.dma_start(arena[0:1, ADAB * PAGE:(ADAB + 1) * PAGE], ap["ada_b"][0:1, 2 * D:3 * D]).then_inc(row_in, 16)
                    sp.dma_start(page(NPOST), ap["norm_post_w"][0].partition_broadcast(P)).then_inc(row_in, 16)

            def slot_fm(s):
                return w_raw[:, s, :].rearrange("p (k c) -> p k c", c=P)

            def slot_tm(s):
                return w_raw[:, s, :].rearrange("p (k c) -> p k c", c=HALF)

            def load(s, dst, src):
                sp.dma_start(dst, src).then_inc(raw_in[s], 16)

            for s, c in enumerate((C_F, C_GH, C_V, C_Q)):
                load(s, slot_fm(s), w_in_fm[c])
            with sp.Fori(1, HEADS) as h:
                for s, c in enumerate((C_F, C_GH, C_V, C_Q)):
                    sp.wait_ge(w_ready, 4 * h + s - 3)
                    load(s, slot_fm(s), w_in_fm[h + c])
            with sp.Fori(0, GROUPS) as g:
                for s in range(4):
                    sp.wait_ge(w_ready, 4 * g + (U_POOL + s - 3))
                    load(s, slot_fm(s), w_in_fm[2 * g + (s // 2 + (C_U, C_G)[s % 2])])
            for n in range(2):
                with sp.Fori(0, 2) as j:
                    for s in range(4):
                        sp.wait_ge(w_ready, 4 * j + (U_OUT + 8 * n + s - 3))
                        load(s, slot_tm(s), w_out_tm[n][4 * j + s])
            for t in range(NT):
                sp.wait_ge(sp_lo, 16 + t + 1)
                sp.dma_start(XR[:, t, :], ap["x"][0, t * P:(t + 1) * P, :]).then_inc(x_in[t], 16)
            for b, blk in enumerate(IN2_BLOCKS):
                for s in range(4):
                    sp.wait_ge(w_ready, U_IN2 + 4 * b + s - 3)
                    load(s, slot_tm(s), w_in2_tm[blk][s])
            for n in range(2):
                for s in range(4):
                    sp.wait_ge(w_ready, U_OUT2 + 4 * n + s - 3)
                    load(s, slot_tm(s), w_out2_tm[n][s])
            for t in range(NT):
                sp.wait_ge(tr_full, 32)
                sp.wait_ge(spilled[0], 16 * NT)
                sp.dma_start(XR[:, t, :], x_mid[0][t]).then_inc(x_in[t], 16)
            with sp.Fori(0, FT // 2) as i:
                for s in range(4):
                    sp.wait_ge(w_ready, 4 * i + (U_GU + s - 3))
                    load(s, slot_fm(s), (gate_fm, up_fm)[s % 2][2 * i + s // 2])
            for j in range(FT):
                s = j % RAW
                sp.wait_ge(w_ready, U_DOWN + j - 3)
                load(s, slot_tm(s), down_tm[j // 11][j % 11])
            for t in range(NT):
                sp.wait_ge(sp_lo, 32 + FT + t + 1)
                sp.wait_ge(spilled[1], 16 * NT)
                sp.dma_start(XR[:, t, :], x_mid[1][t]).then_inc(x_in[t], 16)
            for t in range(NT):
                sp.wait_ge(res_done, 2 * NT + t + 1)
                sp.dma_start(ap["out"][t], XR[:, t, :]).then_inc(out_sent, 16)
            sp.wait_ge(out_sent, 16 * NT)

        @block.gpsimd
        def _(pool):
            unit_scale = ones[:].rearrange("p (a n) -> p a n", a=1).to_broadcast([P, KT, P])

            def split(i, s, first):
                c = s % 2
                raw = w_raw[:, s, :]
                pool.wait_ge(raw_in[s], 16 * i + 16)
                if not (first and s < 2):
                    pool.wait_ge(w_used, 4 * i + s - 1)
                pool.tensor_tensor(w_hi[:, c, :].rearrange("p (a n) -> p a n", n=P), raw.rearrange("p (a n) -> p a n", n=P),
                                   unit_scale, ALU.mult).then_inc(w_rounded, 1)
                pool.wait_ge(w_rounded, 4 * i + s + 1)
                pool.tensor_tensor(w_lo[:, c, :], raw, w_hi[:, c, :].bitcast(F32), ALU.subtract).then_inc(w_ready, 1)

            pool.wait_ge(ones_set, 1)
            for s in range(4):
                split(0, s, True)
            with pool.Fori(1, UNITS // 4) as i:
                for s in range(4):
                    split(i, s, False)
            for s in range(UNITS % 4):
                split(UNITS // 4, s, False)

        @block.tensor
        def _(pe):
            def fm_half(c, out, half):
                o = out[:, half * HALF:(half + 1) * HALF]
                for k in range(KT):
                    wh = w_hi[:, c, k * P:(k + 1) * P]
                    wl = w_lo[:, c, k * P:(k + 1) * P]
                    xh = h_hi[:, k, half * HALF:(half + 1) * HALF]
                    xl = h_lo[:, k, half * HALF:(half + 1) * HALF]
                    pe.matmul(o, wh, xh, start=(k == 0), stop=False)
                    pe.matmul(o, wh, xl, start=False, stop=False)
                    mm = pe.matmul(o, wl, xh, start=False, stop=(k == KT - 1))
                return mm

            def fm_unit(c, out):
                fm_half(c, out, 0)
                return fm_half(c, out, 1)

            def tm_rows(c, kk, k, t, start, stop):
                xh = h_hi[:, k, t * P:(t + 1) * P]
                xl = h_lo[:, k, t * P:(t + 1) * P]
                wh = w_hi[:, c, kk * HALF:(kk + 1) * HALF]
                wl = w_lo[:, c, kk * HALF:(kk + 1) * HALF]
                pe.matmul(psum[:, t, :], xh, wh, start=start, stop=False)
                pe.matmul(psum[:, t, :], xh, wl, start=False, stop=False)
                return pe.matmul(psum[:, t, :], xl, wh, start=False, stop=stop)

            def transposes(n, src, order=range(KT), ready=None):
                for a, k in enumerate(order):
                    if ready is not None and ready[a]:
                        pe.wait_ge(*ready[a])
                    if a >= 2:
                        pe.wait_ge(hi_done, 8 * n + a - 1)
                        pe.wait_ge(lo_done, 8 * n + a - 1)
                    for t in range(NT):
                        o = two_banks(2 + a % 2)[:, t * P:(t + 1) * P]
                        mm = pe.transpose(o, src(t, k), ident[:])
                    mm.then_inc(tr_full, 1)

            pe.wait_ge(vec_in, 16 * len(VEC))
            pe.wait_ge(const_in, 32)
            pe.transpose(psum[:, 4, 0:VROWS], arena[0:VROWS, JUNK0 * PAGE:JUNK0 * PAGE + P], ident[0:VROWS, 0:VROWS]).then_inc(vec_t, 1)
            pe.wait_ge(ada_acc, KT)
            pe.wait_ge(ones_set, 1)
            acc = page(ACC, 3)
            for f in range(16):
                mm = pe.matmul(psum[:, 5, f:f + 1], acc[:, f * P:(f + 1) * P], ones[:, 0:1], start=True, stop=True)
            mm.then_inc(mod_mm, 1)
            pe.wait_ge(row_in, 32)
            for n in range(2):
                pe.matmul(psum[:, n, :], ones[:], acc[:, 2 * D + n * HALF:2 * D + (n + 1) * HALF], start=True, stop=False)
                mm = pe.matmul(psum[:, n, :], ones[0:1, :], arena[0:1, ADAB * PAGE + n * HALF:ADAB * PAGE + (n + 1) * HALF],
                               start=False, stop=True)
            mm.then_inc(mod_mm, 1)
            pe.wait_ge(xn_done, NT)
            pe.wait_ge(mod_done, 3)
            x0 = tiles(X0)
            transposes(0, lambda t, k: x0[:, t, k * P:(k + 1) * P])
            pe.wait_ge(hi_done, 8)
            pe.wait_ge(lo_done, 8)

            V, KD, ATTN, SST = page(B_V), page(B_KD), page(B_ATT), page(B_S)

            def z_unit(u, j, out):
                pe.wait_ge(w_ready, u + 1)
                fm_unit(j % 2, out).then_inc(w_used, 1)

            def blocks128(x, i):
                return x[:, i * P:(i + 1) * P]

            def task_t0(h):
                pe.wait_ge(vt_done, h + 1)
                if not (type(h) is int and h == 0):
                    pe.wait_ge(ln_done, h)
                for i in range(NT):
                    mm = pe.transpose(blocks128(two_banks(2), i), blocks128(page(B_VT), i), ident[:])
                mm.then_inc(task_full, 1)

            def task_t1(h):
                pe.wait_ge(kdec_done, h + 1)
                if not (type(h) is int and h == 0):
                    pe.wait_ge(o1_done, h)
                for i in range(NT):
                    mm = pe.transpose(blocks128(two_banks(3), i), blocks128(page(B_KDT), i), ident[:])
                mm.then_inc(task_full, 1)

            def task_diag(h):
                pe.wait_ge(v_done, h + 1)
                pe.wait_ge(q_done, h + 1)
                pe.wait_ge(k_done, h + 1)
                for i in range(NT):
                    mm = pe.matmul(blocks128(two_banks(2), i), blocks128(page(B_K), i), blocks128(page(B_Q), i), start=True, stop=True)
                mm.then_inc(task_full, 1)

            def task_span(h, j):
                taken = [(kd_done, h + 1), (diag_done, h + 1), (pick_done, NL * h + 1), (pick_done, NL * h + 3),
                         (s_done, (NT - 1) * h + NT - 1), (pick_done, NL * h + 4), (pick_done, NL * h + 5)][j]
                pe.wait_ge(*taken)
                pe.wait_ge(lvl_done, NL * h + j + 1)
                for i in range(NT):
                    mm = pe.matmul(blocks128(two_banks(SPAN_SLOT[j]), i), blocks128(page(B_KL + j % 2), i),
                                   blocks128(page(B_D[j % 3]), i), start=True, stop=True)
                mm.then_inc(task_full, 1)

            def task_u(h):
                pe.wait_ge(pick_done, NL * h + 2)
                pe.wait_ge(kd_done, h + 1)
                for i in range(NT - 1):
                    mm = pe.matmul(blocks128(two_banks(2), i), blocks128(KD, i), blocks128(V, i), start=True, stop=True)
                mm.then_inc(task_full, 1)

            def task_o(h):
                pe.wait_ge(pick_done, NL * h + NL)
                pe.wait_ge(s_done, (NT - 1) * h + NT - 1)
                pe.wait_ge(qe_done, h + 1)
                for i in range(NT):
                    mm = pe.matmul(blocks128(two_banks(3), i), blocks128(V, i), blocks128(ATTN, i), start=True, stop=(i == 0))
                    if i:
                        mm = pe.matmul(blocks128(two_banks(3), i), blocks128(SST, i - 1), blocks128(page(B_QE), i), start=False, stop=True)
                mm.then_inc(task_full, 1)

            def task_ms(h):
                pe.wait_ge(sq_done, h + 1)
                for half in range(2):
                    mm = pe.matmul(psum[:, 4 + half, :], ones[:], page(B_SQ)[:, half * HALF:(half + 1) * HALF], start=True, stop=True)
                mm.then_inc(task_full, 1)

            def head(h, z):
                first = type(h) is int and h == 0
                z(0, 0)
                if not first:
                    task_o(h - 1)
                z(0, 1)
                if not first:
                    task_ms(h - 1)
                z(1, 0)
                task_t0(h)
                task_t1(h)
                z(1, 1)
                task_diag(h)
                task_span(h, 0)
                z(2, 0)
                task_span(h, 1)
                task_span(h, 2)
                task_u(h)
                z(2, 1)
                task_span(h, 3)
                z(3, 0)
                task_span(h, 4)
                task_span(h, 5)
                z(3, 1)
                task_span(h, 6)

            for j in range(4):
                if j >= 2:
                    pe.wait_ge(sig_done, 1)
                    pe.wait_ge(g_done, 1)
                z_unit(j, j, two_banks(j % 2))

            def z_half(it, j, half):
                if half == 0:
                    pe.wait_ge((vt_done, q_done, sig_done, g_done)[j], it + j // 2)
                    pe.wait_ge(w_ready, 4 * it + (j + 1))
                mm = fm_half(j % 2, two_banks(j % 2), half)
                if half:
                    mm.then_inc(w_used, 1)

            head(0, lambda j, half: z_half(1, j, half))
            with pe.Fori(2, HEADS) as it:
                head(it - 1, lambda j, half: z_half(it, j, half))

            def pool_slot(g, j):
                if j % 2 == 0:
                    pe.wait_ge(pu_done, 2 * g + j // 2) if g or j else pe.wait_ge(vt_done, HEADS)
                else:
                    pe.wait_ge(pg_done, 2 * g + j // 2) if g or j > 1 else pe.wait_ge(q_done, HEADS)

            def pool_unit(g, j):
                pool_slot(g, j)
                z_unit(U_POOL + 4 * g + j, j, two_banks(j % 2))

            def pool_mix(g):
                pe.wait_ge(pd_done, 2 * g + 2)
                pe.wait_ge(pw_in, 32)
                pw = page(PW[g // 2])[:, (g % 2) * HALF:(g % 2 + 1) * HALF].rearrange("p (c d) -> p c d", c=2)
                for dt in range(2):
                    if g:
                        pe.wait_ge(pmix_done, 2 * g + dt - 1)
                    else:
                        pe.wait_ge(o1_done if dt == 0 else ln_done, HEADS)
                    for half in range(2):
                        for c in range(2):
                            mm = pe.matmul(psum[:, 4 + 2 * dt + half, :], pw[:, c, dt * P:(dt + 1) * P],
                                           page(U_PAGES[g % 2][c])[:, half * HALF:(half + 1) * HALF],
                                           start=(c == 0), stop=(c == 1))
                    mm.then_inc(pm_full, 1)

            def pool_half(j, half):
                if half == 0:
                    pool_slot(0, j)
                    pe.wait_ge(w_ready, U_POOL + j + 1)
                mm = fm_half(j % 2, two_banks(j % 2), half)
                if half:
                    mm.then_inc(w_used, 1)

            head(HEADS - 1, pool_half)
            for g in range(1, GROUPS):
                for j in range(4):
                    pool_unit(g, j)
                    if g == 1 and j < 2:
                        (task_o, task_ms)[j](HEADS - 1)
                pool_mix(g - 1)
            pool_mix(GROUPS - 1)

            def ring_unit(u, j, s0, start, last, e, n):
                pe.wait_ge(w_ready, u + 1)
                c, slot = u_par(u, j), j_par(j)
                for kk in range(2):
                    pe.wait_ge(sp_lo, s0 + kk + 1)
                    for t in range(NT):
                        if start and kk == 0 and n:
                            pe.wait_ge(ycp_done, 16 * e + 8 * (n - 1) + t + 1)
                        mm = tm_rows(c, kk, 2 * slot + kk, t, start and kk == 0, last and kk == 1)
                        if last and kk == 1 and t < NT - 1:
                            mm.then_inc(yb_full, 1)
                mm.then_inc(w_used, 1)

            par = [0, 0]

            def u_par(u, j):
                return par[0]

            def j_par(j):
                return par[1]

            def stage_ring(e, U0, s_base, per):
                for n in range(2):
                    j0 = per * n
                    edge = [0] + ([per - 1] if per % 2 == 0 else [per - 2, per - 1])
                    mid = per - len(edge)
                    par[:] = [(U0 + j0) % 2, j0 % 2]
                    ring_unit(U0 + j0, j0, s_base + 2 * j0, True, False, e, n)
                    with pe.Fori(0, mid // 2) as i:
                        for a in range(2):
                            j = j0 + 1 + a
                            par[:] = [(U0 + j) % 2, j % 2]
                            ring_unit(2 * i + (U0 + j), None, 4 * i + (s_base + 2 * j), False, False, e, n)
                    for q in edge[1:]:
                        j = j0 + q
                        par[:] = [(U0 + j) % 2, j % 2]
                        ring_unit(U0 + j, j, s_base + 2 * j, False, q == per - 1, e, n)

            stage_ring(0, U_OUT, 0, 8)

            pe.wait_ge(xn_done, 2 * NT)
            transposes(1, lambda t, k: Y[:, t, k * P:(k + 1) * P])
            pe.wait_ge(hi_done, 16)
            pe.wait_ge(lo_done, 16)

            def tm_block(u, first, on_last, free):
                for j in range(4):
                    pe.wait_ge(w_ready, u + (j + 1))
                    for kk in range(2):
                        k = 2 * j + kk
                        for t in range(NT):
                            if k == 0 and free is not None:
                                free(t)
                            mm = tm_rows(j % 2, kk, k, t, k == 0, k == KT - 1)
                            if k == KT - 1 and t < NT - 1:
                                mm.then_inc(on_last, 1)
                    mm.then_inc(w_used, 1)

            tm_block(U_IN2, True, in2_full, None)
            with pe.Fori(1, 5) as b:
                tm_block(4 * b + U_IN2, False, in2_full, lambda t: pe.wait_ge(in2_free, 8 * b + (t - 7)))

            pe.wait_ge(in2_free, 40)
            pe.wait_ge(tril_done, 1)
            for g in range(SGU_G):
                mm = pe.transpose(blocks128(two_banks(0), g), blocks128(page(SPAT), g), ident[:])
            mm.then_inc(spat_full, 1)

            pe.wait_ge(rope_done, 2)
            transposes(2, lambda t, k: (q_b, k_b)[k // 4][:, t, (k % 4) * P:(k % 4 + 1) * P])
            pe.wait_ge(hi_done, 24)
            pe.wait_ge(lo_done, 24)
            pe.wait_ge(spat_tr, 1)

            def qk(n):
                i, h = n // AH, n % AH
                if n >= 2:
                    pe.wait_ge(s_moved, n - 1)
                po = DH * (h % 2)
                for c0 in range(0, (i + 1) * P, HALF):
                    c1 = min(c0 + HALF, (i + 1) * P)
                    o = two_banks(n % 2)[:, c0:c1]
                    qh, ql = [x[po:po + DH, h // 2, i * P:(i + 1) * P] for x in (h_hi, h_lo)]
                    kh, kl = [x[po:po + DH, 4 + h // 2, c0:c1] for x in (h_hi, h_lo)]
                    pe.matmul(o, qh, kh, start=True, stop=False)
                    pe.matmul(o, qh, kl, start=False, stop=False)
                    mm = pe.matmul(o, ql, kh, start=False, stop=True)
                mm.then_inc(s_full, 1)

            def p_t(n):
                pe.wait_ge(p_done, n + 1)
                if n:
                    pe.wait_ge(pt_done, n)
                for j in range(n // AH + 1):
                    mm = pe.transpose(blocks128(two_banks(2), j), blocks128(probs[n % 4], j), ident[:])
                mm.then_inc(pt_full, 1)

            def pv(n):
                i, h = n // AH, n % AH
                pe.wait_ge(pt_done, n + 1)
                if n >= AH:
                    pe.wait_ge(ao_done, (n - AH) // 4 + 1)
                for j in range(i + 1):
                    mm = pe.matmul(two_banks(3)[:, h * P:(h + 1) * P], blocks128(probs_t[n % 2], j),
                                   v_b[:, j, (h // 2) * P:(h // 2 + 1) * P], start=(j == 0), stop=(j == i))
                mm.then_inc(pv_full, 1)

            def sgu(g):
                if g == 0:
                    pe.wait_ge(ln2_done, 1)
                if g >= 2:
                    pe.wait_ge(sgu_done, g - 1)
                pe.matmul(psum[:, 1 + 2 * (g % 2), :], blocks128(page(SPAT_T), g), vs_b[:, :, g * DH:(g + 1) * DH],
                          start=True, stop=True).then_inc(sgu_full, 1)

            N = AH * NT
            for n in range(N + 3):
                if n < N:
                    qk(n)
                if 0 <= n - N_SGU < SGU_G:
                    sgu(n - N_SGU)
                if 0 <= n - 2 < N:
                    p_t(n - 2)
                if 0 <= n - 3 < N:
                    pv(n - 3)

            pe.wait_ge(mixn_done, NT)
            transposes(3, lambda t, k: (att_o, u_b)[k // 4][:, t, (k % 4) * P:(k % 4 + 1) * P], MIX2_ORDER,
                       [None, (ao_done, 2 * NT), None, None, (mixn_done, 2 * NT)] + [None] * 3)
            pe.wait_ge(hi_done, 32)
            pe.wait_ge(lo_done, 32)
            tm_block(U_OUT2, True, yb_full, None)

            def y_free(t):
                pe.wait_ge(ycp_done, 16 + t + 1)
            tm_block(U_OUT2 + 4, False, yb_full, y_free)

            pe.wait_ge(xn_done, 3 * NT)
            transposes(4, lambda t, k: Y[:, t, k * P:(k + 1) * P])
            pe.wait_ge(hi_done, 40)
            pe.wait_ge(lo_done, 40)

            def gu_unit(i, j, first):
                if not first:
                    pe.wait_ge(gate_silu if j % 2 == 0 else act_done, 2 * i + (j // 2 - 1))
                pe.wait_ge(w_ready, 4 * i + (U_GU + j + 1))
                fm_unit(j % 2, two_banks(j)).then_inc(w_used, 1)

            for j in range(4):
                gu_unit(0, j, True)
            with pe.Fori(1, FT // 2) as i:
                for j in range(4):
                    gu_unit(i, j, False)
            pe.wait_ge(act_done, FT)
            stage_ring(2, U_DOWN, 32, 11)

        @block.scalar
        def _(act):
            A = act.activation

            def copy(out, in_):
                return A(out, in_, ACT.Copy)

            for t in range(NT):
                act.dma_start(tiles(X0)[:, t, :], ap["x"][0, t * P:(t + 1) * P, :]).then_inc(x_in[t], 16)
            act.wait_ge(cols_done, 1)
            A(silu_c, col("c", 0, 8), ACT.Silu).then_inc(silu_done, 1)
            act.wait_ge(lb_step, 1)
            A(lb_tmp, lb_tmp, ACT.Exp).then_inc(lb_exp, 1)

            def squares(n, src, junk, count):
                for t in range(NT):
                    if n + t:
                        act.wait_ge(ss_done, n + t)
                    A(junk, src(t), ACT.Square, accum_out=ss[:, t:t + 1]).then_inc(ss_done, 1)

            def root(m):
                act.wait_ge(ms_done, m + 1)
                A(ms, ms, ACT.Sqrt).then_inc(sqrt_done, 1)

            def take_hi(n, mul=None, add=None, order=range(KT)):
                for a, k in enumerate(order):
                    act.wait_ge(tr_full, 8 * n + a + 1)
                    src = two_banks(2 + a % 2)
                    if mul is None:
                        copy(h_hi[:, k, :], src).then_inc(hi_done, 1)
                    else:
                        A(h_hi[:, k, :], src, ACT.Identity, scale=mul(k), bias=add(k) if add else 0.0).then_inc(hi_done, 1)

            act.wait_ge(vec_t, 1)
            for t in range(NT):
                act.wait_ge(x_in[t], 16)
                if t:
                    act.wait_ge(ss_done, t)
                A(page(JUNK0), tiles(X0)[:, t, :], ACT.Square, accum_out=ss[:, t:t + 1]).then_inc(ss_done, 1)
            root(0)
            act.wait_ge(mod_done, 2)
            take_hi(0, lambda k: mul_a[:, k:k + 1], lambda k: mod[:, k:k + 1])

            bB, qe, vt = page(B_B), page(B_QE), page(B_VT)

            def span_exp(h, j):
                act.wait_ge(d_done, NL * h + j + 1)
                A(page(B_D[j % 3]), page(B_D[j % 3]), ACT.Exp).then_inc(e_done, 1)

            def front(it, z0):
                act.wait_ge(w_used, z0 + 1)
                if not (type(it) is int and it == 0):
                    act.wait_ge(fc_done, it)
                A(page(B_SIG), two_banks(0), ACT.Sigmoid).then_inc(sig_done, 1)

            def gate_sig(it):
                act.wait_ge(w_used, 4 * it + 2)
                A(mix_slot(it), two_banks(1), ACT.Sigmoid).then_inc(gsig_done, 1)

            def log_f(it):
                act.wait_ge(fc_done, it + 1)
                A(bB, bB, ACT.Ln).then_inc(lf_done, 1)

            def decays(it):
                act.wait_ge(b_done, it + 1)
                A(end_decay, bB.rearrange("p (c t) -> p c t", t=P)[:, :, P - 1], ACT.Exp).then_inc(end_done, 1)
                act.wait_ge(dk_done, it + 1)
                A(page(B_KDT), page(B_KDT), ACT.Exp).then_inc(ek_done, 1)

            def take_q(it, z0):
                act.wait_ge(w_used, z0 + 4)
                if not (type(it) is int and it == 0):
                    act.wait_ge(lvl_done, NL * it)
                copy(page(B_Q), two_banks(1)).then_inc(q_done, 1)

            def take_v(it, z0):
                act.wait_ge(w_used, z0 + 3)
                copy(vt, two_banks(0)).then_inc(vt_done, 1)

            def begin(h):
                span_exp(h, 0)
                span_exp(h, 1)
                if not (type(h) is int and h == 0):
                    o_squares(h - 1)
                act.wait_ge(b_done, h + 1)
                A(qe, bB, ACT.Exp).then_inc(eb_done, 1)

            def take_vk(h):
                act.wait_ge(task_full, TASKS * h + 1)
                copy(page(B_V), two_banks(2)).then_inc(v_done, 1)
                act.wait_ge(task_full, TASKS * h + 2)
                copy(page(B_KD), two_banks(3)).then_inc(kd_done, 1)

            def o_squares(h):
                act.wait_ge(task_full, TASKS * h + TASK_O)
                A(page(B_SQ), two_banks(3), ACT.Square).then_inc(sq_done, 1)

            def o_norm(h):
                act.wait_ge(task_full, TASKS * h + TASK_MS)
                A(page(B_SQ), two_banks(2), ACT.Ln, scale=1.0 / P, bias=EPS).then_inc(ln_done, 1)
                act.wait_ge(ln_done, h + 1)
                A(page(B_SQ), page(B_SQ), ACT.Exp, scale=-0.5).then_inc(rs_done, 1)

            def mix_slot(it):
                return arena[:, bass.ds((MIX + 8 + it) * PAGE, PAGE)]

            front(0, 0)
            gate_sig(0)
            take_v(0, 0)
            log_f(0)
            take_q(0, 0)
            decays(0)

            def step(it):
                h = it - 1
                begin(h)
                front(it, 4 * it)
                if not (type(it) is int and it == 1):
                    o_norm(h - 1)
                take_vk(h)
                span_exp(h, 2)
                gate_sig(it)
                for j in (3, 4, 5):
                    span_exp(h, j)
                take_v(it, 4 * it)
                span_exp(h, 6)
                log_f(it)
                take_q(it, 4 * it)
                decays(it)

            step(1)
            with act.Fori(2, HEADS) as it:
                step(it)

            def pool_in(g, j):
                act.wait_ge(w_used, U_POOL + 4 * g + j + 1)
                if j % 2 == 0:
                    if g >= 2:
                        act.wait_ge(pm_full, 2 * (g - 2) + 2)
                    copy(page(U_PAGES[g % 2][j // 2]), two_banks(0)).then_inc(pu_done, 1)
                else:
                    A(mixp[2 * g + j // 2], two_banks(1), ACT.Sigmoid).then_inc(pgs_done, 1)

            h = HEADS - 1
            begin(h)
            act.wait_ge(fc_done, HEADS)
            pool_in(0, 0)
            o_norm(h - 1)
            take_vk(h)
            act.dma_start(page(PW[0]).rearrange("p (g c d) -> p g c d", g=2, c=2),
                          ap["pool_w"][0, 0:2].rearrange("g (c p) d -> p g c d", p=P)).then_inc(pw_in, 16)
            span_exp(h, 2)
            pool_in(0, 1)
            for j in (3, 4, 5):
                span_exp(h, j)
            pool_in(0, 2)
            span_exp(h, 6)
            pool_in(0, 3)
            o_squares(h)
            act.dma_start(page(PW[1]).rearrange("p (g c d) -> p g c d", g=2, c=2),
                          ap["pool_w"][0, 2:4].rearrange("g (c p) d -> p g c d", p=P)).then_inc(pw_in, 16)
            act.dma_start(page(RC)[:, 0:64], ap["k_inv_count"]).then_inc(rc_in, 16)
            pool_in(1, 0)
            o_norm(h)
            for j in range(1, 4):
                pool_in(1, j)
            for g in range(2, GROUPS):
                for j in range(4):
                    pool_in(g, j)

            def ring_hi(s0, u0, srcs, j0=0):
                for a, src in enumerate(srcs):
                    j = j0 + a // 2
                    if a % 2 == 0 and j >= 2:
                        act.wait_ge(w_used, u0 + j - 1)
                    copy(h_hi[:, 2 * (j % 2) + a % 2, :], src).then_inc(sp_hi, 1)

            def y_squares(e, n, src):
                for t in range(NT):
                    act.wait_ge(ycp_done, 16 * e + 8 * n + t + 1)
                    if 8 * n + t + 16 * e:
                        act.wait_ge(ysq_done, 16 * e + 8 * n + t)
                    A(h_hi[:, 7, 0:HALF] if e == 2 else page(25)[:, 0:HALF], src(t), ACT.Square,
                      accum_out=ss[:, 8 * n + t:8 * n + t + 1]).then_inc(ysq_done, 1)

            act.wait_ge(w_used, U_OUT)
            act.wait_ge(o_done, HEADS)
            act.wait_ge(pmix_done, 8)
            ring_hi(0, U_OUT, mixp)
            y_squares(0, 0, lambda t: Y[:, t, 0:HALF])
            ring_hi(16, U_OUT, mixp, 8)
            y_squares(0, 1, lambda t: Y[:, t, HALF:D])

            def residual_squares(n, done, spill, sem_out):
                for t in range(NT):
                    act.wait_ge(res_done, n + t + 1)
                    act.wait_ge(ss_done, done + t)
                    A(page(25), XR[:, t, :], ACT.Square, accum_out=ss[:, t:t + 1]).then_inc(ss_done, 1)
                    act.dma_start(spill[t], XR[:, t, :]).then_inc(sem_out, 16)

            root(1)
            act.wait_ge(rstd_done, 2)
            residual_squares(0, 8, x_mid[0], spilled[0])
            root(2)
            take_hi(1, lambda k: col("pre_mix_norm_2", k))

            act.wait_ge(tr_full, 16)
            act.wait_ge(ss_done, 16)
            act.dma_start(LN_ROWS[:, 0:512], ap["sgu_ln_gain_2"][0].partition_broadcast(P)).then_inc(lnrow_in, 16)
            act.dma_start(LN_ROWS[:, 512:1024], ap["sgu_ln_bias_2"][0].partition_broadcast(P)).then_inc(lnrow_in, 16)
            act.dma_start(page(SPAT).rearrange("p (g j) -> p g j", g=SGU_G), ap["sgu_w_spatial_2"][0].rearrange("g i j -> i g j")).then_inc(spat_in, 16)
            act.dma_start(page(25)[:, 0:P], ap["k_tril"]).then_inc(spat_in, 16)
            act.dma_start(ROPE[:, 320:328], ap["k_inv_freq"]).then_inc(freq_in, 16)
            act.wait_ge(rope_step, ROPE_STEPS)
            A(ROPE[:, 0:64], ROPE[:, 0:64], ACT.Sin).then_inc(trig_done, 1)
            A(ROPE[:, 64:128], ROPE[:, 64:128], ACT.Sin).then_inc(trig_done, 1)
            act.wait_ge(tril_done, 1)
            act.dma_start(BIAS, ap["k_bias"]).then_inc(bias_in, 16)
            act.wait_ge(spilled[0], 16 * NT)
            def gelu(b, dst, kw):
                for t in range(NT):
                    if t < NT - 1:
                        act.wait_ge(in2_full, 7 * b + t + 1)
                    else:
                        act.wait_ge(w_used, U_IN2 + 4 * b + 4)
                    A(dst[:, t, :], psum[:, t, :], ACT.Gelu, **kw(t)).then_inc(in2_free, 1)

            gelu(B_IVS, vs_b, lambda t: {"accum_out": sums[:, t:t + 1]})
            act.wait_ge(mean_done, 1)
            for t in range(NT):
                if t:
                    act.wait_ge(var_done, t)
                A(JUNK3, vs_b[:, t, :], ACT.Square, bias=mean[:, t:t + 1], accum_out=ss[:, t:t + 1]).then_inc(var_done, 1)
            root(3)
            gelu(B_IU, u_b, lambda t: {})
            act.wait_ge(spat_full, 1)
            copy(page(SPAT_T), two_banks(0)).then_inc(spat_tr, 1)
            take_hi(2)

            N = AH * NT

            def pt_copy(n):
                w = (n // AH + 1) * P
                act.wait_ge(pt_full, n + 1)
                if n >= 2:
                    act.wait_ge(pv_full, n - 1)
                copy(probs_t[n % 2][:, 0:w], two_banks(2)[:, 0:w]).then_inc(pt_done, 1)

            def mix_square(x, i, t, col_):
                act.wait_ge(ss_done, 16 + i)
                A(JUNK3, x[:, t, :], ACT.Square, accum_out=ss[:, col_:col_ + 1]).then_inc(ss_done, 1)

            for n in range(N + 2):
                if n >= 2:
                    pt_copy(n - 2)
                if n < N:
                    w = (n // AH + 1) * P
                    act.wait_ge(max_done, n + 1)
                    A(probs[n % 4][:, 0:w], probs[n % 4][:, 0:w], ACT.Exp, bias=neg_max[:, n % 8:n % 8 + 1],
                      accum_out=den_[:, n:n + 1]).then_inc(p_done, 1)
                if 0 <= n - N_SGU_SQ < NT:
                    act.wait_ge(sgu_done, SGU_G)
                    mix_square(u_b, n - N_SGU_SQ, n - N_SGU_SQ, NT + n - N_SGU_SQ)
                if n == N_SGU_NORM - 1:
                    root(4)
                if n >= N_SGU_NORM and n % 8 == 4 and (n - 12) // 8 < NT - 1:
                    for t in range(0 if n == N_SGU_NORM else (n - 12) // 8, (n - 12) // 8 + 1):
                        act.wait_ge(ao_done, 2 * t + 2)
                        mix_square(att_o, NT + t, t, t)
            act.wait_ge(ao_done, 2 * NT)
            mix_square(att_o, 2 * NT - 1, NT - 1, NT - 1)
            root(5)
            take_hi(3, lambda k: cols[:, VROW["attn_out_norm_2"] + k:VROW["attn_out_norm_2"] + k + 1], order=MIX2_ORDER)
            act.dma_start(POST_ROW, ap["post_mix_norm_2"][0].partition_broadcast(P)).then_inc(row_in, 16)

            y_squares(1, 0, lambda t: Y[:, t, 0:HALF])
            y_squares(1, 1, lambda t: Y[:, t, HALF:D])
            root(6)
            act.wait_ge(rstd_done, 7)
            residual_squares(NT, 32, x_mid[1], spilled[1])
            root(7)
            take_hi(4, lambda k: col("pre_ffn_norm_2", k))
            act.dma_start(ROW_F, ap["post_ffn_norm_2"][0].partition_broadcast(P)).then_inc(row_in, 16)

            act.wait_ge(spilled[1], 16 * NT)
            act.wait_ge(tr_full, 40)
            with act.Fori(0, FT // 2) as i:
                for j in range(2):
                    act.wait_ge(w_used, 4 * i + (U_GU + 2 * j + 1))
                    A(arena[:, bass.ds((2 * i + j) * PAGE, PAGE)], two_banks(2 * j), ACT.Silu).then_inc(gate_silu, 1)
            act.wait_ge(act_done, FT)
            act.wait_ge(w_used, U_DOWN)
            ring_hi(32, U_DOWN, actp)
            y_squares(2, 0, lambda t: y_half0[:, t, :])
            ring_hi(32 + FT, U_DOWN, actp, 11)
            y_squares(2, 1, lambda t: y_half1[:, t, :])
            root(8)

        @block.vector
        def _(dve):
            TT, TS, STT = dve.tensor_tensor, dve.tensor_scalar, dve.scalar_tensor_tensor

            def mean_square(src, width, eps):
                TS(ms, src, 1.0 / width, eps, ALU.mult, ALU.add).then_inc(ms_done, 1)

            def invert(m):
                dve.wait_ge(sqrt_done, m + 1)
                dve.reciprocal(rstd, ms).then_inc(rstd_done, 1)
                dve.wait_ge(rstd_done, m + 1)

            def stats(m, src, width, eps):
                mean_square(src, width, eps)
                invert(m)

            def take_lo(n, mul=None, add=None, order=range(KT)):
                for a, k in enumerate(order):
                    dve.wait_ge(hi_done, 8 * n + a + 1)
                    src = two_banks(2 + a % 2)
                    hi = h_hi[:, k, :].bitcast(F32)
                    if mul is None:
                        TT(h_lo[:, k, :], src, hi, ALU.subtract).then_inc(lo_done, 1)
                    elif add is None:
                        STT(h_lo[:, k, :], src, mul(k), hi, ALU.mult, ALU.subtract).then_inc(lo_done, 1)
                    else:
                        if k:
                            dve.wait_ge(lo_done, 8 * n + k)
                        TS(page(JUNK0), src, mul(k), add(k), ALU.mult, ALU.add).then_inc(lo_tmp, 1)
                        dve.wait_ge(lo_tmp, k + 1)
                        TT(h_lo[:, k, :], page(JUNK0), hi, ALU.subtract).then_inc(lo_done, 1)

            dve.memset(ones[:], 1.0).then_inc(ones_set, 1)
            dve.wait_ge(vec_t, 1)
            dve.tensor_copy(cols[:], psum[:, 4, 0:VROWS]).then_inc(cols_done, 1)
            dve.wait_ge(cols_done, 1)
            TT(lb_tmp, col("hgrn_lower_bounds", 0, 8), col("hgrn_lower_bounds", 0, 8), ALU.subtract).then_inc(lb_step, 1)
            dve.wait_ge(lb_exp, 1)
            dve.reciprocal(lb, lb_tmp).then_inc(lb_step, 1)
            dve.wait_ge(lb_step, 2)
            TT(lb_tmp, lb_tmp, lb, ALU.mult).then_inc(lb_step, 1)
            dve.wait_ge(lb_step, 3)
            TT(lb, lb_tmp, lb_tmp, ALU.subtract).then_inc(lb_step, 1)
            dve.wait_ge(lb_step, 4)
            TS(one_lb, lb, -1.0, 1.0, ALU.mult, ALU.add).then_inc(lb_step, 1)
            dve.wait_ge(silu_done, 1)
            acc = page(ACC, 3)
            x0 = tiles(X0)
            for k in range(KT):
                if k == 4:
                    dve.wait_ge(ss_done, NT)
                    stats(0, ss[:, 0:8], D, EPS)
                    for t in range(NT):
                        TS(x0[:, t, :], x0[:, t, :], rstd[:, t:t + 1], None, ALU.mult).then_inc(xn_done, 1)
                dve.wait_ge(ada_in[k % 3], 16 * (k // 3 + 1))
                w = page(ADA + 3 * (k % 3), 3)
                if k == 0:
                    TS(acc, w, silu_c[:, 0:1], None, ALU.mult).then_inc(ada_acc, 1)
                else:
                    dve.wait_ge(ada_acc, k)
                    STT(acc, w, silu_c[:, k:k + 1], acc, ALU.mult, ALU.add).then_inc(ada_acc, 1)
            dve.wait_ge(mod_mm, 1)
            TT(mod, psum[:, 5, 0:16], col("ada_b", 0, 16), ALU.add).then_inc(mod_done, 1)
            dve.wait_ge(mod_done, 1)
            STT(mul_a, mod[:, 8:16], 1.0, col("norm_pre_w", 0, 8), ALU.add, ALU.mult).then_inc(mod_done, 1)
            dve.wait_ge(mod_done, 2)
            dve.wait_ge(mod_mm, 2)
            dve.wait_ge(row_in, 32)
            TT(gate_row, two_banks(0), page(NPOST), ALU.mult).then_inc(mod_done, 1)
            take_lo(0, lambda k: mul_a[:, k:k + 1], lambda k: mod[:, k:k + 1])

            sig, kk_, bb, qq, qe = page(B_SIG), page(B_K), page(B_B), page(B_Q), page(B_QE)
            b_chunks = bb.rearrange("p (c t) -> p c t", t=P)

            def gate_g(it):
                dve.wait_ge(gsig_done, it + 1)
                m = arena[:, bass.ds((MIX + 8 + it) * PAGE, PAGE)]
                TT(m, m, two_banks(1), ALU.mult).then_inc(g_done, 1)

            def gate_f(it):
                dve.wait_ge(sig_done, it + 1)
                dve.wait_ge(lb_step, 5)
                i = it
                TS(sig, sig, one_lb[:, bass.ds(i, 1)], lb[:, bass.ds(i, 1)], ALU.mult, ALU.add).then_inc(f_done, 1)
                dve.wait_ge(f_done, it + 1)
                TS(kk_, sig, -1.0, 1.0, ALU.mult, ALU.add).then_inc(k_done, 1)
                TS(bb, sig, F_MIN, None, ALU.max).then_inc(fc_done, 1)

            def decay_sums(it, last=None):
                dve.wait_ge(lf_done, it + 1)
                if last is not None:
                    dve.wait_ge(task_full, last)
                for c in range(NT):
                    x = dve.tensor_tensor_scan(b_chunks[:, c, :], ones[:], b_chunks[:, c, :], 0.0, ALU.mult, ALU.add)
                x.then_inc(b_done, 1)

            def decayed_keys(it):
                dve.wait_ge(b_done, it + 1)
                kdt = page(B_KDT)
                TT(kdt.rearrange("p (c t) -> p c t", t=P), b_chunks[:, :, P - 1:P].to_broadcast([P, NT, P]), b_chunks, ALU.subtract).then_inc(dk_done, 1)
                dve.wait_ge(ek_done, it + 1)
                TT(kdt, kdt, kk_, ALU.mult).then_inc(kdec_done, 1)

            def halves(x, w):
                return x.rearrange("p (n u w) -> p n u w", u=2, w=w)

            def span_d(h, j):
                w = SPANS[j]
                d, b4 = halves(page(B_D[j % 3]), w), halves(bb, w)
                ref = b4[:, :, 0, w - 1:w].to_broadcast([P, S // (2 * w), w])
                if j >= 3:
                    dve.wait_ge(task_full, TASKS * h + SPAN_TASK[j - 3])
                TT(d[:, :, 1, :], b4[:, :, 1, :], ref, ALU.subtract)
                TT(d[:, :, 0, :], ref, b4[:, :, 0, :], ALU.subtract).then_inc(d_done, 1)

            def span_kq(h, j):
                e = page(B_D[j % 3])
                dve.wait_ge(e_done, NL * h + j + 1)
                if j >= 2:
                    dve.wait_ge(task_full, TASKS * h + SPAN_TASK[j - 2])
                TT(page(B_KL + j % 2), kk_, e, ALU.mult).then_inc(kl_done, 1)
                dve.wait_ge(kl_done, NL * h + j + 1)
                TT(e, qq, e, ALU.mult).then_inc(lvl_done, 1)

            att3 = page(B_ATT).rearrange("p (i t) -> p i t", t=P)

            def pick(h, j, at):
                w = SPANS[j]
                dve.wait_ge(const_in, 32)
                dve.wait_ge(task_full, at[j][0])
                dve.wait_ge(pick_done if j else diag_done, at[j][1])
                nb = P // (2 * w)
                data = two_banks(SPAN_SLOT[j])
                m = lvl_mask[:, j, :]
                if w == 64:
                    to, data = [x.rearrange("p (n u w) -> p n u w", u=2, w=w)[:, :, 1, :] for x in (page(B_ATT), data)]
                    m = m.rearrange("p (a c) -> p a c", a=1).to_broadcast([P, NT, 64])
                else:
                    to, data = [x.rearrange("p (i n u w) -> p i n u w", i=NT, u=2, w=w)[:, :, :, 1, :] for x in (page(B_ATT), data)]
                    m = m.rearrange("p (a n w) -> p a n w", a=1, w=w).to_broadcast([P, NT, nb, w])
                dve.copy_predicated(to, m, data).then_inc(pick_done, 1)

            def states(h):
                dve.wait_ge(task_full, TASKS * h + TASK_U)
                dve.wait_ge(end_done, h + 1)
                sst = page(B_S)
                for c in range(NT - 1):
                    u = two_banks(2)[:, c * P:(c + 1) * P]
                    if c == 0:
                        dve.tensor_copy(sst[:, 0:P], u).then_inc(s_done, 1)
                    else:
                        dve.wait_ge(s_done, (NT - 1) * h + c)
                        STT(sst[:, c * P:(c + 1) * P], sst[:, (c - 1) * P:c * P], end_decay[:, c:c + 1], u, ALU.mult, ALU.add).then_inc(s_done, 1)

            def spans(h, gate, f):
                at = [(TASKS * h + SPAN_TASK[min(j, 6) if j < 5 else 6], NL * h + j if j else h + 1) for j in range(NL)]
                if type(h) is not int:
                    at = [tuple(dve.snap(x) for x in a) for a in at]
                span_d(h, 0)
                span_d(h, 1)
                dve.wait_ge(q_done, h + 1)
                span_kq(h, 0)
                span_kq(h, 1)
                dve.wait_ge(eb_done, h + 1)
                TT(qe, qe, qq, ALU.mult).then_inc(qe_done, 1)
                if not (type(h) is int and h == 0):
                    back_3(h - 1)
                span_d(h, 2)
                if not (type(h) is int and h == 0):
                    dve.wait_ge(o_done, h)
                dve.wait_ge(task_full, TASKS * h + 3)
                TT(att3, two_banks(2).rearrange("p (i t) -> p i t", t=P), ident[:].rearrange("p (a t) -> p a t", a=1).to_broadcast([P, NT, P]), ALU.mult).then_inc(diag_done, 1)
                span_kq(h, 2)
                span_d(h, 3)
                pick(h, 0, at)
                gate()
                span_d(h, 4)
                pick(h, 1, at)
                span_d(h, 5)
                pick(h, 2, at)
                span_kq(h, 3)
                states(h)
                span_kq(h, 4)
                span_d(h, 6)
                pick(h, 3, at)
                span_kq(h, 5)
                span_kq(h, 6)
                pick(h, 4, at)
                f()
                pick(h, 5, at)
                pick(h, 6, at)

            def back_3(h):
                dve.wait_ge(rs_done, h + 1)
                t1 = page(B_ATT)
                STT(t1, two_banks(3), col("hgrn_norm_w"), page(B_SQ), ALU.mult, ALU.mult).then_inc(o1_done, 1)
                dve.wait_ge(o1_done, h + 1)
                dve.wait_ge(g_done, h + 1)
                m = arena[:, bass.ds((MIX + 8 + h) * PAGE, PAGE)]
                TT(m, m, t1, ALU.mult).then_inc(o_done, 1)

            gate_f(0)
            gate_g(0)
            decay_sums(0)
            decayed_keys(0)

            def step(it):
                def next_f():
                    gate_f(it)
                    decay_sums(it, TASKS * (it - 1) + SPAN_TASK[6])
                spans(it - 1, lambda: gate_g(it), next_f)
                decayed_keys(it)

            step(1)
            with dve.Fori(2, HEADS) as it:
                step(it)

            def pool_gate(g, j):
                dve.wait_ge(pgs_done, 2 * g + j + 1)
                m = mixp[2 * g + j]
                TT(m, m, two_banks(1), ALU.mult).then_inc(pg_done, 1)

            steps = [0]

            def wstep(x):
                x.then_inc(win_step, 1)
                steps[0] += 1
                dve.wait_ge(win_step, steps[0])

            def window(g):
                for c in range(2):
                    dve.wait_ge(pu_done, 2 * g + c + 1)
                    u = page(U_PAGES[g % 2][c])
                    src, w = u, 1
                    for a in range(g + 1):
                        dst = page((S_A, S_B)[a % 2])
                        dve.tensor_copy(dst[:, 0:w], src[:, 0:w]).then_inc(win_step, 1)
                        steps[0] += 1
                        wstep(TT(dst[:, w:S], src[:, w:S], src[:, 0:S - w], ALU.add))
                        src, w = dst, 2 * w
                    dve.wait_ge(rc_in, 16)
                    wstep(TT(src[:, 0:w], src[:, 0:w], page(RC)[:, 16 * g:16 * g + w], ALU.mult))
                    TT(u[:, 0:w], src[:, 0:w], u[:, 0:w], ALU.subtract).then_inc(win_step, 1)
                    steps[0] += 1
                    STT(u[:, w:S], src[:, w:S], 1.0 / w, u[:, w:S], ALU.mult, ALU.subtract).then_inc(pd_done, 1)
                    dve.wait_ge(pd_done, 2 * g + c + 1)

            def pool_out(g):
                for dt in range(2):
                    dve.wait_ge(pm_full, 2 * g + dt + 1)
                    dve.wait_ge(pg_done, 2 * g + dt + 1)
                    m = mixp[2 * g + dt]
                    STT(m, two_banks(2 + dt), col("pool_scale", 2 * g + dt), m, ALU.mult, ALU.mult).then_inc(pmix_done, 1)

            h = HEADS - 1
            spans(h, lambda: pool_gate(0, 0), lambda: pool_gate(0, 1))
            back_3(h)
            window(0)
            for g in range(1, GROUPS):
                pool_gate(g, 0)
                pool_gate(g, 1)
                pool_out(g - 1)
                window(g)
            pool_out(GROUPS - 1)

            def ring_lo(s0, u0, srcs, j0=0):
                for a, src in enumerate(srcs):
                    j = j0 + a // 2
                    k = 2 * (j % 2) + a % 2
                    dve.wait_ge(sp_hi, s0 + a + 1)
                    TT(h_lo[:, k, :], src, h_hi[:, k, :].bitcast(F32), ALU.subtract).then_inc(sp_lo, 1)

            def y_copy(e, n, u_last, dst):
                for t in range(NT):
                    if t < NT - 1:
                        dve.wait_ge(yb_full, 14 * e + 7 * n + t + 1)
                    else:
                        dve.wait_ge(w_used, u_last)
                    dve.tensor_copy(dst(t), psum[:, t, :]).then_inc(ycp_done, 1)

            def post(e, m, y):
                dve.wait_ge(ysq_done, 16 * e + 16)
                dve.wait_ge(ycp_done, 16 * e + 16)
                TT(sums, ss[:, 0:8], ss[:, 8:16], ALU.add).then_inc(sum_done, 1)
                dve.wait_ge(sum_done, e + 1)
                stats(m, sums, D, EPS)
                for t in range(NT):
                    yy = y(t)
                    for i, (o, r) in enumerate(yy):
                        x = STT(o, o, rstd[:, t:t + 1], r, ALU.mult, ALU.mult)
                        x.then_inc(res_step, 1)
                    dve.wait_ge(res_step, res_n[0] + len(yy))
                    res_n[0] += len(yy)
                    dve.wait_ge(x_in[t], 16 * (e + 2))
                    for i, (o, r) in enumerate(yy):
                        w = D // len(yy)
                        x = TT(XR[:, t, i * w:(i + 1) * w], XR[:, t, i * w:(i + 1) * w], o, ALU.add)
                    x.then_inc(res_done, 1)
            res_n = [0]

            def next_norm(m, done):
                dve.wait_ge(ss_done, done)
                stats(m, ss[:, 0:8], D, EPS)
                for t in range(NT):
                    TS(Y[:, t, :], XR[:, t, :], rstd[:, t:t + 1], None, ALU.mult).then_inc(xn_done, 1)

            ring_lo(0, U_OUT, mixp)
            y_copy(0, 0, U_OUT + 8, lambda t: Y[:, t, 0:HALF])
            ring_lo(16, U_OUT, mixp, 8)
            y_copy(0, 1, U_OUT + 16, lambda t: Y[:, t, HALF:D])
            post(0, 1, lambda t: [(Y[:, t, :], gate_row)])
            next_norm(2, 16)
            take_lo(1, lambda k: col("pre_mix_norm_2", k))

            dve.wait_ge(spat_in, 32)
            dve.wait_ge(tr_full, 16)
            sp3 = page(SPAT).rearrange("p (g j) -> p g j", g=SGU_G)
            tril = page(25)[:, 0:P].rearrange("p (a j) -> p a j", a=1).to_broadcast([P, SGU_G, P])
            TT(sp3, sp3, tril, ALU.mult).then_inc(tril_done, 1)

            steps_r = [0]

            def rstep(x):
                x.then_inc(rope_step, 1)
                steps_r[0] += 1
                dve.wait_ge(rope_step, steps_r[0])

            dve.wait_ge(pos_in, 16)
            dve.wait_ge(freq_in, 16)
            ang, ang2, turns, wrap = [ROPE[:, 64 * i:64 * (i + 1)] for i in range(4)]
            turns_i = ROPE[:, 256:320].bitcast(I32)
            freq, posf = ROPE[:, 320:328], ROPE[:, 328:336]
            rstep(dve.tensor_copy(posf, pos.bitcast(I32)))
            rstep(TT(ang.rearrange("p (t f) -> p t f", f=ROT),
                     posf.rearrange("p (t a) -> p t a", a=1).to_broadcast([P, NT, ROT]),
                     freq.rearrange("p (a f) -> p a f", a=1).to_broadcast([P, NT, ROT]), ALU.mult))
            rstep(TS(turns_i, ang, 1.0 / TWO_PI, None, ALU.mult))
            rstep(dve.tensor_copy(turns, turns_i))
            rstep(STT(ang, turns, -TWO_PI_HI, ang, ALU.mult, ALU.add))
            rstep(STT(ang, turns, -TWO_PI_LO, ang, ALU.mult, ALU.add))

            def wrapped(x):
                rstep(TS(wrap, x, math.pi, -TWO_PI, ALU.is_gt, ALU.mult))
                rstep(TT(x, x, wrap, ALU.add))
                rstep(TS(wrap, x, -math.pi, TWO_PI, ALU.is_lt, ALU.mult))
                rstep(TT(x, x, wrap, ALU.add))
                rstep(TS(x, x, PI_IN, -PI_IN, ALU.min, ALU.max))

            wrapped(ang)
            rstep(TS(ang2, ang, math.pi / 2, None, ALU.add))
            wrapped(ang2)
            assert steps_r[0] == ROPE_STEPS

            def vs_norm():
                dve.wait_ge(in2_free, NT * (B_IVS + 1))
                TS(mean, sums, -1.0 / ATT, None, ALU.mult).then_inc(mean_done, 1)
                dve.wait_ge(var_done, NT)
                stats(3, ss[:, 0:8], ATT, LN_EPS)
                dve.wait_ge(lnrow_in, 32)
                for t in range(NT):
                    x = TS(vs_b[:, t, :], vs_b[:, t, :], mean[:, t:t + 1], rstd[:, t:t + 1], ALU.add, ALU.mult)
                x.then_inc(lnorm, 1)
                dve.wait_ge(lnorm, 1)
                row3 = [LN_ROWS[:, a * ATT:(a + 1) * ATT].rearrange("p (a c) -> p a c", a=1).to_broadcast([P, NT, ATT]) for a in range(2)]
                TT(vs_b, vs_b, row3[0], ALU.mult).then_inc(lnorm, 1)
                dve.wait_ge(lnorm, 2)
                TT(vs_b, vs_b, row3[1], ALU.add).then_inc(ln2_done, 1)

            def in2_copy(b, dst, scale):
                for t in range(NT):
                    if t < NT - 1:
                        dve.wait_ge(in2_full, 7 * b + t + 1)
                    else:
                        dve.wait_ge(w_used, U_IN2 + 4 * b + 4)
                    if scale is None:
                        dve.tensor_copy(dst[:, t, :], psum[:, t, :]).then_inc(in2_free, 1)
                    else:
                        TS(dst[:, t, :], psum[:, t, :], scale, None, ALU.mult).then_inc(in2_free, 1)

            sin4, cos4 = [x.rearrange("p (t a f) -> p t a f", t=NT, a=1).to_broadcast([P, NT, AH, ROT]) for x in (ang, ang2)]
            tmp = [x.rearrange("p (t h f) -> p t h f", t=NT, h=AH) for x in ROPE_T]

            def rotate(i, x):
                dve.wait_ge(trig_done, 2)
                dve.wait_ge(in2_free, NT * ((B_IQ, B_IK)[i] + 1))
                x1, x2 = [x.rearrange("p t (h d) -> p t h d", d=DH)[:, :, :, a * ROT:(a + 1) * ROT] for a in range(2)]
                rstep(TT(tmp[0], x1, cos4, ALU.mult))
                rstep(TT(tmp[1], x2, sin4, ALU.mult))
                rstep(TT(tmp[0], tmp[0], tmp[1], ALU.subtract))
                rstep(TT(tmp[1], x2, cos4, ALU.mult))
                rstep(TT(tmp[2], x1, sin4, ALU.mult))
                rstep(dve.tensor_copy(x1, tmp[0]))
                TT(x2, tmp[1], tmp[2], ALU.add).then_inc(rope_done, 1)
                dve.wait_ge(rope_done, i + 1)

            in2_copy(B_IQ, q_b, DH ** -0.5)
            rotate(0, q_b)
            vs_norm()
            in2_copy(B_IK, k_b, None)
            rotate(1, k_b)
            in2_copy(B_IV, v_b, None)

            def spatial(g):
                dve.wait_ge(sgu_full, g + 1)
                ug = u_b[:, :, g * DH:(g + 1) * DH]
                STT(ug, psum[:, 1 + 2 * (g % 2), :].rearrange("p (t c) -> p t c", c=DH), col("sgu_b_spatial_2", g), ug,
                    ALU.add, ALU.mult).then_inc(sgu_done, 1)

            take_lo(2)

            dve.wait_ge(bias_in, 16)

            def attended(m):
                i, hh = m // 2, m % 2
                dve.wait_ge(pv_full, 4 * m + 4)
                dve.reciprocal(r_den[:, 4 * hh:4 * hh + 4], den_[:, 4 * m:4 * m + 4]).then_inc(den_done, 1)
                dve.wait_ge(den_done, m + 1)
                for a in range(2):
                    o = att_o[:, i, hh * 256:(hh + 1) * 256].rearrange("p (e a d) -> p e a d", a=2, d=DH)[:, :, a, :]
                    src = psum[:, 6 + hh, :].rearrange("p (e a x d) -> p e a x d", a=2, x=2, d=DH)[:, :, a, a, :]
                    r = r_den[:, 4 * hh:4 * hh + 4].rearrange("p (e a x) -> p e a x", a=2, x=1)[:, :, a, :].to_broadcast([P, 2, DH])
                    x = TT(o, src, r, ALU.mult)
                x.then_inc(ao_done, 1)

            for n in range(AH * NT):
                i = n // AH
                w = (i + 1) * P
                dve.wait_ge(s_full, n + 1)
                if n >= 4:
                    dve.wait_ge(pt_full, n - 3)
                TT(probs[n % 4][:, 0:w], two_banks(n % 2)[:, 0:w], BIAS[:, PAGE - w:PAGE], ALU.add).then_inc(s_moved, 1)
                dve.wait_ge(s_moved, n + 1)
                dve.reduce_max(neg_max[:, n % 8:n % 8 + 1], probs[n % 4][:, 0:w], AX.X, negate=True).then_inc(max_done, 1)
                if n >= 6 and n % 4 == 2:
                    attended((n - 6) // 4)
                if 0 <= n - N_SGU < SGU_G:
                    spatial(n - N_SGU)
                if n == N_SGU_NORM - 2:
                    dve.wait_ge(ss_done, 16 + NT)
                    mean_square(ss[:, NT:2 * NT], ATT, EPS)
                if n == N_SGU_NORM:
                    invert(4)
                if 0 <= n - N_SGU_NORM < NT:
                    t = n - N_SGU_NORM
                    TS(u_b[:, t, :], u_b[:, t, :], rstd[:, t:t + 1], None, ALU.mult).then_inc(mixn_done, 1)
            attended(2 * NT - 1)
            dve.wait_ge(ss_done, 16 + 2 * NT)
            stats(5, ss[:, 0:NT], ATT, EPS)
            for t in range(NT):
                TS(att_o[:, t, :], att_o[:, t, :], rstd[:, t:t + 1], None, ALU.mult).then_inc(mixn_done, 1)
            take_lo(3, lambda k: cols[:, VROW["attn_out_norm_2"] + k:VROW["attn_out_norm_2"] + k + 1], order=MIX2_ORDER)
            y_copy(1, 0, U_OUT2 + 4, lambda t: Y[:, t, 0:HALF])
            y_copy(1, 1, U_OUT2 + 8, lambda t: Y[:, t, HALF:D])
            dve.wait_ge(row_in, 48)
            post(1, 6, lambda t: [(Y[:, t, :], POST_ROW)])
            next_norm(7, 40)
            take_lo(4, lambda k: col("pre_ffn_norm_2", k))

            with dve.Fori(0, FT // 2) as i:
                for j in range(2):
                    dve.wait_ge(gate_silu, 2 * i + (j + 1))
                    dve.wait_ge(w_used, 4 * i + (U_GU + 2 * j + 2))
                    a = arena[:, bass.ds((2 * i + j) * PAGE, PAGE)]
                    TT(a, a, two_banks(2 * j + 1), ALU.mult).then_inc(act_done, 1)
            ring_lo(32, U_DOWN, actp)
            y_copy(2, 0, U_DOWN + 11, lambda t: y_half0[:, t, :])
            ring_lo(32 + FT, U_DOWN, actp, 11)
            y_copy(2, 1, U_DOWN + 22, lambda t: y_half1[:, t, :])
            dve.wait_ge(row_in, 64)
            post(2, 8, lambda t: [(y_half0[:, t, :], ROW_F[:, 0:HALF]), (y_half1[:, t, :], ROW_F[:, HALF:D])])


def constants():
    i = np.arange(P)
    mask = np.zeros((P, NL, 64), np.int32)
    for j, w in enumerate(SPANS):
        x = np.arange(64)
        block = x // w
        mask[:, j, :] = (i[:, None] // (2 * w) == block[None, :]) & (i[:, None] % (2 * w) < w)
    d = (S - P) + i[:, None] - np.arange(S)[None, :]
    n = ((d >= 0) & (d <= 128)).astype(int) + ((d >= 0) & (d <= 512) & (d % 4 == 0)) + ((d >= 0) & (d % 16 == 0))
    bias = np.where(n > 0, np.log(np.maximum(n, 1)), NEG).astype(np.float32)
    freq = np.float32(500000.0) ** (-np.arange(0, 2 * ROT, 2, dtype=np.float32) / np.float32(2 * ROT))
    count = np.array([[1.0 / min(t + 1, w) for t in range(16)] for w in POOL_WINDOWS], np.float32).reshape(1, 64)
    return {
        "k_ident": np.eye(P, dtype=np.float32),
        "k_level_mask": mask,
        "k_tril": np.tril(np.ones((P, P), np.float32)),
        "k_bias": bias,
        "k_inv_freq": np.repeat(freq.astype(np.float32).reshape(1, ROT), P, 0),
        "k_inv_count": np.repeat(count, P, 0),
    }


INPUTS = ["x", "c", "norm_pre_w", "ada_w", "ada_b", "w_in", "pool_w", "pool_scale", "hgrn_lower_bounds",
          "hgrn_norm_w", "w_out", "norm_post_w", "positions_2", "pre_mix_norm_2", "w_in_2", "sgu_ln_gain_2",
          "sgu_ln_bias_2", "sgu_w_spatial_2", "sgu_b_spatial_2", "attn_out_norm_2", "sgu_out_norm_2", "w_out_2",
          "post_mix_norm_2", "pre_ffn_norm_2", "w_gate_2", "w_up_2", "w_down_2", "post_ffn_norm_2"]


def kernel(**inputs):
    import concourse.bacc as bacc
    from concourse.bass_utils import run_bass_kernel_spmd

    nc = bacc.Bacc("TRN2", target_bir_lowering=False, num_devices=1)
    arrays = {name: np.ascontiguousarray(inputs[name]) for name in INPUTS}
    arrays.update(constants())
    ap = {}
    for name, a in arrays.items():
        ap[name] = nc.dram_tensor(name, a.shape, mybir.dt.from_np(a.dtype), kind="ExternalInput").ap()
    out = nc.dram_tensor("out", (1, S, D), F32, kind="ExternalOutput").ap()
    ap["out"] = out.rearrange("b (t p) d -> (b t) p d", p=P)
    program(nc, ap)
    r = run_bass_kernel_spmd(nc, [arrays], core_ids=[0])
    return r.results[0]["out"]
```

```python
import math
from contextlib import ExitStack

import numpy as np

import concourse.bass as bass
import concourse.mybir as mybir

F32 = mybir.dt.float32
F32R = mybir.dt.float32r
I32 = mybir.dt.int32
ACT = mybir.ActivationFunctionType
ALU = mybir.AluOpType
AX = mybir.AxisListType

P = 128
D = 1024
S = 1024
KT = D // P
NT = S // P
HALF = 512
PAGE = 1024

HEADS = 8
SPANS = [64, 32, 16, 8, 4, 2, 1]
NL = len(SPANS)
POOL_WINDOWS = (2, 4, 8, 16)
GROUPS = 4
G_ORDER = [0, 2, 3, 1]
F_MIN = 1e-19

DH = 64
AH = 8
ATT = 512
ROT = 8
SGU_G = 8
D_FF = 2816
FT = D_FF // P
EPS = 1e-6
LN_EPS = 1e-5
TWO_PI = 2 * math.pi
TWO_PI_HI = 6.28125
TWO_PI_LO = TWO_PI - TWO_PI_HI
PI_IN = 3.1415925
ROPE_STEPS = 17
NEG = -1e30

VEC = [("ada_b", 24), ("norm_pre_w", 8), ("pool_scale", 8), ("hgrn_lower_bounds", 8),
       ("hgrn_norm_w", 1), ("pre_mix_norm_2", 8), ("attn_out_norm_2", 4), ("sgu_out_norm_2", 4),
       ("pre_ffn_norm_2", 8), ("sgu_b_spatial_2", 8)]
VROW, VROWS = {}, 0
for _name, _n in VEC:
    VROW[_name] = VROWS
    VROWS += _n

U_HGRN = 0
U_POOL = U_HGRN + 4 * HEADS
U_OUT = U_POOL + 4 * GROUPS
U_IN2 = U_OUT + 16
U_OUT2 = U_IN2 + 20
U_GU = U_OUT2 + 8
U_DOWN = U_GU + 2 * FT
UNITS = U_DOWN + FT
RAW = 4

TASKS = 13
SPAN_TASK = [4, 5, 6, 8, 9, 10, 11]
SPAN_SLOT = [3, 2, 3, 3, 2, 3, 2]
TASK_U, TASK_O, TASK_MS = 7, 12, 13
C_U, C_G, C_Q, C_F, C_V, C_GH = 0, 8, 16, 24, 32, 40
IN2_BLOCKS = [0, 4, 1, 2, 3]
B_IQ, B_IK, B_IV, B_IU, B_IVS = [IN2_BLOCKS.index(_b) for _b in range(5)]
N_SGU, N_SGU_SQ, N_SGU_NORM = 8, 17, 28
T_ORDER = [4, 5, 6, 7, 0, 1, 2, 3]
PAIRS = [T_ORDER[2 * _r:2 * _r + 2] for _r in range(NT // 2)]
M_NORM, M_LN, M_SGU, M_ATT = 0, 6, 7, 8
M_RES = [1, 9, 14]
T_BASE = [0, 2 * KT, 4 * KT, 5 * KT, 6 * KT]
T_END = 8 * KT
T_SLOTS = {2: [2, 3, 1], 3: [2, 3, 0, 1]}
MIX2_ORDER = [4, 5, 6, 7, 0, 1, 2, 3]


def program(nc, ap):
    ctx = ExitStack()
    with ctx:
        def sb(name, shape, dt=F32):
            return ctx.enter_context(nc.sbuf_tensor(name, shape, dt))

        def sem(name):
            return ctx.enter_context(nc.semaphore(name))

        h_hi = sb("h_hi", [P, KT, S], F32R)
        h_lo = sb("h_lo", [P, KT, S], F32R)
        w_raw = sb("w_raw", [P, RAW, 1024])
        w_hi = sb("w_hi", [P, 2, 1024], F32R)
        w_lo = sb("w_lo", [P, 2, 1024], F32R)
        arena = sb("arena", [P, 27 * PAGE])
        ident = sb("ident", [P, P])
        ones = sb("ones", [P, P])
        cols = sb("cols", [P, VROWS])
        lvl_mask = sb("lvl_mask", [P, NL, 64], I32)
        st = sb("st", [P, 160])
        psum = ctx.enter_context(nc.psum_tensor("psum", [P, 8, HALF], F32))

        def page(i, n=1):
            return arena[:, i * PAGE:(i + n) * PAGE]

        def tiles(i, n=NT):
            return page(i, n).rearrange("p (t c) -> p t c", c=PAGE)

        def two_banks(slot):
            return psum[:, 2 * slot:2 * slot + 2, :].rearrange("p b n -> p (b n)")

        def half_bank(n, half):
            return 0 if n == 1 and half == 0 else 4

        def col(name, i=0, n=1):
            return cols[:, VROW[name] + i:VROW[name] + i + n]

        silu_c = st[:, 0:8]
        c_col = silu_c
        mod = st[:, 8:24]
        mul_a = st[:, 24:32]
        lb = st[:, 32:40]
        one_lb = st[:, 40:48]
        lb_tmp = st[:, 48:56]
        ss = st[:, 56:72]
        ms = st[:, 72:80]
        rstd = st[:, 80:88]
        end_decay = st[:, 88:96]
        mean = st[:, 96:104]
        neg_max = st[:, 104:112]
        r_den = st[:, 112:120]
        pos = st[:, 120:128]
        sums = st[:, 128:136]
        ms_half0 = st[:, 136:144]
        ms_pair = [st[:, 144 + 4 * i:148 + 4 * i] for i in range(2)]
        rstd_pair = [st[:, 152 + 4 * i:156 + 4 * i] for i in range(2)]
        den_ = page(26)[:, 0:AH * NT]

        X0 = 0
        ADA = 8
        ACC = 17
        GATE_W = [9, 10, 11, 12, 13, 14, 15, 24]
        JUNK0, JUNK1 = 20, 21
        ADAB = 22
        GATE_ROW = 26
        NPOST = 25
        MIX = 0
        B_SIG, B_K, B_B, B_Q, B_QE, B_VT, B_V, B_KDT, B_KD, B_ATT = range(16, 26)
        B_SQ = 7
        B_S, B_D, B_KL = 2, (3, 4, 7), 5
        U_PAGES = [(16, 21), (17, 18)]
        S_A, S_B = 22, 24
        PW = [23, 19]
        RC = 20

        gate_row = page(GATE_ROW)
        mixp = [page(MIX + i) for i in range(16)]
        mix_ring = mixp[8:] + mixp[:8]
        Y = tiles(16)
        XR = tiles(0)
        vs_b, u_b, v_b, q_b, k_b = [page(4 * i, 4).rearrange("p (t c) -> p t c", c=ATT) for i in range(5)]
        SPAT, SPAT_T = 20, 21
        ROPE = page(22)
        ROPE_T = [page(23)[:, 0:512], page(23)[:, 512:1024], page(26)[:, 0:512]]
        JUNK3 = page(26)[:, 512:1024]
        LN_ROWS = page(24)
        BIAS = page(25)
        probs = [page(16 + i) for i in range(4)]
        probs_t = [page(22 + i) for i in range(2)]
        att_o = q_b
        POST_ROW = page(24)
        ROW_F = page(26)
        actp = [page(i) for i in range(FT)]
        y_half0 = page(22, 4).rearrange("p (t c) -> p t c", c=HALF)
        y_half1 = page(8, 4).rearrange("p (t c) -> p t c", c=HALF)

        x_mid = [nc.dram_tensor(f"x_mid{i}", [NT, P, D], F32, kind="Internal").ap() for i in range(2)]

        raw_in = [sem(f"raw_in{i}") for i in range(RAW)]
        w_rounded, w_ready, w_used = sem("w_rounded"), sem("w_ready"), sem("w_used")
        c_in, const_in, vec_in, pos_in, row_in = sem("c_in"), sem("const_in"), sem("vec_in"), sem("pos_in"), sem("row_in")
        x_in = [sem(f"x_in{t}") for t in range(NT)]
        ada_in = [sem(f"ada_in{i}") for i in range(4)]
        gate_in, gate_acc = sem("gate_in"), sem("gate_acc")
        ones_set, vec_t, cols_done = sem("ones_set"), sem("vec_t"), sem("cols_done")
        silu_done, ada_acc, mod_mm, mod_done = sem("silu_done"), sem("ada_acc"), sem("mod_mm"), sem("mod_done")
        lb_step, lb_exp = sem("lb_step"), sem("lb_exp")
        ss_done, ms_done, sqrt_done, rstd_done = sem("ss_done"), sem("ms_done"), sem("sqrt_done"), sem("rstd_done")
        xn_done, tr_full, hi_done, lo_tmp, lo_done = (sem("xn_done"), sem("tr_full"), sem("hi_done"),
                                                      sem("lo_tmp"), sem("lo_done"))
        whole_done = sem("whole_done")
        sig_done, gsig_done, g_done, vt_done, q_done = (sem("sig_done"), sem("gsig_done"), sem("g_done"),
                                                        sem("vt_done"), sem("q_done"))
        f_done, k_done, fc_done, lf_done, b_done = (sem("f_done"), sem("k_done"), sem("fc_done"),
                                                    sem("lf_done"), sem("b_done"))
        eb_done, end_done, dk_done, ek_done, kdec_done, qe_done = (
            sem("eb_done"), sem("end_done"), sem("dk_done"), sem("ek_done"), sem("kdec_done"), sem("qe_done"))
        d_done, e_done, kl_done, lvl_done, task_full = (sem("d_done"), sem("e_done"), sem("kl_done"),
                                                        sem("lvl_done"), sem("task_full"))
        v_done, kd_done, diag_done, pick_done, s_done = (sem("v_done"), sem("kd_done"), sem("diag_done"),
                                                         sem("pick_done"), sem("s_done"))
        sq_done, ln_done, rs_done, o1_done, o_done = (sem("sq_done"), sem("ln_done"), sem("rs_done"),
                                                      sem("o1_done"), sem("o_done"))
        pu_done, pgs_done, pg_done, win_step, pd_done, pm_full, pmix_done, pw_in, rc_in = (
            sem("pu_done"), sem("pgs_done"), sem("pg_done"), sem("win_step"), sem("pd_done"), sem("pm_full"),
            sem("pmix_done"), sem("pw_in"), sem("rc_in"))
        sp_hi, sp_lo, yb_full, ycp_done, ysq_done = (sem("sp_hi"), sem("sp_lo"), sem("yb_full"),
                                                     sem("ycp_done"), sem("ysq_done"))
        sum_done, res_done, spilled = sem("sum_done"), sem("res_done"), [sem("spilled0"), sem("spilled1")]
        in2_free, in2_full, lnrow_in, spat_in, bias_in, freq_in = (
            sem("in2_free"), sem("in2_full"), sem("lnrow_in"), sem("spat_in"), sem("bias_in"), sem("freq_in"))
        mean_done, var_done, lnorm = sem("mean_done"), sem("var_done"), sem("lnorm")
        tril_done, spat_full, spat_tr, sgu_full, sgu_done = (sem("tril_done"), sem("spat_full"), sem("spat_tr"),
                                                             sem("sgu_full"), sem("sgu_done"))
        rope_step, trig_done, rope_done = sem("rope_step"), sem("trig_done"), sem("rope_done")
        s_full, s_moved, max_done, p_done, pt_full, pt_done, pv_full, den_done, ao_done = (
            sem("s_full"), sem("s_moved"), sem("max_done"), sem("p_done"), sem("pt_full"), sem("pt_done"),
            sem("pv_full"), sem("den_done"), sem("ao_done"))
        gate_silu, act_done, out_sent, mixn_done = sem("gate_silu"), sem("act_done"), sem("out_sent"), sem("mixn_done")
        ln2_done = sem("ln2_done")

        block = ctx.enter_context(nc.Block())

        fm = lambda w: w[0].rearrange("(k p) (f c) -> f p k c", p=P, c=P)
        tm = lambda w: w[0].rearrange("(j k p) (n c) -> n j p k c", k=2, p=P, c=HALF)
        w_in_fm, gate_fm, up_fm = fm(ap["w_in"]), fm(ap["w_gate_2"]), fm(ap["w_up_2"])
        w_out_tm, w_in2_tm, w_out2_tm, down_tm = tm(ap["w_out"]), tm(ap["w_in_2"]), tm(ap["w_out_2"]), tm(ap["w_down_2"])

        @block.sync
        def _(sp):
            ada_v = ap["ada_w"][0].rearrange("(k p) n -> k p n", p=P)

            def load_ada(k):
                sp.dma_start(page(ADA + 2 * (k % 4), 2), ada_v[k][:, 0:2 * D]).then_inc(ada_in[k % 4], 16)

            sp.dma_start(c_col, ap["c"].rearrange("a (k p) -> p (a k)", p=P), allow_slow_non_contiguous=True).then_inc(c_in, 16)
            for k in range(4):
                load_ada(k)
            sp.dma_start(ident[:], ap["k_ident"]).then_inc(const_in, 16)
            for name, n in VEC:
                r = VROW[name]
                src = ap[name]
                src = src[0] if len(src.shape) > 2 else src
                if name == "sgu_b_spatial_2":
                    flat = src
                else:
                    flat = src.rearrange("a (r c) -> (a r) c", c=P)
                sp.dma_start(arena[r:r + n, JUNK0 * PAGE:JUNK0 * PAGE + P], flat).then_inc(vec_in, 16)
            sp.dma_start(lvl_mask[:], ap["k_level_mask"]).then_inc(const_in, 16)
            for k in range(4, KT):
                sp.wait_ge(ada_acc, k - 3)
                load_ada(k)

            def slot_fm(s):
                return w_raw[:, s, :].rearrange("p (k c) -> p k c", c=P)

            def slot_tm(s):
                return w_raw[:, s, :].rearrange("p (k c) -> p k c", c=HALF)

            def load(s, dst, src):
                sp.dma_start(dst, src).then_inc(raw_in[s], 16)

            for s, c in enumerate((C_F, C_GH, C_V, C_Q)):
                load(s, slot_fm(s), w_in_fm[c])
            sp.dma_start(pos.bitcast(I32), ap["positions_2"][0].rearrange("(t p) -> p t", p=P), allow_slow_non_contiguous=True).then_inc(pos_in, 16)
            sp.dma_start(arena[0:1, ADAB * PAGE:(ADAB + 1) * PAGE], ap["ada_b"][0:1, 2 * D:3 * D]).then_inc(row_in, 16)
            sp.dma_start(page(NPOST), ap["norm_post_w"][0].partition_broadcast(P)).then_inc(row_in, 16)
            sp.wait_ge(ada_acc, KT)
            for k in range(KT):
                sp.dma_start(page(GATE_W[k]), ada_v[k][:, 2 * D:3 * D]).then_inc(gate_in, 16)
            with sp.Fori(1, HEADS) as h:
                for s, c in enumerate((C_F, C_GH, C_V, C_Q)):
                    sp.wait_ge(w_ready, 4 * h + s - 3)
                    load(s, slot_fm(s), w_in_fm[h + c])
            for i, g in enumerate(G_ORDER):
                for s in range(4):
                    sp.wait_ge(w_ready, U_POOL + 4 * i + s - 3)
                    load(s, slot_fm(s), w_in_fm[2 * g + s // 2 + (C_U, C_G)[s % 2]])
            for n in range(2):
                for j in range(8):
                    sp.wait_ge(w_ready, U_OUT + 8 * n + j - 3)
                    load(j % RAW, slot_tm(j % RAW), w_out_tm[n][(j + 4) % 8])
            for t in range(NT):
                sp.wait_ge(sp_lo, 24 + t + 1)
                sp.dma_start(XR[:, t, :], ap["x"][0, t * P:(t + 1) * P, :]).then_inc(x_in[t], 16)
            for b, blk in enumerate(IN2_BLOCKS):
                for s in range(4):
                    sp.wait_ge(w_ready, U_IN2 + 4 * b + s - 3)
                    load(s, slot_tm(s), w_in2_tm[blk][s])
            for n in range(2):
                for s in range(4):
                    sp.wait_ge(w_ready, U_OUT2 + 4 * n + s - 3)
                    load(s, slot_tm(s), w_out2_tm[n][s])
            for t in range(NT):
                sp.wait_ge(tr_full, T_BASE[4])
                sp.wait_ge(spilled[0], 16 * NT)
                sp.dma_start(XR[:, t, :], x_mid[0][t]).then_inc(x_in[t], 16)
            with sp.Fori(0, FT // 2) as i:
                for s in range(4):
                    sp.wait_ge(w_ready, 4 * i + (U_GU + s - 3))
                    load(s, slot_fm(s), (gate_fm, up_fm)[s % 2][2 * i + s // 2])
            for j in range(FT):
                s = j % RAW
                sp.wait_ge(w_ready, U_DOWN + j - 3)
                load(s, slot_tm(s), down_tm[j // 11][j % 11])
            for t in range(NT):
                sp.wait_ge(sp_lo, 32 + FT + t + 1)
                sp.wait_ge(spilled[1], 16 * NT)
                sp.dma_start(XR[:, t, :], x_mid[1][t]).then_inc(x_in[t], 16)
            for a, t in enumerate(T_ORDER):
                sp.wait_ge(res_done, 2 * NT + a + 1)
                sp.dma_start(ap["out"][t], XR[:, t, :]).then_inc(out_sent, 16)
            sp.wait_ge(out_sent, 16 * NT)

        @block.gpsimd
        def _(pool):
            unit_scale = ones[:].rearrange("p (a n) -> p a n", a=1).to_broadcast([P, KT, P])

            def split(i, s, first):
                c = s % 2
                raw = w_raw[:, s, :]
                pool.wait_ge(raw_in[s], 16 * i + 16)
                if not (first and s < 2):
                    pool.wait_ge(w_used, 4 * i + s - 1)
                pool.tensor_tensor(w_hi[:, c, :].rearrange("p (a n) -> p a n", n=P), raw.rearrange("p (a n) -> p a n", n=P),
                                   unit_scale, ALU.mult).then_inc(w_rounded, 1)
                pool.wait_ge(w_rounded, 4 * i + s + 1)
                pool.tensor_tensor(w_lo[:, c, :], raw, w_hi[:, c, :].bitcast(F32), ALU.subtract).then_inc(w_ready, 1)

            pool.wait_ge(ones_set, 1)
            for s in range(4):
                split(0, s, True)
            with pool.Fori(1, UNITS // 4) as i:
                for s in range(4):
                    split(i, s, False)
            for s in range(UNITS % 4):
                split(UNITS // 4, s, False)

        @block.tensor
        def _(pe):
            def fm_k(c, o, k, half):
                wh = w_hi[:, c, k * P:(k + 1) * P]
                wl = w_lo[:, c, k * P:(k + 1) * P]
                xh = h_hi[:, k, half * HALF:(half + 1) * HALF]
                xl = h_lo[:, k, half * HALF:(half + 1) * HALF]
                pe.matmul(o, wh, xh, start=(k == 0), stop=False)
                pe.matmul(o, wh, xl, start=False, stop=False)
                return pe.matmul(o, wl, xh, start=False, stop=(k == KT - 1))

            def fm_half(c, out, half):
                for k in range(KT):
                    mm = fm_k(c, out[:, half * HALF:(half + 1) * HALF], k, half)
                return mm

            def fm_unit(c, out):
                fm_half(c, out, 0)
                return fm_half(c, out, 1)

            def tm_rows(c, kk, k, t, start, stop):
                xh = h_hi[:, k, t * P:(t + 1) * P]
                xl = h_lo[:, k, t * P:(t + 1) * P]
                wh = w_hi[:, c, kk * HALF:(kk + 1) * HALF]
                wl = w_lo[:, c, kk * HALF:(kk + 1) * HALF]
                pe.matmul(psum[:, t, :], xh, wh, start=start, stop=False)
                pe.matmul(psum[:, t, :], xh, wl, start=False, stop=False)
                return pe.matmul(psum[:, t, :], xl, wh, start=False, stop=stop)

            def transposes(n, src, order=range(KT), ready=None):
                ring = T_SLOTS[n]
                for a, k in enumerate(order):
                    if ready is not None and ready[a]:
                        pe.wait_ge(*ready[a])
                    if a >= len(ring):
                        taken(T_BASE[n] + a - len(ring) + 1)
                    for t in range(NT):
                        o = two_banks(ring[a % len(ring)])[:, t * P:(t + 1) * P]
                        mm = pe.transpose(o, src(t, k), ident[:])
                    mm.then_inc(tr_full, 1)

            def taken(n):
                pe.wait_ge(hi_done, n)
                pe.wait_ge(lo_done, n)

            def transpose_half(n, half, ks, src=None):
                for k in ks:
                    i = T_BASE[n] + KT * (1 - half) + k
                    if i - T_BASE[n] >= 4:
                        taken(i - 3)
                    for a in range(4):
                        t = 4 * half + a
                        mm = pe.transpose(psum[:, half_bank(n, half) + k % 4, a * P:(a + 1) * P], (Y if src is None else src)[:, t, k * P:(k + 1) * P], ident[:])
                    mm.then_inc(tr_full, 1)

            def fm_half_staged(n, half, c, out, src=None):
                first = T_BASE[n] + KT * (1 - half)
                o = out[:, half * HALF:(half + 1) * HALF]
                for k in range(KT):
                    if k < 4:
                        transpose_half(n, half, [k + 4], src)
                    taken(first + k + 1)
                    mm = fm_k(c, o, k, half)
                return mm

            def ready(u):
                pe.wait_ge(w_ready, u + 1)

            pe.wait_ge(vec_in, 16 * len(VEC))
            pe.wait_ge(const_in, 32)
            pe.transpose(psum[:, 1, 0:VROWS], arena[0:VROWS, JUNK0 * PAGE:JUNK0 * PAGE + P], ident[0:VROWS, 0:VROWS]).then_inc(vec_t, 1)
            x0 = tiles(X0)
            pe.wait_ge(xn_done, NT)
            transpose_half(0, 1, range(4), x0)
            pe.wait_ge(ada_acc, KT)
            pe.wait_ge(ones_set, 1)
            acc = page(ACC, 2)
            for f in range(16):
                mm = pe.matmul(psum[:, 0, f:f + 1], acc[:, f * P:(f + 1) * P], ones[:, 0:1], start=True, stop=True)
            mm.then_inc(mod_mm, 1)

            V, KD, ATTN, SST = page(B_V), page(B_KD), page(B_ATT), page(B_S)

            def z_unit(u, j, out):
                pe.wait_ge(w_ready, u + 1)
                fm_unit(j % 2, out).then_inc(w_used, 1)

            def blocks128(x, i):
                return x[:, i * P:(i + 1) * P]

            def task_t0(h):
                pe.wait_ge(vt_done, h + 1)
                if not (type(h) is int and h == 0):
                    pe.wait_ge(ln_done, h)
                for i in range(NT):
                    mm = pe.transpose(blocks128(two_banks(2), i), blocks128(page(B_VT), i), ident[:])
                mm.then_inc(task_full, 1)

            def task_t1(h):
                pe.wait_ge(kdec_done, h + 1)
                if not (type(h) is int and h == 0):
                    pe.wait_ge(o1_done, h)
                for i in range(NT):
                    mm = pe.transpose(blocks128(two_banks(3), i), blocks128(page(B_KDT), i), ident[:])
                mm.then_inc(task_full, 1)

            def task_diag(h):
                pe.wait_ge(v_done, h + 1)
                pe.wait_ge(q_done, h + 1)
                pe.wait_ge(k_done, h + 1)
                for i in range(NT):
                    mm = pe.matmul(blocks128(two_banks(2), i), blocks128(page(B_K), i), blocks128(page(B_Q), i), start=True, stop=True)
                mm.then_inc(task_full, 1)

            def task_span(h, j):
                taken = [(kd_done, h + 1), (diag_done, h + 1), (pick_done, NL * h + 1), (pick_done, NL * h + 3),
                         (s_done, (NT - 1) * h + NT - 1), (pick_done, NL * h + 4), (pick_done, NL * h + 5)][j]
                pe.wait_ge(*taken)
                pe.wait_ge(lvl_done, NL * h + j + 1)
                for i in range(NT):
                    mm = pe.matmul(blocks128(two_banks(SPAN_SLOT[j]), i), blocks128(page(B_KL + j % 2), i),
                                   blocks128(page(B_D[j % 3]), i), start=True, stop=True)
                mm.then_inc(task_full, 1)

            def task_u(h):
                pe.wait_ge(pick_done, NL * h + 2)
                pe.wait_ge(kd_done, h + 1)
                for i in range(NT - 1):
                    mm = pe.matmul(blocks128(two_banks(2), i), blocks128(KD, i), blocks128(V, i), start=True, stop=True)
                mm.then_inc(task_full, 1)

            def task_o(h):
                pe.wait_ge(pick_done, NL * h + NL)
                pe.wait_ge(s_done, (NT - 1) * h + NT - 1)
                pe.wait_ge(qe_done, h + 1)
                for i in range(NT):
                    mm = pe.matmul(blocks128(two_banks(3), i), blocks128(V, i), blocks128(ATTN, i), start=True, stop=(i == 0))
                    if i:
                        mm = pe.matmul(blocks128(two_banks(3), i), blocks128(SST, i - 1), blocks128(page(B_QE), i), start=False, stop=True)
                mm.then_inc(task_full, 1)

            def task_ms(h):
                pe.wait_ge(sq_done, h + 1)
                for half in range(2):
                    mm = pe.matmul(psum[:, 4 + half, :], ones[:], page(B_SQ)[:, half * HALF:(half + 1) * HALF], start=True, stop=True)
                mm.then_inc(task_full, 1)

            def head(h, z):
                first = type(h) is int and h == 0
                z(0, 0)
                if not first:
                    task_o(h - 1)
                z(0, 1)
                if not first:
                    task_ms(h - 1)
                z(1, 0)
                task_t0(h)
                task_t1(h)
                z(1, 1)
                task_diag(h)
                task_span(h, 0)
                z(2, 0)
                task_span(h, 1)
                task_span(h, 2)
                task_u(h)
                z(2, 1)
                task_span(h, 3)
                z(3, 0)
                task_span(h, 4)
                task_span(h, 5)
                z(3, 1)
                task_span(h, 6)

            pe.wait_ge(mod_done, 1)
            ready(0)
            fm_half_staged(0, 1, 0, two_banks(0), x0)
            transpose_half(0, 0, range(4), x0)
            ready(1)
            fm_half(1, two_banks(1), 1)
            fm_half_staged(0, 0, 0, two_banks(0), x0).then_inc(w_used, 1)
            fm_half(1, two_banks(1), 0).then_inc(w_used, 1)
            pe.wait_ge(sig_done, 1)
            z_unit(2, 2, two_banks(0))
            pe.wait_ge(gate_acc, KT)
            pe.wait_ge(row_in, 32)
            for n in range(2):
                pe.matmul(psum[:, 6 + n, :], ones[:], page(GATE_W[0])[:, n * HALF:(n + 1) * HALF], start=True, stop=False)
                mm = pe.matmul(psum[:, 6 + n, :], ones[0:1, :], arena[0:1, ADAB * PAGE + n * HALF:ADAB * PAGE + (n + 1) * HALF],
                               start=False, stop=True)
            mm.then_inc(mod_mm, 1)
            pe.wait_ge(g_done, 1)
            z_unit(3, 3, two_banks(1))

            def z_half(it, j, half):
                if half == 0:
                    pe.wait_ge((vt_done, q_done, sig_done, g_done)[j], it + j // 2)
                    pe.wait_ge(w_ready, 4 * it + (j + 1))
                mm = fm_half(j % 2, two_banks(j % 2), half)
                if half:
                    mm.then_inc(w_used, 1)

            head(0, lambda j, half: z_half(1, j, half))
            with pe.Fori(2, HEADS) as it:
                head(it - 1, lambda j, half: z_half(it, j, half))

            def pool_slot(g, j):
                if j % 2 == 0:
                    pe.wait_ge(pu_done, 2 * g + j // 2) if g or j else pe.wait_ge(vt_done, HEADS)
                else:
                    pe.wait_ge(pg_done, 2 * g + j // 2) if g or j > 1 else pe.wait_ge(q_done, HEADS)

            def pool_unit(g, j):
                pool_slot(g, j)
                z_unit(U_POOL + 4 * g + j, j, two_banks(j % 2))

            def pool_mix(g):
                pe.wait_ge(pd_done, 2 * g + 2)
                pe.wait_ge(pw_in, 32)
                gr = G_ORDER[g]
                pw = page(PW[gr // 2])[:, (gr % 2) * HALF:(gr % 2 + 1) * HALF].rearrange("p (c d) -> p c d", c=2)
                for dt in range(2):
                    if g:
                        pe.wait_ge(pmix_done, 2 * g + dt - 1)
                    else:
                        pe.wait_ge(o1_done if dt == 0 else ln_done, HEADS)
                    for half in range(2):
                        for c in range(2):
                            mm = pe.matmul(psum[:, 4 + 2 * dt + half, :], pw[:, c, dt * P:(dt + 1) * P],
                                           page(U_PAGES[g % 2][c])[:, half * HALF:(half + 1) * HALF],
                                           start=(c == 0), stop=(c == 1))
                    mm.then_inc(pm_full, 1)

            def pool_half(j, half):
                if half == 0:
                    pool_slot(0, j)
                    pe.wait_ge(w_ready, U_POOL + j + 1)
                mm = fm_half(j % 2, two_banks(j % 2), half)
                if half:
                    mm.then_inc(w_used, 1)

            head(HEADS - 1, pool_half)
            for g in range(1, GROUPS):
                for j in range(4):
                    pool_unit(g, j)
                    if g == 1 and j < 2:
                        (task_o, task_ms)[j](HEADS - 1)
                pool_mix(g - 1)
            pool_mix(GROUPS - 1)

            def ring_unit(u, s0, c, slot, start, last, e, n):
                pe.wait_ge(w_ready, u + 1)
                for kk in range(2):
                    pe.wait_ge(sp_lo, s0 + kk + 1)
                    for t in range(NT):
                        if start and kk == 0 and n:
                            pe.wait_ge(ycp_done, 16 * e + 8 * (n - 1) + t + 1)
                        mm = tm_rows(c, kk, 2 * slot + kk, t, start and kk == 0, last and kk == 1)
                        if last and kk == 1 and t < NT - 1:
                            mm.then_inc(yb_full, 1)
                mm.then_inc(w_used, 1)

            def by_tokens(units, row_tiles, s_last):
                def rows(q, t, last):
                    for kk in range(2):
                        mm = tm_rows(units[q][0], kk, row_tiles[2 * q + kk], t, False, q == 1 and kk == 1)
                    if last:
                        mm.then_inc(w_used, 1)
                    elif q == 1:
                        mm.then_inc(yb_full, 1)

                pe.wait_ge(w_ready, units[0][1] + 1)
                if s_last is not None:
                    pe.wait_ge(sp_lo, s_last - 2)
                for t in T_ORDER[:4]:
                    rows(0, t, False)
                pe.wait_ge(w_ready, units[1][1] + 1)
                if s_last is not None:
                    pe.wait_ge(sp_lo, s_last)
                for t in T_ORDER[:4]:
                    rows(1, t, False)
                for t in T_ORDER[4:]:
                    for q in range(2):
                        rows(q, t, t == T_ORDER[-1])

            def stage_ring(e, U0, s_base, per):
                for n in range(2):
                    j0 = per * n
                    tail = 2 if n else 1
                    lead = 1 + (per - 1 - tail) % 2
                    mid = per - lead - tail
                    for q in range(lead):
                        j = j0 + q
                        ring_unit(U0 + j, s_base + 2 * j, (U0 + j) % 2, j % 2, q == 0, False, e, n)
                    with pe.Fori(0, mid // 2) as i:
                        for a in range(2):
                            j = j0 + lead + a
                            ring_unit(2 * i + (U0 + j), 4 * i + (s_base + 2 * j), (U0 + j) % 2, j % 2, False, False, e, n)
                    j = j0 + per - tail
                    if n == 0:
                        ring_unit(U0 + j, s_base + 2 * j, (U0 + j) % 2, j % 2, False, True, e, n)
                    else:
                        by_tokens([((U0 + j + q) % 2, U0 + j + q) for q in range(2)],
                                  [2 * ((j + q) % 2) + kk for q in range(2) for kk in range(2)], s_base + 2 * j + 4)

            stage_ring(0, U_OUT, 0, 8)

            def tm_half(j, half):
                for kk in range(2):
                    for t in range(4 * half, 4 * half + 4):
                        mm = tm_rows(j % 2, kk, 2 * j + kk, t, j == 0 and kk == 0, False)
                return mm

            pe.wait_ge(xn_done, NT + 4)
            transpose_half(1, 1, range(KT))
            taken(T_BASE[1] + KT)
            ready(U_IN2)
            tm_half(0, 1)
            pe.wait_ge(xn_done, 2 * NT)
            transpose_half(1, 0, range(4))
            ready(U_IN2 + 1)
            tm_half(1, 1)
            transpose_half(1, 0, range(4, KT))
            taken(T_BASE[2])
            tm_half(0, 0).then_inc(w_used, 1)
            tm_half(1, 0).then_inc(w_used, 1)

            def tm_block(u, js, on_last, free):
                for j in js:
                    pe.wait_ge(w_ready, u + (j + 1))
                    for kk in range(2):
                        k = 2 * j + kk
                        for t in range(NT):
                            if k == 0 and free is not None:
                                free(t)
                            mm = tm_rows(j % 2, kk, k, t, k == 0, k == KT - 1)
                            if k == KT - 1 and t < NT - 1:
                                mm.then_inc(on_last, 1)
                    mm.then_inc(w_used, 1)

            tm_block(U_IN2, (2, 3), in2_full, None)
            with pe.Fori(1, 5) as b:
                tm_block(4 * b + U_IN2, range(4), in2_full, lambda t: pe.wait_ge(in2_free, 8 * b + (t - 7)))

            pe.wait_ge(in2_free, 40)
            pe.wait_ge(tril_done, 1)
            for g in range(SGU_G):
                mm = pe.transpose(blocks128(two_banks(0), g), blocks128(page(SPAT), g), ident[:])
            mm.then_inc(spat_full, 1)

            pe.wait_ge(rope_done, 2)
            transposes(2, lambda t, k: (q_b, k_b)[k // 4][:, t, (k % 4) * P:(k % 4 + 1) * P])
            taken(T_BASE[3])
            pe.wait_ge(spat_tr, 1)

            def qk(n):
                i, h = n // AH, n % AH
                if n >= 2:
                    pe.wait_ge(s_moved, n - 1)
                po = DH * (h % 2)
                for c0 in range(0, (i + 1) * P, HALF):
                    c1 = min(c0 + HALF, (i + 1) * P)
                    o = two_banks(n % 2)[:, c0:c1]
                    qh, ql = [x[po:po + DH, h // 2, i * P:(i + 1) * P] for x in (h_hi, h_lo)]
                    kh, kl = [x[po:po + DH, 4 + h // 2, c0:c1] for x in (h_hi, h_lo)]
                    pe.matmul(o, qh, kh, start=True, stop=False)
                    pe.matmul(o, qh, kl, start=False, stop=False)
                    mm = pe.matmul(o, ql, kh, start=False, stop=True)
                mm.then_inc(s_full, 1)

            def p_t(n):
                pe.wait_ge(p_done, n + 1)
                if n:
                    pe.wait_ge(pt_done, n)
                for j in range(n // AH + 1):
                    mm = pe.transpose(blocks128(two_banks(2), j), blocks128(probs[n % 4], j), ident[:])
                mm.then_inc(pt_full, 1)

            def pv(n):
                i, h = n // AH, n % AH
                pe.wait_ge(pt_done, n + 1)
                if n >= AH:
                    pe.wait_ge(ao_done, (n - AH) // 4 + 1)
                for j in range(i + 1):
                    mm = pe.matmul(two_banks(3)[:, h * P:(h + 1) * P], blocks128(probs_t[n % 2], j),
                                   v_b[:, j, (h // 2) * P:(h // 2 + 1) * P], start=(j == 0), stop=(j == i))
                mm.then_inc(pv_full, 1)

            def sgu(g):
                if g == 0:
                    pe.wait_ge(ln2_done, 1)
                if g >= 2:
                    pe.wait_ge(sgu_done, g - 1)
                pe.matmul(psum[:, 1 + 2 * (g % 2), :], blocks128(page(SPAT_T), g), vs_b[:, :, g * DH:(g + 1) * DH],
                          start=True, stop=True).then_inc(sgu_full, 1)

            N = AH * NT
            for n in range(N + 3):
                if n < N:
                    qk(n)
                if 0 <= n - N_SGU < SGU_G:
                    sgu(n - N_SGU)
                if 0 <= n - 2 < N:
                    p_t(n - 2)
                if 0 <= n - 3 < N:
                    pv(n - 3)

            pe.wait_ge(mixn_done, NT)
            transposes(3, lambda t, k: (att_o, u_b)[k // 4][:, t, (k % 4) * P:(k % 4 + 1) * P], MIX2_ORDER,
                       [None, (ao_done, 2 * NT), (s_moved, N), None, (mixn_done, 2 * NT)] + [None] * 3)
            taken(T_BASE[4])
            tm_block(U_OUT2, range(4), yb_full, None)

            def y_free(t):
                pe.wait_ge(ycp_done, 16 + t + 1)
            tm_block(U_OUT2 + 4, (0, 1), None, y_free)
            by_tokens([(q % 2, U_OUT2 + 6 + q) for q in range(2)], [4, 5, 6, 7], None)

            pe.wait_ge(xn_done, 2 * NT + 4)
            transpose_half(4, 1, range(4))
            pe.wait_ge(ycp_done, 32)
            ready(U_GU)
            fm_half_staged(4, 1, 0, two_banks(0))
            pe.wait_ge(xn_done, 3 * NT)
            transpose_half(4, 0, range(4))
            ready(U_GU + 1)
            fm_half(1, two_banks(1), 1)
            fm_half_staged(4, 0, 0, two_banks(0)).then_inc(w_used, 1)
            fm_half(1, two_banks(1), 0).then_inc(w_used, 1)

            def gu_unit(i, j, first):
                if not first:
                    pe.wait_ge(gate_silu if j % 2 == 0 else act_done, 2 * i + (j // 2 - 1))
                pe.wait_ge(w_ready, 4 * i + (U_GU + j + 1))
                fm_unit(j % 2, two_banks(j)).then_inc(w_used, 1)

            for j in (2, 3):
                gu_unit(0, j, True)
            with pe.Fori(1, FT // 2) as i:
                for j in range(4):
                    gu_unit(i, j, False)
            pe.wait_ge(act_done, FT)
            stage_ring(2, U_DOWN, 32, 11)

        @block.scalar
        def _(act):
            A = act.activation

            def copy(out, in_):
                return A(out, in_, ACT.Copy)

            for t in range(NT):
                act.dma_start(tiles(X0)[:, t, :], ap["x"][0, t * P:(t + 1) * P, :]).then_inc(x_in[t], 16)
            act.wait_ge(c_in, 16)
            A(silu_c, c_col, ACT.Silu).then_inc(silu_done, 1)

            def root(m):
                act.wait_ge(ms_done, m + 1)
                A(ms, ms, ACT.Sqrt).then_inc(sqrt_done, 1)

            def take_hi(n, mul=None, order=range(KT)):
                for a, k in enumerate(order):
                    act.wait_ge(tr_full, T_BASE[n] + a + 1)
                    src = two_banks(T_SLOTS[n][a % len(T_SLOTS[n])])
                    if mul is None:
                        copy(h_hi[:, k, :], src).then_inc(hi_done, 1)
                    else:
                        A(h_hi[:, k, :], src, ACT.Identity, scale=mul(k)).then_inc(hi_done, 1)

            def take_hi_half(n, half, mul):
                for k in range(KT):
                    act.wait_ge(tr_full, T_BASE[n] + KT * (1 - half) + k + 1)
                    A(h_hi[:, k, half * HALF:(half + 1) * HALF], psum[:, half_bank(n, half) + k % 4, :], ACT.Identity,
                      scale=mul(k)).then_inc(hi_done, 1)

            for t in range(NT):
                act.wait_ge(x_in[t], 16)
                if t:
                    act.wait_ge(ss_done, t)
                A(page(JUNK1), tiles(X0)[:, t, :], ACT.Square, accum_out=ss[:, t:t + 1]).then_inc(ss_done, 1)
            root(M_NORM)
            act.wait_ge(rstd_done, 1)
            for t in T_ORDER:
                A(tiles(X0)[:, t, :], tiles(X0)[:, t, :], ACT.Identity, scale=rstd[:, t:t + 1]).then_inc(xn_done, 1)
            act.wait_ge(lb_step, 1)
            A(lb_tmp, lb_tmp, ACT.Exp).then_inc(lb_exp, 1)
            act.wait_ge(mod_done, 2)
            for half in (1, 0):
                for k in range(KT):
                    i = KT * (1 - half) + k
                    act.wait_ge(tr_full, i + 1)
                    src = psum[:, half_bank(0, half) + k % 4, :]
                    A(h_hi[:, k, half * HALF:(half + 1) * HALF], src, ACT.Identity, scale=mul_a[:, k:k + 1], bias=mod[:, k:k + 1]).then_inc(hi_done, 1)
                    if k % 2:
                        if i >= 2:
                            act.wait_ge(lo_done, i - 1)
                        A(page(JUNK0)[:, HALF:D], src, ACT.Identity, scale=mul_a[:, k:k + 1], bias=mod[:, k:k + 1]).then_inc(whole_done, 1)

            bB, qe, vt = page(B_B), page(B_QE), page(B_VT)

            def span_exp(h, j):
                act.wait_ge(d_done, NL * h + j + 1)
                A(page(B_D[j % 3]), page(B_D[j % 3]), ACT.Exp).then_inc(e_done, 1)

            def front(it, z0):
                act.wait_ge(w_used, z0 + 1)
                if not (type(it) is int and it == 0):
                    act.wait_ge(fc_done, it)
                A(page(B_SIG), two_banks(0), ACT.Sigmoid).then_inc(sig_done, 1)

            def gate_sig(it):
                act.wait_ge(w_used, 4 * it + 2)
                A(mix_slot(it), two_banks(1), ACT.Sigmoid).then_inc(gsig_done, 1)

            def log_f(it):
                act.wait_ge(fc_done, it + 1)
                A(bB, bB, ACT.Ln).then_inc(lf_done, 1)

            def decays(it):
                act.wait_ge(b_done, it + 1)
                A(end_decay, bB.rearrange("p (c t) -> p c t", t=P)[:, :, P - 1], ACT.Exp).then_inc(end_done, 1)
                act.wait_ge(dk_done, it + 1)
                A(page(B_KDT), page(B_KDT), ACT.Exp).then_inc(ek_done, 1)

            def take_q(it, z0):
                act.wait_ge(w_used, z0 + 4)
                if not (type(it) is int and it == 0):
                    act.wait_ge(lvl_done, NL * it)
                copy(page(B_Q), two_banks(1)).then_inc(q_done, 1)

            def take_v(it, z0):
                act.wait_ge(w_used, z0 + 3)
                copy(vt, two_banks(0)).then_inc(vt_done, 1)

            def begin(h):
                span_exp(h, 0)
                span_exp(h, 1)
                if not (type(h) is int and h == 0):
                    o_squares(h - 1)
                act.wait_ge(b_done, h + 1)
                A(qe, bB, ACT.Exp).then_inc(eb_done, 1)

            def take_vk(h):
                act.wait_ge(task_full, TASKS * h + 1)
                copy(page(B_V), two_banks(2)).then_inc(v_done, 1)
                act.wait_ge(task_full, TASKS * h + 2)
                copy(page(B_KD), two_banks(3)).then_inc(kd_done, 1)

            def o_squares(h):
                act.wait_ge(task_full, TASKS * h + TASK_O)
                A(page(B_SQ), two_banks(3), ACT.Square).then_inc(sq_done, 1)

            def o_norm(h):
                act.wait_ge(task_full, TASKS * h + TASK_MS)
                A(page(B_SQ), two_banks(2), ACT.Ln, scale=1.0 / P, bias=EPS).then_inc(ln_done, 1)
                act.wait_ge(ln_done, h + 1)
                A(page(B_SQ), page(B_SQ), ACT.Exp, scale=-0.5).then_inc(rs_done, 1)

            def mix_slot(it):
                return arena[:, bass.ds((MIX + 8 + it) * PAGE, PAGE)]

            front(0, 0)
            gate_sig(0)
            take_v(0, 0)
            log_f(0)
            take_q(0, 0)
            decays(0)

            def step(it):
                h = it - 1
                begin(h)
                front(it, 4 * it)
                if not (type(it) is int and it == 1):
                    o_norm(h - 1)
                take_vk(h)
                span_exp(h, 2)
                gate_sig(it)
                for j in (3, 4, 5):
                    span_exp(h, j)
                take_v(it, 4 * it)
                span_exp(h, 6)
                log_f(it)
                take_q(it, 4 * it)
                decays(it)

            step(1)
            with act.Fori(2, HEADS) as it:
                step(it)

            def pool_in(g, j):
                act.wait_ge(w_used, U_POOL + 4 * g + j + 1)
                if j % 2 == 0:
                    if g >= 2:
                        act.wait_ge(pm_full, 2 * (g - 2) + 2)
                    copy(page(U_PAGES[g % 2][j // 2]), two_banks(0)).then_inc(pu_done, 1)
                else:
                    A(mixp[2 * G_ORDER[g] + j // 2], two_banks(1), ACT.Sigmoid).then_inc(pgs_done, 1)

            h = HEADS - 1
            begin(h)
            act.wait_ge(fc_done, HEADS)
            pool_in(0, 0)
            o_norm(h - 1)
            take_vk(h)
            act.dma_start(page(PW[0]).rearrange("p (g c d) -> p g c d", g=2, c=2),
                          ap["pool_w"][0, 0:2].rearrange("g (c p) d -> p g c d", p=P)).then_inc(pw_in, 16)
            span_exp(h, 2)
            pool_in(0, 1)
            for j in (3, 4, 5):
                span_exp(h, j)
            pool_in(0, 2)
            span_exp(h, 6)
            pool_in(0, 3)
            o_squares(h)
            act.dma_start(page(PW[1]).rearrange("p (g c d) -> p g c d", g=2, c=2),
                          ap["pool_w"][0, 2:4].rearrange("g (c p) d -> p g c d", p=P)).then_inc(pw_in, 16)
            act.dma_start(page(RC)[:, 0:64], ap["k_inv_count"]).then_inc(rc_in, 16)
            pool_in(1, 0)
            o_norm(h)
            for j in range(1, 4):
                pool_in(1, j)
            for g in range(2, GROUPS):
                for j in range(4):
                    pool_in(g, j)

            def ring_hi(s0, u0, srcs, j0=0):
                for a, src in enumerate(srcs):
                    j = j0 + a // 2
                    if a % 2 == 0 and j >= 2:
                        act.wait_ge(w_used, u0 + j - 1)
                    copy(h_hi[:, 2 * (j % 2) + a % 2, :], src).then_inc(sp_hi, 1)

            def y_square(e, n, i, t, u_last):
                if i < NT - 1:
                    act.wait_ge(yb_full, 14 * e + 7 * n + i + 1)
                else:
                    act.wait_ge(w_used, u_last)
                if 16 * e + 8 * n + i:
                    act.wait_ge(ysq_done, 16 * e + 8 * n + i)
                A((page(24)[:, 0:HALF], JUNK3, h_hi[:, 7, 0:HALF])[e], psum[:, t, :], ACT.Square,
                  accum_out=ss[:, 8 * n + t:8 * n + t + 1]).then_inc(ysq_done, 1)

            def half0_squares(e, u_last):
                for t in range(NT):
                    y_square(e, 0, t, t, u_last)

            def residual_pairs(e, u_last, done, n, mul):
                for r in range(5):
                    if r < 4:
                        for a, t in enumerate(PAIRS[r]):
                            y_square(e, 1, 2 * r + a, t, u_last)
                    act.wait_ge(ms_done, M_RES[e] + r + 1)
                    q = ms_pair[r % 2][:, (0 if r < 4 else 2):(4 if r else 2)]
                    A(q, q, ACT.Sqrt).then_inc(sqrt_done, 1)
                    if r == 3:
                        take_hi_half(n, 1, mul)
                    if r:
                        t = PAIRS[r - 1][1]
                        act.wait_ge(rstd_done, M_RES[e] + r + 1)
                        A(Y[:, t, :], XR[:, t, :], ACT.Identity, scale=rstd_pair[r % 2][:, 3:4]).then_inc(xn_done, 1)
                    if r < 4:
                        for a, t in enumerate(PAIRS[r]):
                            act.wait_ge(res_done, NT * e + 2 * r + a + 1)
                            act.wait_ge(ss_done, done + 2 * r + a)
                            A(page(25), XR[:, t, :], ACT.Square, accum_out=ss[:, t:t + 1]).then_inc(ss_done, 1)
                            act.dma_start(x_mid[e][t], XR[:, t, :]).then_inc(spilled[e], 16)
                take_hi_half(n, 0, mul)

            act.wait_ge(w_used, U_OUT)
            act.wait_ge(o_done, HEADS)
            ring_hi(0, U_OUT, mix_ring[:8])
            act.wait_ge(pmix_done, 8)
            ring_hi(8, U_OUT, mix_ring[8:], 4)
            ring_hi(16, U_OUT, mix_ring[:2], 8)
            half0_squares(0, U_OUT + 8)
            ring_hi(18, U_OUT, mix_ring[2:], 9)
            residual_pairs(0, U_OUT + 16, NT, 1, lambda k: col("pre_mix_norm_2", k))

            act.wait_ge(tr_full, T_BASE[2])
            act.wait_ge(ss_done, 16)
            act.dma_start(LN_ROWS[:, 0:512], ap["sgu_ln_gain_2"][0].partition_broadcast(P)).then_inc(lnrow_in, 16)
            act.dma_start(LN_ROWS[:, 512:1024], ap["sgu_ln_bias_2"][0].partition_broadcast(P)).then_inc(lnrow_in, 16)
            act.dma_start(page(SPAT).rearrange("p (g j) -> p g j", g=SGU_G), ap["sgu_w_spatial_2"][0].rearrange("g i j -> i g j")).then_inc(spat_in, 16)
            act.dma_start(page(25)[:, 0:P], ap["k_tril"]).then_inc(spat_in, 16)
            act.dma_start(ROPE[:, 320:328], ap["k_inv_freq"]).then_inc(freq_in, 16)
            act.wait_ge(rope_step, ROPE_STEPS)
            A(ROPE[:, 0:64], ROPE[:, 0:64], ACT.Sin).then_inc(trig_done, 1)
            A(ROPE[:, 64:128], ROPE[:, 64:128], ACT.Sin).then_inc(trig_done, 1)
            act.wait_ge(tril_done, 1)
            act.dma_start(BIAS, ap["k_bias"]).then_inc(bias_in, 16)
            act.wait_ge(spilled[0], 16 * NT)
            def gelu(b, dst, kw):
                for t in range(NT):
                    if t < NT - 1:
                        act.wait_ge(in2_full, 7 * b + t + 1)
                    else:
                        act.wait_ge(w_used, U_IN2 + 4 * b + 4)
                    A(dst[:, t, :], psum[:, t, :], ACT.Gelu, **kw(t)).then_inc(in2_free, 1)

            gelu(B_IVS, vs_b, lambda t: {"accum_out": sums[:, t:t + 1]})
            act.wait_ge(mean_done, 1)
            for t in range(NT):
                if t:
                    act.wait_ge(var_done, t)
                A(JUNK3, vs_b[:, t, :], ACT.Square, bias=mean[:, t:t + 1], accum_out=ss[:, t:t + 1]).then_inc(var_done, 1)
            root(M_LN)
            gelu(B_IU, u_b, lambda t: {})
            act.wait_ge(spat_full, 1)
            copy(page(SPAT_T), two_banks(0)).then_inc(spat_tr, 1)
            take_hi(2)

            N = AH * NT

            def pt_copy(n):
                w = (n // AH + 1) * P
                act.wait_ge(pt_full, n + 1)
                if n >= 2:
                    act.wait_ge(pv_full, n - 1)
                copy(probs_t[n % 2][:, 0:w], two_banks(2)[:, 0:w]).then_inc(pt_done, 1)

            def mix_square(x, i, t, col_):
                act.wait_ge(ss_done, 16 + i)
                A(JUNK3, x[:, t, :], ACT.Square, accum_out=ss[:, col_:col_ + 1]).then_inc(ss_done, 1)

            for n in range(N + 2):
                if n >= 2:
                    pt_copy(n - 2)
                if n < N:
                    w = (n // AH + 1) * P
                    act.wait_ge(max_done, n + 1)
                    A(probs[n % 4][:, 0:w], probs[n % 4][:, 0:w], ACT.Exp, bias=neg_max[:, n % 8:n % 8 + 1],
                      accum_out=den_[:, n:n + 1]).then_inc(p_done, 1)
                if 0 <= n - N_SGU_SQ < NT:
                    act.wait_ge(sgu_done, SGU_G)
                    mix_square(u_b, n - N_SGU_SQ, n - N_SGU_SQ, NT + n - N_SGU_SQ)
                if n == N_SGU_NORM - 1:
                    root(M_SGU)
                if n >= N_SGU_NORM and n % 8 == 4 and (n - 12) // 8 < NT - 1:
                    for t in range(0 if n == N_SGU_NORM else (n - 12) // 8, (n - 12) // 8 + 1):
                        act.wait_ge(ao_done, 2 * t + 2)
                        mix_square(att_o, NT + t, t, t)
            act.wait_ge(ao_done, 2 * NT)
            mix_square(att_o, 2 * NT - 1, NT - 1, NT - 1)
            root(M_ATT)
            take_hi(3, lambda k: cols[:, VROW["attn_out_norm_2"] + k:VROW["attn_out_norm_2"] + k + 1], order=MIX2_ORDER)
            act.dma_start(POST_ROW, ap["post_mix_norm_2"][0].partition_broadcast(P)).then_inc(row_in, 16)

            half0_squares(1, U_OUT2 + 4)
            residual_pairs(1, U_OUT2 + 8, 32, 4, lambda k: col("pre_ffn_norm_2", k))
            act.dma_start(ROW_F, ap["post_ffn_norm_2"][0].partition_broadcast(P)).then_inc(row_in, 16)

            act.wait_ge(spilled[1], 16 * NT)
            act.wait_ge(tr_full, T_END)
            with act.Fori(0, FT // 2) as i:
                for j in range(2):
                    act.wait_ge(w_used, 4 * i + (U_GU + 2 * j + 1))
                    A(arena[:, bass.ds((2 * i + j) * PAGE, PAGE)], two_banks(2 * j), ACT.Silu).then_inc(gate_silu, 1)
            act.wait_ge(act_done, FT)
            act.wait_ge(w_used, U_DOWN)
            ring_hi(32, U_DOWN, actp)
            ring_hi(32 + FT, U_DOWN, actp[:2], 11)
            half0_squares(2, U_DOWN + 11)
            ring_hi(34 + FT, U_DOWN, actp[2:], 12)
            for r in range(4):
                for a, t in enumerate(PAIRS[r]):
                    y_square(2, 1, 2 * r + a, t, U_DOWN + 22)
                act.wait_ge(ms_done, M_RES[2] + r + 1)
                A(ms_pair[r % 2][:, 0:2], ms_pair[r % 2][:, 0:2], ACT.Sqrt).then_inc(sqrt_done, 1)

        @block.vector
        def _(dve):
            TT, TS, STT = dve.tensor_tensor, dve.tensor_scalar, dve.scalar_tensor_tensor

            def mean_square(src, width, eps):
                TS(ms, src, 1.0 / width, eps, ALU.mult, ALU.add).then_inc(ms_done, 1)

            def invert(m):
                dve.wait_ge(sqrt_done, m + 1)
                dve.reciprocal(rstd, ms).then_inc(rstd_done, 1)
                dve.wait_ge(rstd_done, m + 1)

            def stats(m, src, width, eps):
                mean_square(src, width, eps)
                invert(m)

            def take_lo(n, mul=None, order=range(KT)):
                for a, k in enumerate(order):
                    dve.wait_ge(hi_done, T_BASE[n] + a + 1)
                    src = two_banks(T_SLOTS[n][a % len(T_SLOTS[n])])
                    hi = h_hi[:, k, :].bitcast(F32)
                    if mul is None:
                        TT(h_lo[:, k, :], src, hi, ALU.subtract).then_inc(lo_done, 1)
                    else:
                        STT(h_lo[:, k, :], src, mul(k), hi, ALU.mult, ALU.subtract).then_inc(lo_done, 1)

            def take_lo_half(n, half, mul):
                for k in range(KT):
                    dve.wait_ge(hi_done, T_BASE[n] + KT * (1 - half) + k + 1)
                    at = h_hi[:, k, half * HALF:(half + 1) * HALF].bitcast(F32)
                    STT(h_lo[:, k, half * HALF:(half + 1) * HALF], psum[:, half_bank(n, half) + k % 4, :], mul(k), at,
                        ALU.mult, ALU.subtract).then_inc(lo_done, 1)

            dve.memset(ones[:], 1.0).then_inc(ones_set, 1)

            def small_vectors():
                dve.wait_ge(vec_t, 1)
                dve.tensor_copy(cols[:], psum[:, 1, 0:VROWS]).then_inc(cols_done, 1)
                dve.wait_ge(cols_done, 1)
                TT(lb_tmp, col("hgrn_lower_bounds", 0, 8), col("hgrn_lower_bounds", 0, 8), ALU.subtract).then_inc(lb_step, 1)
                dve.wait_ge(lb_exp, 1)
                dve.reciprocal(lb, lb_tmp).then_inc(lb_step, 1)
                dve.wait_ge(lb_step, 2)
                TT(lb_tmp, lb_tmp, lb, ALU.mult).then_inc(lb_step, 1)
                dve.wait_ge(lb_step, 3)
                TT(lb, lb_tmp, lb_tmp, ALU.subtract).then_inc(lb_step, 1)
                dve.wait_ge(lb_step, 4)
                TS(one_lb, lb, -1.0, 1.0, ALU.mult, ALU.add).then_inc(lb_step, 1)

            dve.wait_ge(silu_done, 1)
            acc = page(ACC, 2)
            x0 = tiles(X0)
            for k in range(KT):
                if k == 4:
                    dve.wait_ge(ss_done, NT)
                    stats(M_NORM, ss[:, 0:8], D, EPS)
                dve.wait_ge(ada_in[k % 4], 16 * (k // 4 + 1))
                w = page(ADA + 2 * (k % 4), 2)
                if k == 0:
                    TS(acc, w, silu_c[:, 0:1], None, ALU.mult).then_inc(ada_acc, 1)
                else:
                    dve.wait_ge(ada_acc, k)
                    STT(acc, w, silu_c[:, k:k + 1], acc, ALU.mult, ALU.add).then_inc(ada_acc, 1)
            small_vectors()
            dve.wait_ge(mod_mm, 1)
            TT(mod, psum[:, 0, 0:16], col("ada_b", 0, 16), ALU.add).then_inc(mod_done, 1)
            dve.wait_ge(mod_done, 1)
            STT(mul_a, mod[:, 8:16], 1.0, col("norm_pre_w", 0, 8), ALU.add, ALU.mult).then_inc(mod_done, 1)
            dve.wait_ge(mod_done, 2)
            for half in (1, 0):
                for k in range(KT):
                    i = KT * (1 - half) + k
                    dve.wait_ge(hi_done, i + 1)
                    if k % 2:
                        dve.wait_ge(whole_done, i // 2 + 1)
                        x = page(JUNK0)[:, HALF:D]
                    else:
                        if i:
                            dve.wait_ge(lo_done, i - 1)
                        x = page(JUNK0)[:, 0:HALF]
                        TS(x, psum[:, half_bank(0, half) + k % 4, :], mul_a[:, k:k + 1], mod[:, k:k + 1], ALU.mult, ALU.add).then_inc(lo_tmp, 1)
                        dve.wait_ge(lo_tmp, i // 2 + 1)
                    TT(h_lo[:, k, half * HALF:(half + 1) * HALF], x, h_hi[:, k, half * HALF:(half + 1) * HALF].bitcast(F32), ALU.subtract).then_inc(lo_done, 1)

            gate_sum = page(GATE_W[0])
            dve.wait_ge(gate_in, 16 * KT)
            TS(gate_sum, gate_sum, silu_c[:, 0:1], None, ALU.mult).then_inc(gate_acc, 1)
            for k in range(1, KT):
                dve.wait_ge(gate_acc, k)
                STT(gate_sum, page(GATE_W[k]), silu_c[:, k:k + 1], gate_sum, ALU.mult, ALU.add).then_inc(gate_acc, 1)

            sig, kk_, bb, qq, qe = page(B_SIG), page(B_K), page(B_B), page(B_Q), page(B_QE)
            b_chunks = bb.rearrange("p (c t) -> p c t", t=P)

            def gate_g(it):
                dve.wait_ge(gsig_done, it + 1)
                m = arena[:, bass.ds((MIX + 8 + it) * PAGE, PAGE)]
                TT(m, m, two_banks(1), ALU.mult).then_inc(g_done, 1)

            def gate_f(it):
                dve.wait_ge(sig_done, it + 1)
                dve.wait_ge(lb_step, 5)
                i = it
                TS(sig, sig, one_lb[:, bass.ds(i, 1)], lb[:, bass.ds(i, 1)], ALU.mult, ALU.add).then_inc(f_done, 1)
                dve.wait_ge(f_done, it + 1)
                TS(kk_, sig, -1.0, 1.0, ALU.mult, ALU.add).then_inc(k_done, 1)
                TS(bb, sig, F_MIN, None, ALU.max).then_inc(fc_done, 1)

            def decay_sums(it, last=None):
                dve.wait_ge(lf_done, it + 1)
                if last is not None:
                    dve.wait_ge(task_full, last)
                for c in range(NT):
                    x = dve.tensor_tensor_scan(b_chunks[:, c, :], ones[:], b_chunks[:, c, :], 0.0, ALU.mult, ALU.add)
                x.then_inc(b_done, 1)

            def decayed_keys(it):
                dve.wait_ge(b_done, it + 1)
                kdt = page(B_KDT)
                TT(kdt.rearrange("p (c t) -> p c t", t=P), b_chunks[:, :, P - 1:P].to_broadcast([P, NT, P]), b_chunks, ALU.subtract).then_inc(dk_done, 1)
                dve.wait_ge(ek_done, it + 1)
                TT(kdt, kdt, kk_, ALU.mult).then_inc(kdec_done, 1)

            def halves(x, w):
                return x.rearrange("p (n u w) -> p n u w", u=2, w=w)

            def span_d(h, j):
                w = SPANS[j]
                d, b4 = halves(page(B_D[j % 3]), w), halves(bb, w)
                ref = b4[:, :, 0, w - 1:w].to_broadcast([P, S // (2 * w), w])
                if j >= 3:
                    dve.wait_ge(task_full, TASKS * h + SPAN_TASK[j - 3])
                TT(d[:, :, 1, :], b4[:, :, 1, :], ref, ALU.subtract)
                TT(d[:, :, 0, :], ref, b4[:, :, 0, :], ALU.subtract).then_inc(d_done, 1)

            def span_kq(h, j):
                e = page(B_D[j % 3])
                dve.wait_ge(e_done, NL * h + j + 1)
                if j >= 2:
                    dve.wait_ge(task_full, TASKS * h + SPAN_TASK[j - 2])
                TT(page(B_KL + j % 2), kk_, e, ALU.mult).then_inc(kl_done, 1)
                dve.wait_ge(kl_done, NL * h + j + 1)
                TT(e, qq, e, ALU.mult).then_inc(lvl_done, 1)

            att3 = page(B_ATT).rearrange("p (i t) -> p i t", t=P)

            def pick(h, j, at):
                w = SPANS[j]
                dve.wait_ge(const_in, 32)
                dve.wait_ge(task_full, at[j][0])
                dve.wait_ge(pick_done if j else diag_done, at[j][1])
                nb = P // (2 * w)
                data = two_banks(SPAN_SLOT[j])
                m = lvl_mask[:, j, :]
                if w == 64:
                    to, data = [x.rearrange("p (n u w) -> p n u w", u=2, w=w)[:, :, 1, :] for x in (page(B_ATT), data)]
                    m = m.rearrange("p (a c) -> p a c", a=1).to_broadcast([P, NT, 64])
                else:
                    to, data = [x.rearrange("p (i n u w) -> p i n u w", i=NT, u=2, w=w)[:, :, :, 1, :] for x in (page(B_ATT), data)]
                    m = m.rearrange("p (a n w) -> p a n w", a=1, w=w).to_broadcast([P, NT, nb, w])
                dve.copy_predicated(to, m, data).then_inc(pick_done, 1)

            def states(h):
                dve.wait_ge(task_full, TASKS * h + TASK_U)
                dve.wait_ge(end_done, h + 1)
                sst = page(B_S)
                for c in range(NT - 1):
                    u = two_banks(2)[:, c * P:(c + 1) * P]
                    if c == 0:
                        dve.tensor_copy(sst[:, 0:P], u).then_inc(s_done, 1)
                    else:
                        dve.wait_ge(s_done, (NT - 1) * h + c)
                        STT(sst[:, c * P:(c + 1) * P], sst[:, (c - 1) * P:c * P], end_decay[:, c:c + 1], u, ALU.mult, ALU.add).then_inc(s_done, 1)

            def spans(h, gate, f):
                at = [(TASKS * h + SPAN_TASK[min(j, 6) if j < 5 else 6], NL * h + j if j else h + 1) for j in range(NL)]
                if type(h) is not int:
                    at = [tuple(dve.snap(x) for x in a) for a in at]
                span_d(h, 0)
                span_d(h, 1)
                dve.wait_ge(q_done, h + 1)
                span_kq(h, 0)
                span_kq(h, 1)
                dve.wait_ge(eb_done, h + 1)
                TT(qe, qe, qq, ALU.mult).then_inc(qe_done, 1)
                if not (type(h) is int and h == 0):
                    back_3(h - 1)
                span_d(h, 2)
                if not (type(h) is int and h == 0):
                    dve.wait_ge(o_done, h)
                dve.wait_ge(task_full, TASKS * h + 3)
                TT(att3, two_banks(2).rearrange("p (i t) -> p i t", t=P), ident[:].rearrange("p (a t) -> p a t", a=1).to_broadcast([P, NT, P]), ALU.mult).then_inc(diag_done, 1)
                span_kq(h, 2)
                span_d(h, 3)
                pick(h, 0, at)
                gate()
                span_d(h, 4)
                pick(h, 1, at)
                span_d(h, 5)
                pick(h, 2, at)
                span_kq(h, 3)
                states(h)
                span_kq(h, 4)
                span_d(h, 6)
                pick(h, 3, at)
                span_kq(h, 5)
                span_kq(h, 6)
                pick(h, 4, at)
                f()
                pick(h, 5, at)
                pick(h, 6, at)

            def back_3(h):
                dve.wait_ge(rs_done, h + 1)
                t1 = page(B_ATT)
                STT(t1, two_banks(3), col("hgrn_norm_w"), page(B_SQ), ALU.mult, ALU.mult).then_inc(o1_done, 1)
                dve.wait_ge(o1_done, h + 1)
                dve.wait_ge(g_done, h + 1)
                m = arena[:, bass.ds((MIX + 8 + h) * PAGE, PAGE)]
                TT(m, m, t1, ALU.mult).then_inc(o_done, 1)

            gate_f(0)
            gate_g(0)
            dve.wait_ge(mod_mm, 2)
            dve.wait_ge(row_in, 32)
            TT(gate_row, two_banks(3), page(NPOST), ALU.mult).then_inc(mod_done, 1)
            decay_sums(0)
            decayed_keys(0)

            def step(it):
                def next_f():
                    gate_f(it)
                    decay_sums(it, TASKS * (it - 1) + SPAN_TASK[6])
                spans(it - 1, lambda: gate_g(it), next_f)
                decayed_keys(it)

            step(1)
            with dve.Fori(2, HEADS) as it:
                step(it)

            def pool_gate(g, j):
                dve.wait_ge(pgs_done, 2 * g + j + 1)
                m = mixp[2 * G_ORDER[g] + j]
                TT(m, m, two_banks(1), ALU.mult).then_inc(pg_done, 1)

            steps = [0]

            def wstep(x):
                x.then_inc(win_step, 1)
                steps[0] += 1
                dve.wait_ge(win_step, steps[0])

            def window(g, c):
                dve.wait_ge(pu_done, 2 * g + c + 1)
                u = page(U_PAGES[g % 2][c])
                src, w = u, 1
                for a in range(G_ORDER[g] + 1):
                    dst = page((S_A, S_B)[a % 2])
                    dve.tensor_copy(dst[:, 0:w], src[:, 0:w]).then_inc(win_step, 1)
                    steps[0] += 1
                    wstep(TT(dst[:, w:S], src[:, w:S], src[:, 0:S - w], ALU.add))
                    src, w = dst, 2 * w
                dve.wait_ge(rc_in, 16)
                wstep(TT(src[:, 0:w], src[:, 0:w], page(RC)[:, 16 * G_ORDER[g]:16 * G_ORDER[g] + w], ALU.mult))
                TT(u[:, 0:w], src[:, 0:w], u[:, 0:w], ALU.subtract).then_inc(win_step, 1)
                steps[0] += 1
                STT(u[:, w:S], src[:, w:S], 1.0 / w, u[:, w:S], ALU.mult, ALU.subtract).then_inc(pd_done, 1)
                dve.wait_ge(pd_done, 2 * g + c + 1)

            def pool_out(g):
                for dt in range(2):
                    dve.wait_ge(pm_full, 2 * g + dt + 1)
                    dve.wait_ge(pg_done, 2 * g + dt + 1)
                    m = mixp[2 * G_ORDER[g] + dt]
                    STT(m, two_banks(2 + dt), col("pool_scale", 2 * G_ORDER[g] + dt), m, ALU.mult, ALU.mult).then_inc(pmix_done, 1)

            h = HEADS - 1
            spans(h, lambda: pool_gate(0, 0), lambda: pool_gate(0, 1))
            dve.wait_ge(task_full, TASKS * h + TASK_O)
            window(0, 0)
            window(0, 1)
            back_3(h)
            pool_gate(1, 0)
            for g in range(1, GROUPS):
                for c in range(2):
                    window(g, c)
                    if g > 1 or c:
                        pool_gate(g, c)
                pool_out(g - 1)
            pool_out(GROUPS - 1)

            def ring_lo(s0, u0, srcs, j0=0):
                for a, src in enumerate(srcs):
                    j = j0 + a // 2
                    k = 2 * (j % 2) + a % 2
                    dve.wait_ge(sp_hi, s0 + a + 1)
                    TT(h_lo[:, k, :], src, h_hi[:, k, :].bitcast(F32), ALU.subtract).then_inc(sp_lo, 1)

            def half0_rows(e, y, row):
                for t in range(NT):
                    dve.wait_ge(ysq_done, 16 * e + t + 1)
                    TT(y(t), psum[:, t, :], row[:, 0:HALF], ALU.mult).then_inc(ycp_done, 1)
                TS(ms_half0, ss[:, 0:NT], 1.0 / D, EPS, ALU.mult, ALU.add).then_inc(sum_done, 1)

            def residual_pairs(e, done, y, row, n=None, mul=None):
                for r in range(5 if n is not None else 4):
                    m, rs = ms_pair[r % 2], rstd_pair[r % 2]
                    if r < 4:
                        for a, t in enumerate(PAIRS[r]):
                            dve.wait_ge(ysq_done, 16 * e + NT + 2 * r + a + 1)
                            TT(y(t)[-1][:, -HALF:], psum[:, t, :], row[:, HALF:D], ALU.mult).then_inc(ycp_done, 1)
                        dve.wait_ge(sum_done, e + 1)
                        t0 = PAIRS[r][0]
                        x = STT(m[:, 0:2], ss[:, NT + t0:NT + t0 + 2], 1.0 / D, ms_half0[:, t0:t0 + 2], ALU.mult, ALU.add)
                    if r and n is not None:
                        dve.wait_ge(ss_done, done + 2 * r)
                        t0 = PAIRS[r - 1][0]
                        x = TS(m[:, 2:4], ss[:, t0:t0 + 2], 1.0 / D, EPS, ALU.mult, ALU.add)
                    x.then_inc(ms_done, 1)
                    dve.wait_ge(sqrt_done, M_RES[e] + r + 1)
                    cs = slice(0 if r < 4 else 2, 4 if r and n is not None else 2)
                    dve.reciprocal(rs[:, cs], m[:, cs]).then_inc(rstd_done, 1)
                    dve.wait_ge(rstd_done, M_RES[e] + r + 1)
                    if r == 3 and n is not None:
                        take_lo_half(n, 1, mul)
                    if r and n is not None:
                        t = PAIRS[r - 1][0]
                        TS(Y[:, t, :], XR[:, t, :], rs[:, 2:3], None, ALU.mult).then_inc(xn_done, 1)
                    if r < 4:
                        for a, t in enumerate(PAIRS[r]):
                            dve.wait_ge(x_in[t], 16 * (e + 2))
                            dve.wait_ge(ycp_done, 16 * e + NT + 2 * r + a + 1)
                            w0 = 0
                            for yy in y(t):
                                w = yy.shape[-1]
                                x = STT(XR[:, t, w0:w0 + w], yy, rs[:, a:a + 1], XR[:, t, w0:w0 + w], ALU.mult, ALU.add)
                                w0 += w
                            x.then_inc(res_done, 1)
                if n is not None:
                    take_lo_half(n, 0, mul)

            ring_lo(0, U_OUT, mix_ring)
            ring_lo(16, U_OUT, mix_ring[:2], 8)
            half0_rows(0, lambda t: Y[:, t, 0:HALF], gate_row)
            ring_lo(18, U_OUT, mix_ring[2:], 9)
            residual_pairs(0, NT, lambda t: [Y[:, t, :]], gate_row, 1, lambda k: col("pre_mix_norm_2", k))

            dve.wait_ge(spat_in, 32)
            dve.wait_ge(tr_full, T_BASE[2])
            sp3 = page(SPAT).rearrange("p (g j) -> p g j", g=SGU_G)
            tril = page(25)[:, 0:P].rearrange("p (a j) -> p a j", a=1).to_broadcast([P, SGU_G, P])
            TT(sp3, sp3, tril, ALU.mult).then_inc(tril_done, 1)

            steps_r = [0]

            def rstep(x):
                x.then_inc(rope_step, 1)
                steps_r[0] += 1
                dve.wait_ge(rope_step, steps_r[0])

            dve.wait_ge(pos_in, 16)
            dve.wait_ge(freq_in, 16)
            ang, ang2, turns, wrap = [ROPE[:, 64 * i:64 * (i + 1)] for i in range(4)]
            turns_i = ROPE[:, 256:320].bitcast(I32)
            freq, posf = ROPE[:, 320:328], ROPE[:, 328:336]
            rstep(dve.tensor_copy(posf, pos.bitcast(I32)))
            rstep(TT(ang.rearrange("p (t f) -> p t f", f=ROT),
                     posf.rearrange("p (t a) -> p t a", a=1).to_broadcast([P, NT, ROT]),
                     freq.rearrange("p (a f) -> p a f", a=1).to_broadcast([P, NT, ROT]), ALU.mult))
            rstep(TS(turns_i, ang, 1.0 / TWO_PI, None, ALU.mult))
            rstep(dve.tensor_copy(turns, turns_i))
            rstep(STT(ang, turns, -TWO_PI_HI, ang, ALU.mult, ALU.add))
            rstep(STT(ang, turns, -TWO_PI_LO, ang, ALU.mult, ALU.add))

            def wrapped(x):
                rstep(TS(wrap, x, math.pi, -TWO_PI, ALU.is_gt, ALU.mult))
                rstep(TT(x, x, wrap, ALU.add))
                rstep(TS(wrap, x, -math.pi, TWO_PI, ALU.is_lt, ALU.mult))
                rstep(TT(x, x, wrap, ALU.add))
                rstep(TS(x, x, PI_IN, -PI_IN, ALU.min, ALU.max))

            wrapped(ang)
            rstep(TS(ang2, ang, math.pi / 2, None, ALU.add))
            wrapped(ang2)
            assert steps_r[0] == ROPE_STEPS

            def vs_norm():
                dve.wait_ge(in2_free, NT * (B_IVS + 1))
                TS(mean, sums, -1.0 / ATT, None, ALU.mult).then_inc(mean_done, 1)
                dve.wait_ge(var_done, NT)
                stats(M_LN, ss[:, 0:8], ATT, LN_EPS)
                dve.wait_ge(lnrow_in, 32)
                for t in range(NT):
                    x = TS(vs_b[:, t, :], vs_b[:, t, :], mean[:, t:t + 1], rstd[:, t:t + 1], ALU.add, ALU.mult)
                x.then_inc(lnorm, 1)
                dve.wait_ge(lnorm, 1)
                row3 = [LN_ROWS[:, a * ATT:(a + 1) * ATT].rearrange("p (a c) -> p a c", a=1).to_broadcast([P, NT, ATT]) for a in range(2)]
                TT(vs_b, vs_b, row3[0], ALU.mult).then_inc(lnorm, 1)
                dve.wait_ge(lnorm, 2)
                TT(vs_b, vs_b, row3[1], ALU.add).then_inc(ln2_done, 1)

            def in2_copy(b, dst, scale):
                for t in range(NT):
                    if t < NT - 1:
                        dve.wait_ge(in2_full, 7 * b + t + 1)
                    else:
                        dve.wait_ge(w_used, U_IN2 + 4 * b + 4)
                    if scale is None:
                        dve.tensor_copy(dst[:, t, :], psum[:, t, :]).then_inc(in2_free, 1)
                    else:
                        TS(dst[:, t, :], psum[:, t, :], scale, None, ALU.mult).then_inc(in2_free, 1)

            sin4, cos4 = [x.rearrange("p (t a f) -> p t a f", t=NT, a=1).to_broadcast([P, NT, AH, ROT]) for x in (ang, ang2)]
            tmp = [x.rearrange("p (t h f) -> p t h f", t=NT, h=AH) for x in ROPE_T]

            def rotate(i, x):
                dve.wait_ge(trig_done, 2)
                dve.wait_ge(in2_free, NT * ((B_IQ, B_IK)[i] + 1))
                x1, x2 = [x.rearrange("p t (h d) -> p t h d", d=DH)[:, :, :, a * ROT:(a + 1) * ROT] for a in range(2)]
                rstep(TT(tmp[0], x1, cos4, ALU.mult))
                rstep(TT(tmp[1], x2, sin4, ALU.mult))
                rstep(TT(tmp[0], tmp[0], tmp[1], ALU.subtract))
                rstep(TT(tmp[1], x2, cos4, ALU.mult))
                rstep(TT(tmp[2], x1, sin4, ALU.mult))
                rstep(dve.tensor_copy(x1, tmp[0]))
                TT(x2, tmp[1], tmp[2], ALU.add).then_inc(rope_done, 1)
                dve.wait_ge(rope_done, i + 1)

            in2_copy(B_IQ, q_b, DH ** -0.5)
            rotate(0, q_b)
            vs_norm()
            in2_copy(B_IK, k_b, None)
            rotate(1, k_b)
            in2_copy(B_IV, v_b, None)

            def spatial(g):
                dve.wait_ge(sgu_full, g + 1)
                ug = u_b[:, :, g * DH:(g + 1) * DH]
                STT(ug, psum[:, 1 + 2 * (g % 2), :].rearrange("p (t c) -> p t c", c=DH), col("sgu_b_spatial_2", g), ug,
                    ALU.add, ALU.mult).then_inc(sgu_done, 1)

            take_lo(2)

            dve.wait_ge(bias_in, 16)

            def attended(m):
                i, hh = m // 2, m % 2
                dve.wait_ge(pv_full, 4 * m + 4)
                dve.reciprocal(r_den[:, 4 * hh:4 * hh + 4], den_[:, 4 * m:4 * m + 4]).then_inc(den_done, 1)
                dve.wait_ge(den_done, m + 1)
                for a in range(2):
                    o = att_o[:, i, hh * 256:(hh + 1) * 256].rearrange("p (e a d) -> p e a d", a=2, d=DH)[:, :, a, :]
                    src = psum[:, 6 + hh, :].rearrange("p (e a x d) -> p e a x d", a=2, x=2, d=DH)[:, :, a, a, :]
                    r = r_den[:, 4 * hh:4 * hh + 4].rearrange("p (e a x) -> p e a x", a=2, x=1)[:, :, a, :].to_broadcast([P, 2, DH])
                    x = TT(o, src, r, ALU.mult)
                x.then_inc(ao_done, 1)

            for n in range(AH * NT):
                i = n // AH
                w = (i + 1) * P
                dve.wait_ge(s_full, n + 1)
                if n >= 4:
                    dve.wait_ge(pt_full, n - 3)
                TT(probs[n % 4][:, 0:w], two_banks(n % 2)[:, 0:w], BIAS[:, PAGE - w:PAGE], ALU.add).then_inc(s_moved, 1)
                dve.wait_ge(s_moved, n + 1)
                dve.reduce_max(neg_max[:, n % 8:n % 8 + 1], probs[n % 4][:, 0:w], AX.X, negate=True).then_inc(max_done, 1)
                if n >= 6 and n % 4 == 2:
                    attended((n - 6) // 4)
                if 0 <= n - N_SGU < SGU_G:
                    spatial(n - N_SGU)
                if n == N_SGU_NORM - 2:
                    dve.wait_ge(ss_done, 16 + NT)
                    mean_square(ss[:, NT:2 * NT], ATT, EPS)
                if n == N_SGU_NORM:
                    invert(M_SGU)
                if 0 <= n - N_SGU_NORM < NT:
                    t = n - N_SGU_NORM
                    TS(u_b[:, t, :], u_b[:, t, :], rstd[:, t:t + 1], None, ALU.mult).then_inc(mixn_done, 1)
            attended(2 * NT - 1)
            dve.wait_ge(ss_done, 16 + 2 * NT)
            stats(M_ATT, ss[:, 0:NT], ATT, EPS)
            for t in range(NT):
                TS(att_o[:, t, :], att_o[:, t, :], rstd[:, t:t + 1], None, ALU.mult).then_inc(mixn_done, 1)
            take_lo(3, lambda k: cols[:, VROW["attn_out_norm_2"] + k:VROW["attn_out_norm_2"] + k + 1], order=MIX2_ORDER)
            dve.wait_ge(row_in, 48)
            half0_rows(1, lambda t: Y[:, t, 0:HALF], POST_ROW)
            residual_pairs(1, 32, lambda t: [Y[:, t, :]], POST_ROW, 4, lambda k: col("pre_ffn_norm_2", k))

            with dve.Fori(0, FT // 2) as i:
                for j in range(2):
                    dve.wait_ge(gate_silu, 2 * i + (j + 1))
                    dve.wait_ge(w_used, 4 * i + (U_GU + 2 * j + 2))
                    a = arena[:, bass.ds((2 * i + j) * PAGE, PAGE)]
                    TT(a, a, two_banks(2 * j + 1), ALU.mult).then_inc(act_done, 1)
            ring_lo(32, U_DOWN, actp)
            dve.wait_ge(row_in, 64)
            ring_lo(32 + FT, U_DOWN, actp[:2], 11)
            half0_rows(2, lambda t: y_half0[:, t, :], ROW_F)
            ring_lo(34 + FT, U_DOWN, actp[2:], 12)
            residual_pairs(2, None, lambda t: [y_half0[:, t, :], y_half1[:, t, :]], ROW_F)


def constants():
    i = np.arange(P)
    mask = np.zeros((P, NL, 64), np.int32)
    for j, w in enumerate(SPANS):
        x = np.arange(64)
        block = x // w
        mask[:, j, :] = (i[:, None] // (2 * w) == block[None, :]) & (i[:, None] % (2 * w) < w)
    d = (S - P) + i[:, None] - np.arange(S)[None, :]
    n = ((d >= 0) & (d <= 128)).astype(int) + ((d >= 0) & (d <= 512) & (d % 4 == 0)) + ((d >= 0) & (d % 16 == 0))
    bias = np.where(n > 0, np.log(np.maximum(n, 1)), NEG).astype(np.float32)
    freq = np.float32(500000.0) ** (-np.arange(0, 2 * ROT, 2, dtype=np.float32) / np.float32(2 * ROT))
    count = np.array([[1.0 / min(t + 1, w) for t in range(16)] for w in POOL_WINDOWS], np.float32).reshape(1, 64)
    return {
        "k_ident": np.eye(P, dtype=np.float32),
        "k_level_mask": mask,
        "k_tril": np.tril(np.ones((P, P), np.float32)),
        "k_bias": bias,
        "k_inv_freq": np.repeat(freq.astype(np.float32).reshape(1, ROT), P, 0),
        "k_inv_count": np.repeat(count, P, 0),
    }


INPUTS = ["x", "c", "norm_pre_w", "ada_w", "ada_b", "w_in", "pool_w", "pool_scale", "hgrn_lower_bounds",
          "hgrn_norm_w", "w_out", "norm_post_w", "positions_2", "pre_mix_norm_2", "w_in_2", "sgu_ln_gain_2",
          "sgu_ln_bias_2", "sgu_w_spatial_2", "sgu_b_spatial_2", "attn_out_norm_2", "sgu_out_norm_2", "w_out_2",
          "post_mix_norm_2", "pre_ffn_norm_2", "w_gate_2", "w_up_2", "w_down_2", "post_ffn_norm_2"]


def kernel(**inputs):
    import concourse.bacc as bacc
    from concourse.bass_utils import run_bass_kernel_spmd

    nc = bacc.Bacc("TRN2", target_bir_lowering=False, num_devices=1)
    arrays = {name: np.ascontiguousarray(inputs[name]) for name in INPUTS}
    arrays.update(constants())
    ap = {}
    for name, a in arrays.items():
        ap[name] = nc.dram_tensor(name, a.shape, mybir.dt.from_np(a.dtype), kind="ExternalInput").ap()
    out = nc.dram_tensor("out", (1, S, D), F32, kind="ExternalOutput").ap()
    ap["out"] = out.rearrange("b (t p) d -> (b t) p d", p=P)
    program(nc, ap)
    r = run_bass_kernel_spmd(nc, [arrays], core_ids=[0])
    return r.results[0]["out"]
```
